# Optimizing a Trainium2 kernel written in Bass

```python
import jax, jax.numpy as jnp
from jax import lax
import numpy as np

D_MODEL = 1024
BATCH = 1
SEQ = 512
DEPTH = 1

D_MIX = D_MODEL
D_LRU = D_MIX // 2
LRU_BLOCKS = 8
LRU_BLOCK = D_LRU // LRU_BLOCKS
CONV_WIDTH = 4
LRU_C = 8.0
N_HEADS = 8
N_KV_HEADS = 2
GQA_GROUP = N_HEADS // N_KV_HEADS
HEAD_DIM = (D_MIX - D_LRU) // N_HEADS
D_ATTN = N_HEADS * HEAD_DIM
WINDOW = 128
BLOCK_Q = 128
D_FF = 2816
RMS_EPS = 1e-6
D_IN = 2 * D_LRU + (N_HEADS + 2 * N_KV_HEADS) * HEAD_DIM
MASK_VALUE = -1e30


def rms_norm(x, g):
    xf = x.astype(jnp.float32)
    y = xf * lax.rsqrt(jnp.mean(xf * xf, axis=-1, keepdims=True) + RMS_EPS)
    return (y * g.astype(jnp.float32)).astype(x.dtype)

def swiglu(x, w_gu, w_down):
    gate, up = jnp.split(x @ w_gu, 2, axis=-1)
    return (jax.nn.silu(gate) * up) @ w_down

def causal_depthwise_conv(x, w, b):
    c = x.shape[-1]
    rhs = w.astype(x.dtype)[:, None, :]
    y = lax.conv_general_dilated(x, rhs, window_strides=(1,), padding=[(CONV_WIDTH - 1, 0)],
                                 dimension_numbers=("NWC", "WIO", "NWC"), feature_group_count=c)
    return y + b.astype(x.dtype)

def block_diag(x, w, b):
    bsz, s, _ = x.shape
    xh = x.reshape(bsz, s, LRU_BLOCKS, LRU_BLOCK)
    y = jnp.einsum("bshi,hij->bshj", xh, w).reshape(bsz, s, D_LRU)
    return y + b

def rg_lru(x_in, conv_w, conv_b, w_rg, b_rg, w_ig, b_ig, lam):
    xc = causal_depthwise_conv(x_in, conv_w, conv_b)
    r = jax.nn.sigmoid(block_diag(xc, w_rg, b_rg).astype(jnp.float32))
    i = jax.nn.sigmoid(block_diag(xc, w_ig, b_ig).astype(jnp.float32))
    log_a = LRU_C * r * jax.nn.log_sigmoid(lam.astype(jnp.float32))
    a = jnp.exp(log_a)
    mult = jnp.sqrt(-jnp.expm1(2.0 * log_a))
    u = mult * (i * xc.astype(jnp.float32))

    def combine(left, right):
        a_l, u_l = left
        a_r, u_r = right
        return a_l * a_r, a_r * u_l + u_r

    _, h = lax.associative_scan(combine, (a, u), axis=1)
    return h.astype(x_in.dtype)

def sliding_window_sink_attention(q, k, v, sinks):
    bsz, s = q.shape[0], q.shape[1]
    nb = s // BLOCK_Q
    qb = q.reshape(bsz, nb, BLOCK_Q, N_KV_HEADS, GQA_GROUP, HEAD_DIM)
    kb = k.reshape(bsz, nb, BLOCK_Q, N_KV_HEADS, HEAD_DIM)
    vb = v.reshape(bsz, nb, BLOCK_Q, N_KV_HEADS, HEAD_DIM)
    k_band = jnp.concatenate([jnp.concatenate([jnp.zeros_like(kb[:, :1]), kb[:, :-1]], axis=1), kb], axis=2)
    v_band = jnp.concatenate([jnp.concatenate([jnp.zeros_like(vb[:, :1]), vb[:, :-1]], axis=1), vb], axis=2)
    scale = HEAD_DIM ** -0.5
    scores = jnp.einsum("bnqkgd,bnjkd->bnkgqj", qb, k_band).astype(jnp.float32) * scale
    qi = jnp.arange(BLOCK_Q)[:, None]
    kj = jnp.arange(2 * BLOCK_Q)[None, :]
    rel = qi + BLOCK_Q - kj
    band = (rel >= 0) & (rel < WINDOW)
    blk = jnp.arange(nb)[:, None, None]
    mask = band[None] & ((blk > 0) | (kj >= BLOCK_Q)[None])
    scores = jnp.where(mask[None, :, None, None], scores, MASK_VALUE)
    sink = sinks.astype(jnp.float32).reshape(1, 1, N_KV_HEADS, GQA_GROUP, 1, 1)
    m = jnp.maximum(jnp.max(scores, axis=-1, keepdims=True), sink)
    p = jnp.exp(scores - m)
    denom = jnp.sum(p, axis=-1, keepdims=True) + jnp.exp(sink - m)
    p = (p / denom).astype(v.dtype)
    out = jnp.einsum("bnkgqj,bnjkd->bnqkgd", p, v_band)
    return out.reshape(bsz, s, D_ATTN)

def hybrid_mixer(h, w_in, conv_w, conv_b, w_rg, b_rg, w_ig, b_ig, lam, sinks, g_lru_out, g_attn_out, w_o):
    bsz, s, _ = h.shape
    proj = h @ w_in
    o1 = D_LRU
    o2 = o1 + D_LRU
    o3 = o2 + D_ATTN
    o4 = o3 + N_KV_HEADS * HEAD_DIM
    x_lru = proj[..., :o1]
    gate_lru = proj[..., o1:o2]
    q = proj[..., o2:o3].reshape(bsz, s, N_HEADS, HEAD_DIM)
    k = proj[..., o3:o4].reshape(bsz, s, N_KV_HEADS, HEAD_DIM)
    v = proj[..., o4:].reshape(bsz, s, N_KV_HEADS, HEAD_DIM)
    y_lru = rg_lru(x_lru, conv_w, conv_b, w_rg, b_rg, w_ig, b_ig, lam) * jax.nn.gelu(gate_lru)
    y_attn = sliding_window_sink_attention(q, k, v, sinks)
    y = jnp.concatenate([rms_norm(y_lru, g_lru_out), rms_norm(y_attn, g_attn_out)], axis=-1)
    return y @ w_o

def first_inputs(seed: int = 0) -> dict:
    key = jax.random.key(seed)
    ks = jax.random.split(key, 32)
    f32 = jnp.float32

    def nrm(k, shape, scale):
        return jax.random.normal(k, shape, f32) * scale

    def gain(k, n):
        return 1.0 + 0.05 * jax.random.normal(k, (DEPTH, n), f32)

    u = jax.random.uniform(ks[13], (DEPTH, D_LRU), f32, 0.9, 0.999)
    return {
        "x": jax.random.normal(ks[0], (BATCH, SEQ, D_MODEL), f32),
        "ffn1_pre_g": gain(ks[1], D_MODEL),
        "ffn1_w_gu": nrm(ks[2], (DEPTH, D_MODEL, 2 * D_FF), D_MODEL ** -0.5),
        "ffn1_w_down": nrm(ks[3], (DEPTH, D_FF, D_MODEL), D_FF ** -0.5),
        "ffn1_post_g": gain(ks[4], D_MODEL),
        "mix_pre_g": gain(ks[5], D_MODEL),
        "w_in": nrm(ks[6], (DEPTH, D_MODEL, D_IN), D_MODEL ** -0.5),
        "conv_w": nrm(ks[7], (DEPTH, CONV_WIDTH, D_LRU), CONV_WIDTH ** -0.5),
        "conv_b": nrm(ks[8], (DEPTH, D_LRU), 0.01),
        "w_rg": nrm(ks[9], (DEPTH, LRU_BLOCKS, LRU_BLOCK, LRU_BLOCK), LRU_BLOCK ** -0.5),
        "b_rg": nrm(ks[10], (DEPTH, D_LRU), 0.01),
        "w_ig": nrm(ks[11], (DEPTH, LRU_BLOCKS, LRU_BLOCK, LRU_BLOCK), LRU_BLOCK ** -0.5),
        "b_ig": nrm(ks[12], (DEPTH, D_LRU), 0.01),
        "lru_lambda": jnp.log(u) - jnp.log1p(-u),
        "sinks": nrm(ks[14], (DEPTH, N_HEADS), 1.0),
        "g_lru_out": gain(ks[15], D_LRU),
        "g_attn_out": gain(ks[16], D_ATTN),
        "w_o": nrm(ks[17], (DEPTH, D_MIX, D_MODEL), D_MIX ** -0.5),
        "mix_post_g": gain(ks[18], D_MODEL),
        "ffn2_pre_g": gain(ks[19], D_MODEL),
        "ffn2_w_gu": nrm(ks[20], (DEPTH, D_MODEL, 2 * D_FF), D_MODEL ** -0.5),
        "ffn2_w_down": nrm(ks[21], (DEPTH, D_FF, D_MODEL), D_FF ** -0.5),
        "ffn2_post_g": gain(ks[22], D_MODEL),
    }

def first_block(x, ffn1_pre_g, ffn1_w_gu, ffn1_w_down, ffn1_post_g, mix_pre_g, w_in, conv_w, conv_b,
              w_rg, b_rg, w_ig, b_ig, lru_lambda, sinks, g_lru_out, g_attn_out, w_o, mix_post_g,
              ffn2_pre_g, ffn2_w_gu, ffn2_w_down, ffn2_post_g):
    for l in range(DEPTH):
        x = x + 0.5 * rms_norm(swiglu(rms_norm(x, ffn1_pre_g[l]), ffn1_w_gu[l], ffn1_w_down[l]), ffn1_post_g[l])
        y = hybrid_mixer(rms_norm(x, mix_pre_g[l]), w_in[l], conv_w[l], conv_b[l], w_rg[l], b_rg[l],
                         w_ig[l], b_ig[l], lru_lambda[l], sinks[l], g_lru_out[l], g_attn_out[l], w_o[l])
        x = x + rms_norm(y, mix_post_g[l])
        x = x + 0.5 * rms_norm(swiglu(rms_norm(x, ffn2_pre_g[l]), ffn2_w_gu[l], ffn2_w_down[l]), ffn2_post_g[l])
    return x


DEPTH_2 = 2

GRID_W = 64
CTX_LEN = 256
N_MIXERS = 4
D_FF_2 = -(-8 * D_MODEL // (3 * 256)) * 256
DEEPNORM_ALPHA = (2 * DEPTH_2) ** 0.25
DEEPNORM_BETA = (8 * DEPTH_2) ** -0.25
LN_EPS = 1e-5
ROPE_BASE = 10000.0
CHUNK = 64
NEG_INF = -1e30

RET_HEADS = 4
RET_DK = D_MODEL // RET_HEADS
RET_DV = 2 * RET_DK
NA_HEADS = 16
NA_DH = D_MODEL // NA_HEADS
NA_WIN_ROWS = 8
NA_WIN_COLS = 16
NA_QBLOCK_W = 16
NA_BAND_W = NA_QBLOCK_W + NA_WIN_COLS
MLA_HEADS = 16
MLA_NOPE = 64
MLA_ROPE = 32
MLA_V = 64
MLA_Q_LORA = 512
MLA_KV_LORA = 256
MLA_QBLOCK = 128
HG_EXPAND = 128
HG_HEADS = D_MODEL // HG_EXPAND
HG_DI = D_MODEL // HG_HEADS
HG_FDIM = HG_HEADS * HG_EXPAND


def layer_norm(x, g, b):
    xf = x.astype(jnp.float32)
    xc = xf - jnp.mean(xf, -1, keepdims=True)
    var = jnp.mean(xc * xc, -1, keepdims=True)
    return (xc * lax.rsqrt(var + LN_EPS) * g.astype(jnp.float32) + b.astype(jnp.float32)).astype(x.dtype)

def rms_norm_2(x, g=None):
    xf = x.astype(jnp.float32)
    y = xf * lax.rsqrt(jnp.mean(xf * xf, -1, keepdims=True) + RMS_EPS)
    if g is not None:
        y = y * g.astype(jnp.float32)
    return y.astype(x.dtype)

def modulate(h, shift, scale):
    return h * (1 + scale) + shift

def axial_rope(n_tokens, rot_dim):
    t = jnp.arange(n_tokens)
    rows = (t // GRID_W).astype(jnp.float32)
    cols = (t % GRID_W).astype(jnp.float32)
    n_freq = rot_dim // 4
    inv = ROPE_BASE ** (-jnp.arange(n_freq, dtype=jnp.float32) / n_freq)
    ang = jnp.concatenate([rows[:, None] * inv, cols[:, None] * inv], -1)
    return jnp.cos(ang)[:, None, :], jnp.sin(ang)[:, None, :]

def apply_rope(x, cos, sin):
    x1, x2 = jnp.split(x.astype(jnp.float32), 2, axis=-1)
    return jnp.concatenate([x1 * cos - x2 * sin, x1 * sin + x2 * cos], -1).astype(x.dtype)

def chunk_gla(q, k, v, log_f, s0):
    B, H, L, dk = q.shape
    dv = v.shape[-1]
    n = L // CHUNK

    def to_chunks(a):
        return a.astype(jnp.float32).reshape(B, H, n, CHUNK, a.shape[-1]).transpose(2, 0, 1, 3, 4)

    mask = jnp.tril(jnp.ones((CHUNK, CHUNK), bool))

    def step(S, inp):
        qi, ki, vi, gi = inp
        b = jnp.cumsum(gi, axis=-2)
        b_last = b[..., -1:, :]
        q_d = qi * jnp.exp(b)
        att = jnp.where(mask, jnp.einsum('bhtk,bhsk->bhts', q_d, ki * jnp.exp(-b)), 0.0)
        o = jnp.einsum('bhts,bhsv->bhtv', att, vi) + jnp.einsum('bhtk,bhkv->bhtv', q_d, S)
        S_new = jnp.exp(b_last[..., 0, :])[..., None] * S + jnp.einsum('bhsk,bhsv->bhkv', ki * jnp.exp(b_last - b), vi)
        return S_new, o

    S_fin, oc = lax.scan(step, s0, (to_chunks(q), to_chunks(k), to_chunks(v), to_chunks(log_f)))
    return oc.transpose(1, 2, 0, 3, 4).reshape(B, H, L, dv), S_fin

def bidirectional_scan(ctx_terms, lat_terms):
    qc, kcf, kcb, vc, gcf, gcb = ctx_terms
    ql, klf, klb, vl, glf, glb = lat_terms
    B, H, _, dk = qc.shape
    s0 = jnp.zeros((B, H, dk, vc.shape[-1]), jnp.float32)
    flip = lambda t: jnp.flip(t, axis=2)
    o_cf, s_cf = chunk_gla(qc, kcf, vc, gcf, s0)
    o_cb, s_cb = chunk_gla(flip(qc), flip(kcb), flip(vc), flip(gcb), s0)
    o_lf, _ = chunk_gla(ql, klf, vl, glf, s_cf)
    o_lb, _ = chunk_gla(flip(ql), flip(klb), flip(vl), flip(glb), s_cb)
    return o_cf + flip(o_cb), o_lf + flip(o_lb)

def retention_mixer(a_ctx, a_lat, w_in, decay_param, w_out, want_ctx):
    B, L, _ = a_lat.shape
    hk, hv = RET_HEADS * RET_DK, RET_HEADS * RET_DV
    log_gamma = -jnp.exp(decay_param.astype(jnp.float32))

    def project(a, rope):
        n = a.shape[1]
        q, k, v, g = jnp.split(a @ w_in, [hk, 2 * hk, 2 * hk + hv], axis=-1)
        q = q.reshape(B, n, RET_HEADS, RET_DK)
        k = k.reshape(B, n, RET_HEADS, RET_DK)
        if rope is not None:
            q, k = apply_rope(q, *rope), apply_rope(k, *rope)
        k = k * RET_DK ** -0.5
        v = v.reshape(B, n, RET_HEADS, RET_DV)
        decay = lambda lg: jnp.broadcast_to(lg[None, :, None, None], (B, RET_HEADS, n, RET_DK))
        qh, kh, vh = (t.transpose(0, 2, 1, 3) for t in (q, k, v))
        return (qh, kh, kh, vh, decay(log_gamma[0]), decay(log_gamma[1])), g

    ctx_terms, g_ctx = project(a_ctx, None)
    lat_terms, g_lat = project(a_lat, axial_rope(L, RET_DK))
    o_ctx, o_lat = bidirectional_scan(ctx_terms, lat_terms)

    def readout(o, g):
        n = o.shape[2]
        y = rms_norm_2(o).transpose(0, 2, 1, 3).reshape(B, n, hv).astype(g.dtype)
        return (jax.nn.silu(g) * y) @ w_out

    return (readout(o_ctx, g_ctx) if want_ctx else None), readout(o_lat, g_lat)

def neighbourhood_mixer(a_ctx, a_lat, w_qkv, rpb, w_out, want_ctx):
    B, L, _ = a_lat.shape
    Lc = a_ctx.shape[1]
    rows = L // GRID_W
    wr = min(NA_WIN_ROWS, rows)
    scale = NA_DH ** -0.5
    q, k, v = jnp.split(a_lat @ w_qkv, 3, axis=-1)
    grid = lambda t: t.reshape(B, rows, GRID_W, NA_HEADS, NA_DH)
    q, k, v = grid(q * scale), grid(k), grid(v)
    qc, kc, vc = (t.reshape(B, Lc, NA_HEADS, NA_DH) for t in jnp.split(a_ctx @ w_qkv, 3, axis=-1))

    n_cb = GRID_W // NA_QBLOCK_W
    band0 = np.clip(np.arange(n_cb) * NA_QBLOCK_W - NA_WIN_COLS // 2, 0, GRID_W - NA_BAND_W)
    kcol = band0[:, None] + np.arange(NA_BAND_W)
    qcol = np.arange(GRID_W).reshape(n_cb, NA_QBLOCK_W)
    wstart = np.clip(qcol - NA_WIN_COLS // 2, 0, GRID_W - NA_WIN_COLS)
    kc3 = kcol[:, None, :]
    col_ok = (kc3 >= wstart[..., None]) & (kc3 < wstart[..., None] + NA_WIN_COLS)
    c_idx = np.clip(kc3 - qcol[..., None] + NA_WIN_COLS - 1, 0, 2 * NA_WIN_COLS - 2)

    def row(r):
        rs = jnp.clip(r - wr // 2, 0, rows - wr)
        qr = lax.dynamic_index_in_dim(q, r, axis=1, keepdims=False).reshape(B, n_cb, NA_QBLOCK_W, NA_HEADS, NA_DH)
        kb = lax.dynamic_slice_in_dim(k, rs, wr, axis=1)[:, :, kcol]
        vb = lax.dynamic_slice_in_dim(v, rs, wr, axis=1)[:, :, kcol]
        r_idx = rs + jnp.arange(wr) - r + NA_WIN_ROWS - 1
        bias = rpb[:, r_idx[None, None, :, None], c_idx[:, :, None, :]]
        s_lat = jnp.einsum('bnqhd,brnkhd->bhnqrk', qr, kb).astype(jnp.float32) + bias[None].astype(jnp.float32)
        s_lat = jnp.where(col_ok[:, :, None, :], s_lat, NEG_INF).reshape(B, NA_HEADS, n_cb, NA_QBLOCK_W, wr * NA_BAND_W)
        s_ctx = jnp.einsum('bnqhd,bchd->bhnqc', qr, kc).astype(jnp.float32)
        p = jax.nn.softmax(jnp.concatenate([s_lat, s_ctx], -1), -1).astype(v.dtype)
        p_lat = p[..., :wr * NA_BAND_W].reshape(B, NA_HEADS, n_cb, NA_QBLOCK_W, wr, NA_BAND_W)
        o = jnp.einsum('bhnqrk,brnkhd->bnqhd', p_lat, vb) + jnp.einsum('bhnqc,bchd->bnqhd', p[..., wr * NA_BAND_W:], vc)
        return o.reshape(B, GRID_W, NA_HEADS * NA_DH)

    o_lat = lax.map(row, jnp.arange(rows)).transpose(1, 0, 2, 3).reshape(B, L, NA_HEADS * NA_DH)
    y_ctx = None
    if want_ctx:
        s = jnp.einsum('bqhd,bkhd->bhqk', qc * scale, kc).astype(jnp.float32)
        p = jax.nn.softmax(s, -1).astype(vc.dtype)
        y_ctx = jnp.einsum('bhqk,bkhd->bqhd', p, vc).reshape(B, Lc, NA_HEADS * NA_DH) @ w_out
    return y_ctx, o_lat @ w_out

def mla_mixer(a_ctx, a_lat, w_down, q_norm, kv_norm, w_uq, w_ukv, w_out, want_ctx):
    B, L, _ = a_lat.shape
    scale = (MLA_NOPE + MLA_ROPE) ** -0.5

    def project(a, rope):
        n = a.shape[1]
        cq, ckv, kr = jnp.split(a @ w_down, [MLA_Q_LORA, MLA_Q_LORA + MLA_KV_LORA], axis=-1)
        q = (rms_norm_2(cq, q_norm) @ w_uq).reshape(B, n, MLA_HEADS, MLA_NOPE + MLA_ROPE)
        kv = (rms_norm_2(ckv, kv_norm) @ w_ukv).reshape(B, n, MLA_HEADS, MLA_NOPE + MLA_V)
        q_nope, q_rope = jnp.split(q, [MLA_NOPE], axis=-1)
        k_nope, v = jnp.split(kv, [MLA_NOPE], axis=-1)
        kr = kr[:, :, None, :]
        if rope is not None:
            q_rope, kr = apply_rope(q_rope, *rope), apply_rope(kr, *rope)
        q = jnp.concatenate([q_nope, q_rope], -1) * scale
        k = jnp.concatenate([k_nope, jnp.broadcast_to(kr, (B, n, MLA_HEADS, MLA_ROPE))], -1)
        return q, k, v

    qc, kc, vc = project(a_ctx, None)
    ql, kl, vl = project(a_lat, axial_rope(L, MLA_ROPE))
    k_all = jnp.concatenate([kc, kl], axis=1)
    v_all = jnp.concatenate([vc, vl], axis=1)

    def attend(qb, keys, vals):
        s = jnp.einsum('bqhd,bkhd->bhqk', qb, keys).astype(jnp.float32)
        p = jax.nn.softmax(s, -1).astype(vals.dtype)
        return jnp.einsum('bhqk,bkhd->bqhd', p, vals)

    nb = L // MLA_QBLOCK
    qblocks = ql.reshape(B, nb, MLA_QBLOCK, MLA_HEADS, MLA_NOPE + MLA_ROPE).transpose(1, 0, 2, 3, 4)
    o = lax.map(lambda qb: attend(qb, k_all, v_all), qblocks)
    o_lat = o.transpose(1, 0, 2, 3, 4).reshape(B, L, MLA_HEADS * MLA_V)
    y_ctx = attend(qc, kc, vc).reshape(B, -1, MLA_HEADS * MLA_V) @ w_out if want_ctx else None
    return y_ctx, o_lat @ w_out

def hgrn2_mixer(a_ctx, a_lat, w_in, lower_bounds, norm_g, w_out, layer_idx, want_ctx):
    B = a_lat.shape[0]
    lb_soft = jax.nn.softmax(lower_bounds.astype(jnp.float32), axis=0)
    lb = (jnp.cumsum(lb_soft, axis=0) - lb_soft[0])[layer_idx]

    def project(a):
        n = a.shape[1]
        q, f_f, f_b, i, g = jnp.split(a @ w_in, [HG_FDIM, 2 * HG_FDIM, 3 * HG_FDIM, 3 * HG_FDIM + HG_HEADS * HG_DI], axis=-1)
        heads = lambda t, d: t.reshape(B, n, HG_HEADS, d).transpose(0, 2, 1, 3)
        q = heads(jax.nn.silu(q), HG_EXPAND) * HG_EXPAND ** -0.5

        def gate(f):
            forget = lb + (1 - lb) * jax.nn.sigmoid(f.astype(jnp.float32))
            return heads(1 - forget, HG_EXPAND), heads(jnp.log(forget), HG_EXPAND)

        kf, gf = gate(f_f)
        kb, gb = gate(f_b)
        return (q, kf, kb, heads(i, HG_DI), gf, gb), g

    ctx_terms, g_ctx = project(a_ctx)
    lat_terms, g_lat = project(a_lat)
    o_ctx, o_lat = bidirectional_scan(ctx_terms, lat_terms)

    def readout(o, g):
        n = o.shape[2]
        y = rms_norm_2(o, norm_g).transpose(0, 2, 1, 3).reshape(B, n, HG_HEADS * HG_DI).astype(g.dtype)
        return (y * jax.nn.silu(g)) @ w_out

    return (readout(o_ctx, g_ctx) if want_ctx else None), readout(o_lat, g_lat)

def swiglu_2(a, w13, w2):
    gate, up = jnp.split(a @ w13, 2, axis=-1)
    return (jax.nn.silu(gate) * up) @ w2

def second_inputs(seed: int = 0) -> dict:
    key = jax.random.key(seed)
    ks = iter(jax.random.split(key, 32))
    nrm = lambda shape, std: std * jax.random.normal(next(ks), shape, jnp.float32)
    D, F, beta = D_MODEL, D_FF_2, DEEPNORM_BETA
    ret_decay_base = jnp.log(-jnp.log1p(-(2.0 ** (-5.0 - jnp.arange(RET_HEADS, dtype=jnp.float32)))))
    return {
        'x': nrm((BATCH, SEQ, D), 1.0),
        'c': nrm((BATCH, D), 1.0),
        'ctx': nrm((BATCH, CTX_LEN, D), 1.0),
        'c_ctx': nrm((D,), 1.0),
        'ada_w': nrm((DEPTH_2, D, 6 * D), D ** -0.5),
        'ada_b': nrm((DEPTH_2, 6 * D), 0.01),
        'ln_g': 1.0 + nrm((DEPTH_2, 2, D), 0.01),
        'ln_b': nrm((DEPTH_2, 2, D), 0.01),
        'ffn_w13': nrm((DEPTH_2, D, 2 * F), D ** -0.5),
        'ffn_w2': nrm((DEPTH_2, F, D), beta * F ** -0.5),
        'ret_w_in': nrm((D, 2 * RET_HEADS * RET_DK + 2 * RET_HEADS * RET_DV), D ** -0.5),
        'ret_decay': ret_decay_base[None, :] + nrm((2, RET_HEADS), 0.01),
        'ret_w_out': nrm((RET_HEADS * RET_DV, D), beta * (RET_HEADS * RET_DV) ** -0.5),
        'na_w_qkv': nrm((D, 3 * NA_HEADS * NA_DH), D ** -0.5),
        'na_rpb': nrm((NA_HEADS, 2 * NA_WIN_ROWS - 1, 2 * NA_WIN_COLS - 1), 0.02),
        'na_w_out': nrm((NA_HEADS * NA_DH, D), beta * (NA_HEADS * NA_DH) ** -0.5),
        'mla_w_down': nrm((D, MLA_Q_LORA + MLA_KV_LORA + MLA_ROPE), D ** -0.5),
        'mla_q_norm': 1.0 + nrm((MLA_Q_LORA,), 0.01),
        'mla_kv_norm': 1.0 + nrm((MLA_KV_LORA,), 0.01),
        'mla_w_uq': nrm((MLA_Q_LORA, MLA_HEADS * (MLA_NOPE + MLA_ROPE)), MLA_Q_LORA ** -0.5),
        'mla_w_ukv': nrm((MLA_KV_LORA, MLA_HEADS * (MLA_NOPE + MLA_V)), MLA_KV_LORA ** -0.5),
        'mla_w_out': nrm((MLA_HEADS * MLA_V, D), beta * (MLA_HEADS * MLA_V) ** -0.5),
        'hg_w_in': nrm((D, 3 * HG_FDIM + 2 * HG_HEADS * HG_DI), D ** -0.5),
        'hg_lower_bounds': nrm((DEPTH_2, HG_FDIM), 0.1),
        'hg_norm_g': 1.0 + nrm((HG_DI,), 0.01),
        'hg_w_out': nrm((HG_HEADS * HG_DI, D), beta * (HG_HEADS * HG_DI) ** -0.5),
    }

def second_block(x, c, ctx, c_ctx, ada_w, ada_b, ln_g, ln_b, ffn_w13, ffn_w2,
              ret_w_in, ret_decay, ret_w_out,
              na_w_qkv, na_rpb, na_w_out,
              mla_w_down, mla_q_norm, mla_kv_norm, mla_w_uq, mla_w_ukv, mla_w_out,
              hg_w_in, hg_lower_bounds, hg_norm_g, hg_w_out):
    h_lat, h_ctx = x, ctx
    cond_lat = jax.nn.silu(c)[:, None, :]
    cond_ctx = jax.nn.silu(c_ctx)[None, None, :]
    for i in range(DEPTH_2):
        want_ctx = i < DEPTH_2 - 1
        m_lat = jnp.split(cond_lat @ ada_w[i] + ada_b[i], 6, axis=-1)
        m_ctx = jnp.split(cond_ctx @ ada_w[i] + ada_b[i], 6, axis=-1)
        a_lat = modulate(h_lat, m_lat[0], m_lat[1])
        a_ctx = modulate(h_ctx, m_ctx[0], m_ctx[1])
        kind = i % N_MIXERS
        if kind == 0:
            y_ctx, y_lat = retention_mixer(a_ctx, a_lat, ret_w_in, ret_decay, ret_w_out, want_ctx)
        elif kind == 1:
            y_ctx, y_lat = neighbourhood_mixer(a_ctx, a_lat, na_w_qkv, na_rpb, na_w_out, want_ctx)
        elif kind == 2:
            y_ctx, y_lat = mla_mixer(a_ctx, a_lat, mla_w_down, mla_q_norm, mla_kv_norm, mla_w_uq, mla_w_ukv, mla_w_out, want_ctx)
        else:
            y_ctx, y_lat = hgrn2_mixer(a_ctx, a_lat, hg_w_in, hg_lower_bounds, hg_norm_g, hg_w_out, i, want_ctx)
        h_lat = layer_norm(DEEPNORM_ALPHA * h_lat + m_lat[2] * y_lat, ln_g[i, 0], ln_b[i, 0])
        f_lat = swiglu_2(modulate(h_lat, m_lat[3], m_lat[4]), ffn_w13[i], ffn_w2[i])
        h_lat = layer_norm(DEEPNORM_ALPHA * h_lat + m_lat[5] * f_lat, ln_g[i, 1], ln_b[i, 1])
        if want_ctx:
            h_ctx = layer_norm(DEEPNORM_ALPHA * h_ctx + m_ctx[2] * y_ctx, ln_g[i, 0], ln_b[i, 0])
            f_ctx = swiglu_2(modulate(h_ctx, m_ctx[3], m_ctx[4]), ffn_w13[i], ffn_w2[i])
            h_ctx = layer_norm(DEEPNORM_ALPHA * h_ctx + m_ctx[5] * f_ctx, ln_g[i, 1], ln_b[i, 1])
    return h_lat


def setup_inputs(seed=0):
    out = dict(first_inputs(seed))
    for name, value in second_inputs(seed + 1).items():
        if name != "x":
            out[name + "_2"] = value
    return out


def reference(
    x, ffn1_pre_g, ffn1_w_gu, ffn1_w_down, ffn1_post_g, mix_pre_g, w_in, conv_w, conv_b, w_rg,
    b_rg, w_ig, b_ig, lru_lambda, sinks, g_lru_out, g_attn_out, w_o, mix_post_g, ffn2_pre_g,
    ffn2_w_gu, ffn2_w_down, ffn2_post_g, c_2, ctx_2, c_ctx_2, ada_w_2, ada_b_2, ln_g_2, ln_b_2,
    ffn_w13_2, ffn_w2_2, ret_w_in_2, ret_decay_2, ret_w_out_2, na_w_qkv_2, na_rpb_2, na_w_out_2,
    mla_w_down_2, mla_q_norm_2, mla_kv_norm_2, mla_w_uq_2, mla_w_ukv_2, mla_w_out_2, hg_w_in_2,
    hg_lower_bounds_2, hg_norm_g_2, hg_w_out_2,
):
    x = first_block(
        x, ffn1_pre_g, ffn1_w_gu, ffn1_w_down, ffn1_post_g, mix_pre_g, w_in, conv_w, conv_b,
        w_rg, b_rg, w_ig, b_ig, lru_lambda, sinks, g_lru_out, g_attn_out, w_o, mix_post_g,
        ffn2_pre_g, ffn2_w_gu, ffn2_w_down, ffn2_post_g,
    )
    return second_block(
        x, c_2, ctx_2, c_ctx_2, ada_w_2, ada_b_2, ln_g_2, ln_b_2, ffn_w13_2, ffn_w2_2,
        ret_w_in_2, ret_decay_2, ret_w_out_2, na_w_qkv_2, na_rpb_2, na_w_out_2, mla_w_down_2,
        mla_q_norm_2, mla_kv_norm_2, mla_w_uq_2, mla_w_ukv_2, mla_w_out_2, hg_w_in_2,
        hg_lower_bounds_2, hg_norm_g_2, hg_w_out_2,
    )


_drawn_inputs = setup_inputs


def setup_inputs(seed=0):
    import zlib

    import numpy as np

    out = dict(_drawn_inputs(seed))
    spreads = {}
    factors = {'b_rg': 23.322,
     'b_ig': 8.0,
     'ffn2_post_g': 3.373,
     'ada_b_2': 5.858,
     'ln_g_2': 2.856,
     'ln_b_2': 2.764,
     'na_rpb_2': 64.0}
    for name, (base, spread) in spreads.items():
        noise = np.random.default_rng([zlib.crc32(name.encode()), seed]).standard_normal(out[name].shape)
        drawn = base * np.exp(spread * noise) if base else spread * noise
        out[name] = __import__('jax').numpy.asarray(drawn.astype(out[name].dtype))
    for name, factor in factors.items():
        out[name] = (out[name] * factor).astype(out[name].dtype)
    return out
```

```python
import numpy as np
from contextlib import ExitStack

import concourse.bass as bass
from concourse import mybir

ALU = mybir.AluOpType
ACT = mybir.ActivationFunctionType
F32 = mybir.dt.float32
F32R = mybir.dt.float32r
AX_X = mybir.AxisListType.X

P = 128
L = 512
LC = 256
D = 1024
DC = D // P
FC = 2816 // P
SLOT = 1024
NR = 3
NH = 4
PARTS1 = (8, 7, 7)
PARTS2 = (5, 5, 4, 4, 4)
ALPHA = float((2 * 2) ** 0.25)
RMS_EPS = 1e-6
LN_EPS = 1e-5
NEG = -1e30
SEG1 = ((0, 512),)
SEG2 = ((0, 512), (512, 256))
HEAD_ORDER = (0, 4, 1, 5, 2, 6, 3, 7)

PARAMS = [
    ("ffn1_pre_g", 8), ("ffn1_post_g", 8), ("mix_pre_g", 8), ("conv_w", 16), ("conv_b", 4),
    ("b_rg", 4), ("b_ig", 4), ("lam", 4), ("g_mix", 8), ("mix_post_g", 8),
    ("ffn2_pre_g", 8), ("ffn2_post_g", 8), ("cond", 16), ("ada_b", 96), ("ln_g", 32), ("ln_b", 32),
    ("sinks", 8), ("decay", 8),
]
POFF, _n = {}, 0
for _name, _w in PARAMS:
    POFF[_name] = _n
    _n += _w
NPAR = _n

CONSTS = [("ident", 128), ("one1024", 128), ("one512", 128), ("comb", 2), ("eps", 2)]


class Engines:

    def __init__(self, sem):
        self.sem = sem
        self.queues = {k: [] for k in ("pe", "act", "dve", "pool", "sp")}
        self.now = {}
        self.count = {}
        self.waited = {}

    def stage(self, name):
        for k in ("pe", "act", "dve", "pool"):
            self.now[k] = self.sem(f"s_{k}_{name}")

    def wait(self, eng, *tokens):
        for t in tokens:
            if t is None:
                continue
            if isinstance(t, list):
                self.wait(eng, *t)
                continue
            s, v = t
            if self.waited.get((eng, id(s)), 0) < v:
                self.waited[(eng, id(s))] = v
                self.queues[eng].append(lambda e, s=s, v=v: e.wait_ge(s, v))

    def op(self, eng, waits, fn, signal=True, sem=None, step=1):
        self.wait(eng, *waits)
        if not signal:
            self.queues[eng].append(fn)
            return None
        s = self.now[eng] if sem is None else sem
        self.count[id(s)] = self.count.get(id(s), 0) + step
        self.queues[eng].append(lambda e: fn(e).then_inc(s, step))
        return (s, self.count[id(s)])

    def replay(self, eng, e):
        for fn in self.queues[eng]:
            fn(e)


def queue_program(q, mem, dram, sems, plan, seen):
    X, H, HID, WHI, WLO, RAW = mem["X"], mem["H"], mem["HID"], mem["WHI"], mem["WLO"], mem["RAW"]
    M, TMP, PAR, CON, MOD, PS = mem["MISC"], mem["TMP"], mem["PAR"], mem["CON"], mem["MOD"], mem["PS"]

    def pe(waits, fn, signal=True):
        return q.op("pe", waits, fn, signal)

    def act(waits, fn):
        return q.op("act", waits, fn)

    def dve(waits, fn):
        return q.op("dve", waits, fn)

    def pool(waits, fn):
        return q.op("pool", waits, fn)

    def load(waits, dst, src, sem):
        return q.op("sp", waits, lambda e: e.dma_start(dst, src), sem=sem, step=16)

    def par(name, c, p0=0, p1=P):
        return PAR[p0:p1, POFF[name] + c:POFF[name] + c + 1]

    ident = CON[:, 0:128]
    one1024 = CON[:, 128:256]
    one512 = CON[:, 256:384]
    comb = CON[0:4, 384:386]
    EPS = {RMS_EPS: CON[:, 386:387], LN_EPS: CON[:, 387:388]}

    free = {b: [] for b in range(8)}
    turn = {}

    def bank(pool_=(0, 1, 2, 3, 4, 5)):
        i = turn.get(pool_, 0)
        turn[pool_] = i + 1
        return pool_[i % len(pool_)]

    ring = {"used": 0, "conv": 0, "dma": 0}
    dma_done, hi_done, lo_done, mm_done = {}, {}, {}, {}

    def issue_load(j):
        if j < NR:
            waits = []
        else:
            waits = [hi_done[j - NR], lo_done[j - NR]]
        src, shape = plan[j]
        n = int(np.prod(shape))
        dst = RAW[:, j % NR, 0:n]
        if len(shape) == 2:
            dst = dst.rearrange("p (a b) -> p a b", a=shape[0])
        dma_done[j] = load(waits, dst, src, sems["ring"][j % NR])

    def issue_split(j):
        n = int(np.prod(plan[j][1]))
        over = [mm_done[j - NH]] if j >= NH else []
        raw, hi, lo = RAW[:, j % NR, 0:n], WHI[:, j % NH, 0:n], WLO[:, j % NH, 0:n]
        hi_done[j] = act([dma_done[j], *over], lambda e: e.copy(hi, raw))
        lo_done[j] = dve([dma_done[j], hi_done[j], *over], lambda e: e.tensor_tensor(lo, raw, hi, ALU.subtract))

    def next_block(src, shape):
        j = ring["used"]
        ring["used"] += 1
        seen.append((src, shape))
        if plan is None:
            return j % NH, []
        while ring["conv"] < min(j + NH, len(plan)):
            k = ring["conv"]
            while ring["dma"] < min(k + NR, len(plan)) and (ring["dma"] < NR or ring["dma"] - NR < k):
                issue_load(ring["dma"])
                ring["dma"] += 1
            issue_split(k)
            ring["conv"] += 1
        return j % NH, [hi_done[j], lo_done[j]]

    def block_over(token):
        mm_done[ring["used"] - 1] = token

    def products(out, whi, wlo, xhi, xlo, waits, first, last, signal):
        pe(waits, lambda e: e.matmul(out, whi, xlo, start=first, stop=False), False)
        pe([], lambda e: e.matmul(out, wlo, xhi, start=False, stop=False), False)
        return pe([], lambda e: e.matmul(out, whi, xhi, start=False, stop=last), signal)

    def xs(c, t0=0, n=L):
        return X[:, c * 768 + t0:c * 768 + t0 + n]

    def hs(part, c, t0, n):
        base = part * 6144 + c * 768 + t0
        return H[:, base:base + n]

    def column_groups(src, shape, nk, segs, acts, act_waits, post, banks=None, sub=None):
        slot, ready = next_block(src, shape)
        done = None
        for t0, n in segs:
            b = bank(banks) if banks else bank()
            out = PS[:, b, 0:n]
            base = 0 if sub is None else sub
            for k in range(nk):
                xhi, xlo = acts(0, k, t0, n), acts(1, k, t0, n)
                whi = WHI[:, slot, base + k * P:base + (k + 1) * P]
                wlo = WLO[:, slot, base + k * P:base + (k + 1) * P]
                done = products(out, whi, wlo, xhi, xlo, [*ready, *act_waits(k, t0), *(free[b] if k == 0 else [])],
                                k == 0, k == nk - 1, k == nk - 1)
            free[b] = post(b, t0, n, done)
        block_over(done)
        return done

    ra = {"a": 0, "b": 0}
    rfree = {("a", 0): [], ("a", 1): [], ("b", 0): [], ("b", 1): []}

    def tmp(which, n):
        i = ra[which] % 2
        ra[which] += 1
        base = (0 if which == "a" else 1024) + i * 512
        return TMP[:, base:base + n], (which, i)

    def rs_view(n, t0=0):
        return TMP[:, 2048 + t0:2048 + t0 + n]

    def split(hi, lo, src, waits, over):
        a = act([waits, over], lambda e: e.copy(hi, src))
        d = dve([waits, over, a], lambda e: e.tensor_tensor(lo, src, hi, ALU.subtract))
        return [a, d]

    def mean_square(tiles, waits, n, ones, b):
        last = None
        for i, t in enumerate(tiles):
            sq, key = tmp("a", n)
            a = act([waits[i], rfree[key]], lambda e, sq=sq, t=t: e.activation(sq, t, ACT.Square))
            last = pe([a, *(free[b] if i == 0 else [])],
                      lambda e, sq=sq, i=i: e.matmul(PS[:, b, 0:n], ones, sq, start=i == 0, stop=i == len(tiles) - 1))
            rfree[key] = [last]
        return last

    def rstd(b, n, t0, waits, eps, over):
        a = act([waits, over], lambda e: e.activation(rs_view(n, t0), PS[:, b, 0:n], ACT.Sqrt, bias=EPS[eps]))
        free[b] = [a]
        return dve([a], lambda e: e.reciprocal(rs_view(n, t0), rs_view(n, t0)))

    rs_readers = {0: [], 512: []}

    def rms_to_h(gain, x_ready, over):
        b = bank()
        s = mean_square([xs(c) for c in range(DC)], x_ready, L, one1024, b)
        r = rstd(b, L, 0, s, RMS_EPS, rs_readers[0])
        ready = []
        rs_readers[0] = []
        for c in range(DC):
            t, key = tmp("b", L)
            d = dve([x_ready[c], r, rfree[key]], lambda e, t=t, c=c: e.scalar_tensor_tensor(
                out=t, in0=xs(c), scalar=par(gain, c), in1=rs_view(L), op0=ALU.mult, op1=ALU.mult))
            rs_readers[0] = [d]
            got = split(hs(0, c, 0, L), hs(1, c, 0, L), t, d, over)
            rfree[key] = got
            ready.append(got)
        return ready

    ada = {"n": 0, "limit": 48}
    ABANK, MBANK = 6, 7

    def ada_step():
        i = ada["n"]
        if i >= ada["limit"]:
            return
        ada["n"] += 1
        layer, r = divmod(i, 48)
        n, blk = divmod(r, 4)
        slot, ready = next_block(dram["ada"][layer, n, blk], (SLOT,))
        out = PS[:, ABANK, 0:512]
        done = None
        for kk in range(2):
            k = blk * 2 + kk
            cnd = H[:, k * 768 + 512:k * 768 + 640]
            for w in (WHI, WLO):
                first = k == 0 and w is WHI
                last = k == 7 and w is WLO
                mv = w[:, slot, kk * 512:(kk + 1) * 512]
                done = pe([*ready, *cond_ready, *(free[ABANK] if first else [])],
                          lambda e, cnd=cnd, mv=mv, first=first, last=last: e.matmul(out, cnd, mv, start=first, stop=last),
                          kk == 1 and w is WLO)
        block_over(done)
        if blk < 3:
            return
        row = X[0:4, 0:1536].rearrange("p (c t) -> p c t", t=768)[:, :, 512:768]
        a = act([done, ada.get("row_read")], lambda e: e.copy(row, PS[0:4, ABANK, 0:512].rearrange("p (c t) -> p c t", c=2)))
        free[ABANK] = [a]
        for j in range(4):
            col = n * 4 + j
            ada["row_read"] = pe([a, *(free[MBANK] if col == 0 else [])], lambda e, j=j, col=col: e.matmul(
                PS[:, MBANK, col * 2:col * 2 + 2],
                X[0:4, (j // 2) * 768 + 512 + (j % 2) * 128:(j // 2) * 768 + 640 + (j % 2) * 128], comb,
                start=True, stop=True, skip_group_check=True))
        if n < 11:
            return
        for who in range(2):
            src = PS[:, MBANK, 0:96].rearrange("p (c w) -> p w c", w=2)[:, who, :]
            d = dve([ada["row_read"], par_ready], lambda e, src=src, who=who: e.tensor_tensor(
                MOD[:, (layer * 2 + who) * 48:(layer * 2 + who + 1) * 48], src,
                PAR[:, POFF["ada_b"] + layer * 48:POFF["ada_b"] + layer * 48 + 48], ALU.add))
            for g in (1, 4):
                v = MOD[:, (layer * 2 + who) * 48 + g * 8:(layer * 2 + who) * 48 + g * 8 + 8]
                mod_ready[layer] = dve([d], lambda e, v=v: e.tensor_scalar(v, v, 1.0, None, ALU.add))
        free[MBANK] = [d]

    mod_ready = {}

    def mod(layer, who, g, c):
        o = (layer * 2 + who) * 48 + g * 8 + c
        return MOD[:, o:o + 1]

    def ffn(gu, dn, parts, segs, h_ready, down_post, between=None):
        def hid(half, k, t0, n):
            base = half * 4096 + k * (512 if len(segs) == 1 else 768) + t0
            return HID[:, base:base + n]

        hacts = lambda half, k, t0, n: hs(half, k, t0, n)
        c0 = 0
        over = state["hid_over"]
        last = None
        for pi, size in enumerate(parts):
            ready = {}
            for k in range(size):
                gate = {}

                def gate_post(b, t0, n, done):
                    s, key = tmp("a", n)
                    a = act([done, rfree[key]], lambda e: e.activation(s, PS[:, b, 0:n], ACT.Silu))
                    gate[t0] = (s, key, a)
                    return [a]

                def up_post(b, t0, n, done, k=k):
                    s, key, a = gate[t0]
                    t, key2 = tmp("b", n)
                    d = dve([done, a, rfree[key2]], lambda e: e.tensor_tensor(t, s, PS[:, b, 0:n], ALU.mult))
                    rfree[key] = [d]
                    got = split(hid(0, k, t0, n), hid(1, k, t0, n), t, d, over)
                    rfree[key2] = got
                    ready[(k, t0)] = got
                    return [d]

                hw = lambda kk, t0: h_ready[kk] if isinstance(h_ready, list) else h_ready[(kk, t0)]
                column_groups(gu[c0 + k], (SLOT,), DC, segs, hacts, hw, gate_post)
                if between:
                    between()
                last_h = column_groups(gu[FC + c0 + k], (SLOT,), DC, segs, hacts, hw, up_post)
                if between:
                    between()
            for j in range(DC):
                last = column_groups(dn[j][:, c0 * P:(c0 + size) * P], (size * P,), size, segs, hid,
                                     lambda kk, t0: ready[(kk, t0)],
                                     lambda b, t0, n, done, j=j: down_post(pi, j, b, t0, n, done))
                if between:
                    between()
            over = [last]
            c0 += size
        state["h_over"] = [last_h]
        state["hid_over"] = over

    state = {"h_over": [], "hid_over": []}

    def first_ffn(pre, post, gu, dn, x_ready, between=None):
        F = lambda j: M[:, j * 512:(j + 1) * 512]
        h_ready = rms_to_h(pre, x_ready, state["h_over"])
        f_ready = [None] * DC

        def down_post(pi, j, b, t0, n, done):
            if pi == 0:
                f_ready[j] = act([done, state.get("misc_over")], lambda e: e.copy(F(j), PS[:, b, 0:n]))
            else:
                f_ready[j] = dve([done, f_ready[j]], lambda e: e.tensor_tensor(F(j), F(j), PS[:, b, 0:n], ALU.add))
            return [f_ready[j]]

        ffn(gu, dn, PARTS1, SEG1, h_ready, down_post, between)
        return add_normed(post, F, f_ready, x_ready, 0.5)

    def add_normed(post, F, f_ready, x_ready, scale):
        b = bank()
        s = mean_square([F(j) for j in range(DC)], f_ready, L, one1024, b)
        r = rstd(b, L, 0, s, RMS_EPS, rs_readers[0])
        if scale != 1.0:
            r = dve([r], lambda e: e.tensor_scalar(rs_view(L), rs_view(L), scale, None, ALU.mult))
        out = []
        for j in range(DC):
            d = dve([f_ready[j], r], lambda e, j=j: e.scalar_tensor_tensor(
                out=F(j), in0=F(j), scalar=par(post, j), in1=rs_view(L), op0=ALU.mult, op1=ALU.mult))
            rs_readers[0] = [d]
            eng = dve
            x = eng([d, x_ready[j]], lambda e, j=j: e.tensor_tensor(xs(j), xs(j), F(j), ALU.add))
            out.append(x)
        state["misc_over"] = out
        return out

    q.stage("start")
    par_ready = load([], PAR[:, :], dram["params"], sems["par"])
    con_ready = load([], CON[:, :], dram["consts"], sems["par"])
    par_ready = con_ready
    x_ready = [load([], xs(c), dram["x"][c], sems["x"][c]) for c in range(DC)]
    cnd_all = H[:, 0:6144].rearrange("p (k t) -> p k t", t=768)[:, :, 512:640]
    z = TMP[:, 1024:1152]
    d0 = dve([], lambda e: e.memset(z, 0.0))
    d1 = None
    for k in range(8):
        d1 = dve([d0], lambda e, k=k: e.tensor_copy(cnd_all[:, k, :], z))
    sc = TMP[:, 1152:1168]
    a0 = act([par_ready], lambda e: e.activation(sc, PAR[:, POFF["cond"]:POFF["cond"] + 16], ACT.Silu))
    sc2 = sc.rearrange("p (k w) -> p k w", w=2)
    a1 = act([a0, d1], lambda e: e.copy(cnd_all[:, :, 0:2], sc2))
    d2 = dve([a1], lambda e: e.tensor_tensor(cnd_all[:, :, 2:4], sc2, cnd_all[:, :, 0:2], ALU.subtract))
    cond_ready = [d2, con_ready]
    rfree[("b", 0)] = [d2, d1]
    q.wait("pe", con_ready)
    q.wait("dve", par_ready)
    q.wait("act", par_ready)

    def modulate(layer, g, segs, c, x_tok, over):
        out = {}
        for t0, n in segs:
            who = 0 if t0 == 0 else 1
            t, key = tmp("b", n)
            d = dve([x_tok, mod_ready[layer], rfree[key]], lambda e, t=t, t0=t0, n=n, who=who: e.tensor_scalar(
                t, xs(c, t0, n), mod(layer, who, g + 1, c), mod(layer, who, g, c), ALU.mult, ALU.add))
            got = split(hs(0, c, t0, n), hs(1, c, t0, n), t, d, over)
            rfree[key] = got
            out[(c, t0)] = got
        return out

    def layer_norm(layer, which, segs, x_ready, final=None, permute=False):
        out = {}
        for t0, n in segs:
            b = bank()
            last = None
            for c in range(DC):
                last = pe([x_ready[(c, t0)], *(free[b] if c == 0 else [])], lambda e, c=c, t0=t0, n=n, b=b: e.matmul(
                    PS[:, b, 0:n], one1024, xs(c, t0, n), start=c == 0, stop=c == DC - 1), c == DC - 1)
            mid = []
            for c in range(DC):
                mid.append(dve([last, x_ready[(c, t0)]], lambda e, c=c, t0=t0, n=n, b=b: e.tensor_tensor(
                    xs(c, t0, n), xs(c, t0, n), PS[:, b, 0:n], ALU.subtract)))
            free[b] = [mid[-1]]
            b2 = bank()
            s = mean_square([xs(c, t0, n) for c in range(DC)], mid, n, one1024, b2)
            r = rstd(b2, n, t0, s, LN_EPS, rs_readers[t0])
            for c in range(DC):
                o = POFF["ln_g"] + (layer * 2 + which) * 8 + c
                o2 = POFF["ln_b"] + (layer * 2 + which) * 8 + c
                t, key = tmp("b", n)
                d = dve([mid[c], r, rfree[key]], lambda e, c=c, t0=t0, n=n, t=t, o=o: e.scalar_tensor_tensor(
                    out=t, in0=xs(c, t0, n), scalar=PAR[:, o:o + 1], in1=rs_view(n, t0), op0=ALU.mult, op1=ALU.mult))
                rs_readers[t0] = [d]
                dst = xs(c, t0, n)
                src = t
                if permute and t0 == 0:
                    dst = dst.rearrange("p (c r) -> p r c", r=8)
                    src = t.rearrange("p (r c) -> p r c", c=64)
                a = act([d], lambda e, dst=dst, src=src, o2=o2: e.activation(
                    dst, src, ACT.Identity, bias=PAR[:, o2:o2 + 1]))
                rfree[key] = [a]
                out[(c, t0)] = a
                if final:
                    final(c, t0, n, a)
        return out

    def scale_alpha(x_tok, readers):
        out = {}
        for (c, t0), tok in x_tok.items():
            n = 512 if t0 == 0 else 256
            out[(c, t0)] = pool([tok, readers[(c, t0)]], lambda e, c=c, t0=t0, n=n: e.tensor_scalar(
                xs(c, t0, n), xs(c, t0, n), ALPHA, None, ALU.mult))
        return out

    def gated_add(layer, g, x_tok):
        def post(pi, j, b, t0, n, done):
            who = 0 if t0 == 0 else 1
            x_tok[(j, t0)] = dve([done, x_tok[(j, t0)]], lambda e: e.scalar_tensor_tensor(
                out=xs(j, t0, n), in0=PS[:, b, 0:n], scalar=mod(layer, who, g, j), in1=xs(j, t0, n),
                op0=ALU.mult, op1=ALU.add))
            return [x_tok[(j, t0)]]
        return post

    def begin_sublayer(layer, g, segs, x_tok):
        h_ready = {}
        for c in range(DC):
            h_ready |= modulate(layer, g, segs, c, [x_tok[(c, t0)] for t0, _ in segs], state["h_over"])
        return h_ready, scale_alpha(x_tok, h_ready)


    def first_mixer(x_ready):
        QA, KA, VA, SA, PT, OA, XL = 0, 2048, 2560, 3072, 5120, 7168, 9216
        BD, MASK, GA, SM = 11280, 12304, 12560, 14608
        XC, AA, UA = 0, 3072, 5120
        pro = state["misc_over"]
        bd_ready = load([pro], M[:, BD:BD + 1024], dram["gates"], sems["misc"])
        mask_ready = load([pro], M[:, MASK:MASK + 256], dram["mask1"], sems["misc"])
        bd_ready = mask_ready
        h_ready = rms_to_h("mix_pre_g", x_ready, state["h_over"])
        hw = lambda k, t0: h_ready[k]
        hacts = lambda half, k, t0, n: hs(half, k, t0, n)
        win = dram["w_in"]

        sm = lambda o, n: M[:, SM + o:SM + o + n]
        nsink = sm(0, 8)
        t = dve([pro, par_ready], lambda e: e.tensor_scalar(nsink, PAR[:, POFF["sinks"]:POFF["sinks"] + 8], -1.0, None, ALU.mult))
        nsink_ready = t
        lam = PAR[:, POFF["lam"]:POFF["lam"] + 4]
        en, den, ratio, z, pl, mn, cls, sp_ = (sm(8 + 4 * i, 4) for i in range(8))
        t = dve([pro], lambda e: e.tensor_scalar(mn, lam, -1.0, None, ALU.mult))
        t = dve([t], lambda e: e.tensor_tensor(en, mn, lam, ALU.min))
        t = act([t], lambda e: e.activation(en, en, ACT.Exp))
        t = dve([t], lambda e: e.tensor_scalar(den, en, 2.0, None, ALU.add))
        t = dve([t], lambda e: e.reciprocal(sp_, den))
        t = dve([t], lambda e: e.tensor_tensor(ratio, en, sp_, ALU.mult))
        t = dve([t], lambda e: e.tensor_tensor(z, ratio, ratio, ALU.mult))
        t = dve([t], lambda e: e.tensor_scalar(pl, z, 1.0 / 15, 1.0 / 13, ALU.mult, ALU.add))
        for k in (11, 9, 7, 5, 3, 1):
            t = dve([t], lambda e: e.tensor_tensor(pl, pl, z, ALU.mult))
            t = dve([t], lambda e, k=k: e.tensor_scalar(pl, pl, 1.0 / k, None, ALU.add))
        t = dve([t], lambda e: e.tensor_tensor(pl, pl, ratio, ALU.mult))
        t = dve([t], lambda e: e.tensor_scalar(mn, lam, 0.0, None, ALU.min))
        t = dve([t], lambda e: e.scalar_tensor_tensor(out=cls, in0=pl, scalar=-2.0, in1=mn, op0=ALU.mult, op1=ALU.add))
        cls_ready = dve([t], lambda e: e.tensor_scalar(cls, cls, 8.0, None, ALU.mult))

        q_ready = {}

        def q_post(b, t0, n, done, c):
            q_ready[c] = act([done, pro], lambda e: e.copy(M[:, QA + c * 512:QA + (c + 1) * 512], PS[:, b, :]))
            return [q_ready[c]]

        for c in range(4):
            column_groups(win[8 + c], (SLOT,), DC, SEG1, hacts, hw, lambda b, t0, n, d, c=c: q_post(b, t0, n, d, c))
        column_groups(win[12], (SLOT,), DC, SEG1, hacts, hw,
                      lambda b, t0, n, d: q_post(b, t0, n, d, 4))
        slot, ready = next_block(win[13], (SLOT,))
        b = bank()
        done = None
        for tt in range(4):
            out = PS[:, b, tt * P:(tt + 1) * P]
            for k in range(DC):
                w = slice(k * P, (k + 1) * P)
                hi, lo = hs(0, k, tt * P, P), hs(1, k, tt * P, P)
                done = products(out, hi, lo, WHI[:, slot, w], WLO[:, slot, w],
                                [*ready, h_ready[k], *(free[b] if tt == 0 and k == 0 else [])], k == 0, k == DC - 1,
                                k == DC - 1)
        block_over(done)
        v_ready = dve([done, pro], lambda e, b=b: e.tensor_copy(M[:, VA:VA + 512], PS[:, b, :]))
        free[b] = [v_ready]
        for bb in range(8):
            q.wait("pe", free[bb])

        XLc = lambda c, o, n: M[:, XL + c * 515 + o:XL + c * 515 + o + n]
        Gc = lambda c: M[:, GA + c * 512:GA + (c + 1) * 512]
        pad = [dve([pro], lambda e, c=c: e.memset(XLc(c, 0, 3), 0.0)) for c in range(4)]
        xl_ready, g_ready = {}, {}

        def lru_projection(i):
            def post(b, t0, n, done):
                if i < 4:
                    xl_ready[i] = act([done, pro], lambda e: e.copy(XLc(i, 3, 512), PS[:, b, :]))
                    return [xl_ready[i]]
                g_ready[i - 4] = act([done, pro], lambda e: e.activation(Gc(i - 4), PS[:, b, :], ACT.Gelu_apprx_tanh))
                return [g_ready[i - 4]]

            last = column_groups(win[i], (SLOT,), DC, SEG1, hacts, hw, post, banks=(7,))
            state["h_over"] = [last]

        units = [(n, kv) for n in range(4) for kv in range(2)]
        st = {}
        att_free = {("s", 0): [], ("s", 1): [], ("p", 0): [], ("p", 1): []}

        def scores(i):
            n, kv = units[i]
            NK = P if n == 0 else 2 * P
            k0 = n * P - (NK - P)
            b0 = (0, 2)[i % 2]
            pp = slice(kv * 64, kv * 64 + 64)
            for g in range(4):
                bb = b0 + g // 2
                done = pe([q_ready[g], q_ready[4], free[bb] if g % 2 == 0 else []], lambda e, g=g, bb=bb: e.matmul(
                    PS[:, bb, (g % 2) * 256:(g % 2) * 256 + NK], M[pp, QA + g * 512 + n * P:QA + g * 512 + (n + 1) * P],
                    M[pp, KA + k0:KA + k0 + NK], start=True, stop=True, skip_group_check=True), g == 3)
            ps = PS[:, b0:b0 + 2, :].rearrange("p b (g k) -> p (b g) k", k=256)[:, :, 0:NK]
            s = M[:, SA + (i % 2) * 1024:SA + (i % 2) * 1024 + 4 * NK].rearrange("p (g k) -> p g k", g=4)
            mk = M[:, MASK + 256 - NK:MASK + 256].unsqueeze(1).to_broadcast([P, 4, NK])
            d = dve([done, mask_ready, att_free[("s", i % 2)]], lambda e: e.scalar_tensor_tensor(
                out=s, in0=ps, scalar=0.125, in1=mk, op0=ALU.mult, op1=ALU.add))
            free[b0] = free[b0 + 1] = [d]
            o = 48 + (i % 2) * 24
            nm, es, sums, rec = sm(o, 4), sm(o + 4, 4), sm(o + 8, 4), sm(o + 12, 4)
            m1 = dve([d], lambda e: e.tensor_reduce(nm, s, AX_X, ALU.max, negate=True))
            m2 = dve([m1, nsink_ready], lambda e: e.tensor_tensor(nm, nm, sm(kv * 4, 4), ALU.min))
            m3 = dve([m2], lambda e: e.tensor_tensor(es, nm, sm(kv * 4, 4), ALU.subtract))
            x = [act([m2], lambda e, g=g: e.activation(s[:, g, :], s[:, g, :], ACT.Exp, bias=nm[:, g:g + 1],
                                                       accum_out=sums[:, g:g + 1])) for g in range(4)]
            x.append(act([m3], lambda e: e.activation(es, es, ACT.Exp)))
            r1 = dve(x, lambda e: e.tensor_tensor(es, es, sums, ALU.add))
            r2 = dve([r1], lambda e: e.reciprocal(rec, es))
            p = [dve([r2], lambda e, g=g: e.tensor_scalar(s[:, g, :], s[:, g, :], rec[:, g:g + 1], None, ALU.mult))
                 for g in range(4)]
            st[i] = (s, NK, p)

        def turn_weights(i):
            s, NK, p = st[i]
            n, kv = units[i]
            KT = NK // P
            ev = []
            for kt in range(KT):
                bb = 4 + kt
                for g in range(4):
                    done = pe([p[g], free[bb] if g == 0 else []], lambda e, g=g, bb=bb, kt=kt: e.transpose(
                        PS[:, bb, g * P:(g + 1) * P], s[:, g, kt * P:(kt + 1) * P], ident), g == 3)
                dst = M[:, PT + (i % 2) * 1024 + kt * 512:PT + (i % 2) * 1024 + (kt + 1) * 512]
                over = att_free[("p", i % 2)]
                fn = lambda e, dst=dst, bb=bb: e.tensor_copy(dst, PS[:, bb, :])
                fa = lambda e, dst=dst, bb=bb: e.copy(dst, PS[:, bb, :])
                ev.append(act([done, over], fa) if kt == 0 else dve([done, over], fn))
                free[bb] = [ev[-1]]
            att_free[("s", i % 2)] = [done]
            st[i] = (KT, ev)

        o_ready = {}

        def attend(i):
            n, kv = units[i]
            KT, ev = st[i]
            pp = slice(kv * 64, kv * 64 + 64)
            for kt in range(KT):
                tt = n - (KT - 1) + kt
                done = pe([ev[kt], v_ready, free[6] if kt == 0 else []], lambda e, kt=kt, tt=tt: e.matmul(
                    PS[pp, 6, :], M[:, VA + tt * P + kv * 64:VA + tt * P + kv * 64 + 64],
                    M[:, PT + (i % 2) * 1024 + kt * 512:PT + (i % 2) * 1024 + (kt + 1) * 512],
                    start=kt == 0, stop=kt == KT - 1), kt == KT - 1)
            att_free[("p", i % 2)] = [done]
            src = PS[pp, 6, :].rearrange("p (g t) -> p g t", g=4)
            dst = M[pp, OA:OA + 2048].rearrange("p (g t) -> p g t", g=4)[:, :, n * P:(n + 1) * P]
            d = dve([done, pro], lambda e: e.tensor_copy(dst, src))
            free[6] = [d]
            o_ready[(n, kv)] = d

        for i in range(10):
            if i < 8:
                scores(i)
                lru_projection(i)
            if 0 <= i - 1 < 8:
                turn_weights(i - 1)
            if 0 <= i - 2 < 8:
                attend(i - 2)
        all_o = list(o_ready.values())

        def y_part(src, waits, c0, b):
            s = mean_square(src, waits, L, one512, b)
            r = rstd(b, L, 0, s, RMS_EPS, rs_readers[0])
            out = []
            for c in range(4):
                d = dve([r, waits[c]], lambda e, c=c: e.scalar_tensor_tensor(
                    out=src[c], in0=src[c], scalar=par("g_mix", c0 + c), in1=rs_view(L), op0=ALU.mult, op1=ALU.mult))
                rs_readers[0] = [d]
                k = c0 + c
                out.append(split(HID[:, k * 512:(k + 1) * 512], HID[:, 4096 + k * 512:4096 + (k + 1) * 512],
                                 src[c], d, state["hid_over"]))
            return out

        y_att = y_part([M[:, OA + c * 512:OA + (c + 1) * 512] for c in range(4)], [all_o] * 4, 4, 6)

        att_done = [all_o, q_ready[4]]
        XCc = lambda c: M[:, XC + c * 512:XC + (c + 1) * 512]
        Ac = lambda c: M[:, AA + c * 512:AA + (c + 1) * 512]
        Uc = lambda c: M[:, UA + c * 512:UA + (c + 1) * 512]
        cw = lambda j, c: par("conv_w", j * 4 + c)
        xc_ready, h_done = {}, {}
        for c in range(4):
            t = dve([xl_ready[c], pad[c], att_done], lambda e, c=c: e.tensor_scalar(
                XCc(c), XLc(c, 0, 512), cw(0, c), par("conv_b", c), ALU.mult, ALU.add))
            for j in range(1, 4):
                t = dve([t], lambda e, c=c, j=j: e.scalar_tensor_tensor(
                    out=XCc(c), in0=XLc(c, j, 512), scalar=cw(j, c), in1=XCc(c), op0=ALU.mult, op1=ALU.add))
            xc_ready[c] = t
        r_ready, i_ready = {}, {}
        for c in range(4):
            for gi, (dst, bias, reg) in enumerate(((Ac, "b_rg", r_ready), (Uc, "b_ig", i_ready))):
                b = bank()
                mm = pe([xc_ready[c], bd_ready, free[b]], lambda e, c=c, gi=gi, b=b: e.matmul(
                    PS[:, b, :], M[:, BD + gi * 512 + c * P:BD + gi * 512 + (c + 1) * P], XCc(c), start=True, stop=True))
                reg[c] = act([mm, att_done], lambda e, c=c, b=b, dst=dst, bias=bias: e.activation(
                    dst(c), PS[:, b, :], ACT.Sigmoid, bias=par(bias, c)))
                free[b] = [reg[c]]
        for c in range(4):
            la = dve([r_ready[c], cls_ready], lambda e, c=c: e.tensor_scalar(Ac(c), Ac(c), cls[:, c:c + 1], None, ALU.mult))
            th, key = tmp("a", L)
            a1 = act([la, rfree[key]], lambda e, c=c, th=th: e.activation(th, Ac(c), ACT.Tanh))
            a2 = act([la, a1], lambda e, c=c: e.activation(Ac(c), Ac(c), ACT.Exp))
            sq, key2 = tmp("b", L)
            t = dve([a2, rfree[key2]], lambda e, c=c, sq=sq: e.tensor_tensor(sq, Ac(c), Ac(c), ALU.mult))
            t = dve([t, a1], lambda e, c=c, sq=sq, th=th: e.scalar_tensor_tensor(
                out=sq, in0=sq, scalar=1.0, in1=th, op0=ALU.add, op1=ALU.mult))
            rfree[key] = [t]
            t = dve([t], lambda e, sq=sq: e.tensor_scalar(sq, sq, -1.0, 0.0, ALU.mult, ALU.max))
            t = act([t], lambda e, sq=sq: e.activation(sq, sq, ACT.Sqrt))
            t2 = dve([i_ready[c]], lambda e, c=c: e.tensor_tensor(Uc(c), Uc(c), XCc(c), ALU.mult))
            t = dve([t, t2], lambda e, c=c, sq=sq: e.tensor_tensor(Uc(c), Uc(c), sq, ALU.mult))
            rfree[key2] = [t]
            t = dve([t, a2], lambda e, c=c: e.tensor_tensor_scan(XLc(c, 0, 512), Ac(c), Uc(c), 0.0, ALU.mult, ALU.add))
            h_done[c] = dve([t, g_ready[c]], lambda e, c=c: e.tensor_tensor(Gc(c), XLc(c, 0, 512), Gc(c), ALU.mult))
        y_lru = y_part([Gc(c) for c in range(4)], [h_done[c] for c in range(4)], 0, bank())

        y_ready = y_lru + y_att
        F = lambda j: M[:, j * 512:(j + 1) * 512]
        f_ready = [None] * DC

        def o_post(b, t0, n, done, j):
            f_ready[j] = act([done, *h_done.values()], lambda e: e.copy(F(j), PS[:, b, :]))
            return [f_ready[j]]

        yacts = lambda half, k, t0, n: HID[:, half * 4096 + k * 512:half * 4096 + (k + 1) * 512]
        for j in range(DC):
            last = column_groups(dram["w_o"][j], (SLOT,), DC, SEG1, yacts, lambda k, t0: y_ready[k],
                                 lambda b, t0, n, d, j=j: o_post(b, t0, n, d, j))
        state["hid_over"] = [last]
        return add_normed("mix_post_g", F, f_ready, x_ready, 1.0)

    def retention(h_ready, xt):
        QK, VV, OC, PA, ST, DI, CS, GG = 0, 3072, 6144, 7168, 8192, 9728, 10880, 11904
        pro = [state["misc_over"]]
        dist_ready = load(pro, M[:, DI:DI + 1152], dram["dist"], sems["misc"])
        cs_ready = load(pro, M[:, CS:CS + 1024], dram["rope"], sems["misc"])
        dist_ready = cs_ready
        hw = lambda k, t0: h_ready[(k, t0)]
        hacts = lambda half, k, t0, n: hs(half, k, t0, n)
        sm = lambda o, n: TMP[:, 2816 + o:2816 + o + n]
        dec = PAR[:, POFF["decay"]:POFF["decay"] + 8]
        eg, lg, nlb = sm(0, 8), sm(8, 8), sm(16, 8)
        t = act([pro, par_ready], lambda e: e.activation(eg, dec, ACT.Exp))
        t = dve([t], lambda e: e.tensor_scalar(lg, eg, -1.0, None, ALU.mult))
        lg_ready = dve([t], lambda e: e.tensor_scalar(nlb, eg, 768.0, -1.0, ALU.mult, ALU.mult))
        cos, sin = M[:, CS:CS + 512], M[:, CS + 512:CS + 1024]
        qk = lambda w, k, t0, n: M[:, QK + (w * 2 + k) * 768 + t0:QK + (w * 2 + k) * 768 + t0 + n]
        ov = {"qk": pro, "v": pro, "oc": pro, "p": [[], []], "st": pro, "g": pro, "ol": pro}
        first_y = True

        for h in range(4):
            d_ = M[:, DI:DI + 1152]
            LL, GS = M[:, ST:ST + 896], M[:, ST + 896:ST + 1536]
            tA, tB = M[:, PA:PA + 896], TMP[:, 1024:1920]
            t1 = dve([dist_ready, lg_ready, ov["st"], *ov["p"][0], *ov["p"][1]], lambda e, h=h: e.tensor_scalar(
                tA, d_[:, 0:896], 0.0, lg[:, h:h + 1], ALU.max, ALU.mult))
            t2 = dve([ov["st"], rfree[("b", 0)], rfree[("b", 1)]], lambda e, h=h: e.tensor_scalar(
                tB, d_[:, 0:896], 0.0, eg[:, 4 + h:5 + h], ALU.min, ALU.mult))
            t3 = dve([t1, t2], lambda e: e.tensor_tensor(tA, tA, tB, ALU.add))
            t4 = act([t3, ov["st"]], lambda e: e.activation(LL, tA, ACT.Exp))
            ll_ready = dve([t4], lambda e: e.tensor_tensor(LL[:, 384:512], LL[:, 384:512], ident, ALU.add))
            t5 = act([lg_ready, ov["st"]], lambda e, h=h: e.activation(GS, d_[:, 512:1152], ACT.Exp, scale=lg[:, h:h + 1]))
            t6 = act([t3, lg_ready], lambda e, h=h: e.activation(tB[:, 0:640], d_[:, 512:1152], ACT.Exp,
                                                             scale=eg[:, 4 + h:5 + h], bias=nlb[:, 4 + h:5 + h]))
            gs_ready = dve([t5, t6], lambda e: e.tensor_tensor(GS, GS, tB[:, 0:640], ALU.add))
            rfree[("b", 0)] = rfree[("b", 1)] = [gs_ready]
            ov["p"] = [[t4], [t4]]

            dones = {}
            for blk in range(4):
                slot, ready = next_block(dram["ret_v"][h, blk], (SLOT,))
                for tt in range(6):
                    b = tt
                    for kk in range(2):
                        k = blk * 2 + kk
                        w = slice(kk * 512, (kk + 1) * 512)
                        t0 = 0 if tt < 4 else 512
                        dones[tt] = products(PS[:, b, :], hs(0, k, tt * P, P), hs(1, k, tt * P, P),
                                             WHI[:, slot, w], WLO[:, slot, w],
                                             [*ready, h_ready[(k, t0)], *(free[b] if k == 0 else [])],
                                             k == 0, k == 7, (k == 7) or (kk == 1 and tt == 5))
                block_over(dones[5])
            v_ready = {}
            for tt in range(6):
                dst = M[:, VV + tt * 512:VV + (tt + 1) * 512]
                v_ready[tt] = act([dones[tt], ov["v"]], lambda e, tt=tt, dst=dst: e.copy(dst, PS[:, tt, :]))
                free[tt] = [v_ready[tt]]

            qk_ready = {}
            for w in range(2):
                halves = {}

                def qk_post(b, t0, n, done, w=w, halves=halves):
                    k = halves["k"]
                    if t0 == 512:
                        a = act([done, ov["qk"]], lambda e, k=k: e.copy(qk(w, k, 512, 256), PS[:, b, 0:256]))
                        qk_ready[(w, k, 512)] = a
                        return [a]
                    if k == 0:
                        halves["b"], halves["done"] = b, done
                        return []
                    b0, d0_ = halves["b"], halves["done"]
                    for half in range(2):
                        (u, ku), (v, kv_) = tmp("b", 512), tmp("b", 512)
                        s1, s2 = (cos, sin) if half == 0 else (sin, cos)
                        x1 = dve([d0_, rfree[ku], cs_ready], lambda e, u=u, s1=s1: e.tensor_tensor(u, PS[:, b0, :], s1, ALU.mult))
                        x2 = dve([done, rfree[kv_]], lambda e, v=v, s2=s2: e.tensor_tensor(v, PS[:, b, :], s2, ALU.mult))
                        op = ALU.subtract if half == 0 else ALU.add
                        x3 = dve([x1, x2, ov["qk"]], lambda e, u=u, v=v, op=op, half=half: e.tensor_tensor(
                            qk(w, half, 0, 512), u, v, op))
                        rfree[ku] = rfree[kv_] = [x3]
                        qk_ready[(w, half, 0)] = x3
                    free[b0] = [x2]
                    return [x2]

                for k in range(2):
                    halves["k"] = k
                    column_groups(dram["ret_qk"][w * 8 + h * 2 + k], (SLOT,), DC, SEG2, hacts, hw, qk_post)
                    if k == 0:
                        free[halves["b"]] = [halves["done"]]
                        held = halves["b"]

            g_ready = {}

            def g_post(b, t0, n, done, c):
                dst = M[:, GG + c * 768 + t0:GG + c * 768 + t0 + n]
                g_ready[(c, t0)] = act([done, ov["g"]], lambda e: e.activation(dst, PS[:, b, 0:n], ACT.Silu))
                return [g_ready[(c, t0)]]

            for c in range(4):
                last_h = column_groups(dram["ret_g"][h * 4 + c], (SLOT,), DC, SEG2, hacts, hw,
                                       lambda b, t0, n, d, c=c: g_post(b, t0, n, d, c))
            state["h_over"] = [last_h]

            y_ready = {}
            o_tok = {}
            for t0, n, tiles in ((512, 256, (4, 5)), (0, 512, (0, 1, 2, 3, 4, 5))):
                weights = {}

                def score(i, t0=t0, n=n, tiles=tiles, weights=weights):
                    kt = tiles[i]
                    b = (4, 5)[i % 2]
                    kseg = 0 if kt < 4 else 512
                    for k in range(2):
                        done = pe([qk_ready[(0, k, t0)], qk_ready[(1, k, kseg)], free[b] if k == 0 else []],
                                  lambda e, k=k, b=b, kt=kt: e.matmul(PS[:, b, 0:n], qk(1, k, kt * P, P), qk(0, k, t0, n),
                                                                      start=k == 0, stop=k == 1), k == 1)
                    if t0 == 0 and kt < 4:
                        dd, dr = LL[:, 384 - 128 * kt:384 - 128 * kt + 512], ll_ready
                    elif t0 == 0:
                        dd, dr = GS[:, 128 - 128 * (kt - 4):128 - 128 * (kt - 4) + 512], gs_ready
                    else:
                        dd, dr = LL[:, 384 - 128 * (kt - 4):384 - 128 * (kt - 4) + 256], ll_ready
                    pw = M[:, PA + (i % 2) * 512:PA + (i % 2) * 512 + n]
                    d = dve([done, dr, ov["p"][i % 2]], lambda e, b=b: e.scalar_tensor_tensor(
                        out=pw, in0=PS[:, b, 0:n], scalar=0.0625, in1=dd, op0=ALU.mult, op1=ALU.mult))
                    free[b] = [d]
                    weights[i] = (pw, d)
                    ov["last_score"] = done

                def value(i, t0=t0, n=n, tiles=tiles, weights=weights):
                    pw, d = weights[i]
                    kt = tiles[i]
                    for c in range(4):
                        done = pe([d, v_ready[kt], free[c] if i == 0 else []], lambda e, c=c, kt=kt: e.matmul(
                            PS[:, c, 0:n], M[:, VV + kt * 512 + c * P:VV + kt * 512 + (c + 1) * P], pw,
                            start=i == 0, stop=i == len(tiles) - 1), c == 3 or i == len(tiles) - 1)
                        o_tok[(c, t0)] = done
                    ov["p"][i % 2] = [done]

                for i in range(len(tiles) + 1):
                    if i < len(tiles):
                        score(i)
                    if i >= 1:
                        value(i - 1)
                if t0 == 512:
                    ov["st_last"] = ov["p"]
                src = []
                wt = []
                for c in range(4):
                    if t0 == 512:
                        dst = M[:, OC + c * 256:OC + (c + 1) * 256]
                        over = ov["oc"]
                    else:
                        dst = M[:, QK + c * 512:QK + (c + 1) * 512]
                        over = [ov["last_score"]]
                    a = act([o_tok[(c, t0)], over], lambda e, dst=dst, c=c, n=n: e.copy(dst, PS[:, c, 0:n]))
                    free[c] = [a]
                    src.append(dst)
                    wt.append(a)
                bb = 6 if t0 == 0 else 7
                s = mean_square(src, wt, n, one512, bb)
                r = rstd(bb, n, t0, s, RMS_EPS, rs_readers[t0])
                for c in range(4):
                    gv = M[:, GG + c * 768 + t0:GG + c * 768 + t0 + n]
                    o, rs = src[c], rs_view(n, t0)
                    x1 = dve([r, wt[c]], lambda e, o=o, rs=rs: e.tensor_tensor(o, o, rs, ALU.mult))
                    rs_readers[t0] = [x1]
                    x2 = dve([x1, g_ready[(c, t0)]], lambda e, o=o, gv=gv: e.tensor_tensor(gv, o, gv, ALU.mult))
                    hi = HID[:, c * 768 + t0:c * 768 + t0 + n]
                    lo = HID[:, 4096 + c * 768 + t0:4096 + c * 768 + t0 + n]
                    y_ready[(c, t0)] = split(hi, lo, gv, x2, state["hid_over"])
                    if t0 == 0:
                        ov["qk"] = [x2]
                    else:
                        ov["oc"] = [x2]
            ov["v"] = [o_tok[(3, 0)]]
            ov["st"] = [ov["last_score"], free[5], free[4]]
            ov["g"] = [y_ready[k] for k in y_ready]

            yacts = lambda half, k, t0, n: HID[:, half * 4096 + k * 768 + t0:half * 4096 + k * 768 + t0 + n]
            post = gated_add(0, 2, xt)
            for j2 in range(4):
                slot, ready = next_block(dram["ret_o"][j2 * 2:j2 * 2 + 2, :, h * 512:(h + 1) * 512].rearrange("a p n -> p a n"),
                                         (2, 512))
                for jj in range(2):
                    j = j2 * 2 + jj
                    for t0, n in SEG2:
                        b = bank()
                        for k in range(4):
                            o = jj * 512 + k * P
                            done = products(PS[:, b, 0:n], WHI[:, slot, o:o + P], WLO[:, slot, o:o + P],
                                            yacts(0, k, t0, n), yacts(1, k, t0, n),
                                            [*ready, y_ready[(k, t0)], *(free[b] if k == 0 else [])], k == 0, k == 3, k == 3)
                        free[b] = post(0, j, b, t0, n, done)
                block_over(done)
            state["hid_over"] = [done]
        state["misc_over"] = [ov["g"], ov["v"], ov["qk"], ov["st"], ov["oc"]]
        return xt

    def neighbourhood(h_ready, xt):
        QA, KA, VV, SA, PT, BM, SM = 0, 2048, 5120, 9728, 10752, 11776, 14900
        pro = [state["misc_over"]]
        xtail = X[:, :].rearrange("p (c t) -> p c t", t=768)
        tail_over = [h_ready[(c, 512)] for c in range(DC)]
        STRIP, MSK = BM + 1536, BM + 1536 + 384
        msk_ready = load(pro, M[:, MSK:MSK + 768], dram["mask2"], sems["misc"])
        hw = lambda k, t0: h_ready[(k, t0)]
        hacts = lambda half, k, t0, n: hs(half, k, t0, n)
        sm = lambda o, n: M[:, SM + o:SM + o + n]
        bm3 = M[:, BM:BM + 1536].rearrange("p (y k) -> p y k", y=3)
        zero = pool(pro, lambda e: e.memset(M[:, BM:BM + 1536], 0.0))
        ov = {"q": pro, "k": pro, "v": pro, "s": [pro, pro], "p": [pro, pro], "bm": [zero], "strip": pro}
        band0 = (0, 64, 192, 256)
        kind = (0, 1, 1, 2)
        off = (16, 8, 0)
        starts = {0: 0, 128: 1, 256: 2, 384: 3, 64: 4, 192: 5, 320: 6}
        y_over = []

        for half in range(2):
            q_ready, k_ready = {}, {}

            def q_post(b, t0, n, done, c):
                q_ready[c] = act([done, ov["q"]], lambda e: e.mul(M[:, QA + c * 512:QA + (c + 1) * 512], PS[:, b, :], 0.125))
                return [q_ready[c]]

            def k_post(b, t0, n, done, c):
                dst = M[:, KA + c * 768 + t0:KA + c * 768 + t0 + n]
                k_ready[(c, t0)] = act([done, ov["k"]], lambda e: e.copy(dst, PS[:, b, 0:n]))
                return [k_ready[(c, t0)]]

            dones = {}
            for blk in range(4):
                slot, ready = next_block(dram["na_v"][half, blk], (SLOT,))
                for tt in range(6):
                    for kk in range(2):
                        k = blk * 2 + kk
                        w = slice(kk * 512, (kk + 1) * 512)
                        t0 = 0 if tt < 4 else 512
                        dones[tt] = products(PS[:, tt, :], hs(0, k, tt * P, P), hs(1, k, tt * P, P),
                                             WHI[:, slot, w], WLO[:, slot, w],
                                             [*ready, h_ready[(k, t0)], *(free[tt] if k == 0 else [])],
                                             k == 0, k == 7, (k == 7) or (kk == 1 and tt == 5))
                block_over(dones[5])
            v_ready = {}
            vslot = lambda tt: tt if tt < 4 else tt + 3
            VC = lambda s_: M[:, VV + s_ * 512:VV + (s_ + 1) * 512]
            for tt in range(6):
                v_ready[vslot(tt)] = act([dones[tt], ov["v"]], lambda e, tt=tt: e.copy(VC(vslot(tt)), PS[:, tt, :]))
                free[tt] = [v_ready[vslot(tt)]]
            for i, s_ in enumerate((4, 5, 6)):
                load([v_ready[i], v_ready[i + 1], ov["v"]], M[0:64, VV + s_ * 512:VV + (s_ + 1) * 512],
                     M[64:128, VV + i * 512:VV + (i + 1) * 512], sems["misc"])
                v_ready[s_] = load([v_ready[i + 1]], M[64:128, VV + s_ * 512:VV + (s_ + 1) * 512],
                                   M[0:64, VV + (i + 1) * 512:VV + (i + 2) * 512], sems["misc"])
            for s_ in (4, 5):
                v_ready[s_] = v_ready[6]
            for c in range(4):
                column_groups(dram["na_qk"][half * 4 + c], (SLOT,), DC, SEG1, hacts, hw,
                              lambda b, t0, n, d, c=c: q_post(b, t0, n, d, c))
            for c in range(4):
                last_h = column_groups(dram["na_qk"][8 + half * 4 + c], (SLOT,), DC, SEG2, hacts, hw,
                                       lambda b, t0, n, d, c=c: k_post(b, t0, n, d, c))
            state["h_over"] = [last_h]

            st = {}
            units = [(hh, b) for hh in range(8) for b in range(4)]

            def bias(hh):
                s = load([ov["strip"]], M[:, STRIP:STRIP + 384], dram["rpb"][half * 8 + hh], sems["strip"])
                last = None
                for y in range(3):
                    last = pool([s, msk_ready, ov["bm"]], lambda e, y=y: e.tensor_tensor(
                        bm3[:, y, 0:256], M[:, STRIP + off[y] * 8:STRIP + off[y] * 8 + 256],
                        M[:, MSK + y * 256:MSK + (y + 1) * 256], ALU.add))
                ov["strip"] = [last]
                return last

            bm_ready = {}

            def scores(i):
                hh, b = units[i]
                if b == 0:
                    bm_ready[hh] = bias(hh)
                c, pp = hh // 2, slice((hh % 2) * 64, (hh % 2) * 64 + 64)
                bb = (0, 1)[i % 2]
                pe([q_ready[c], k_ready[(c, 0)], free[bb]], lambda e: e.matmul(
                    PS[:, bb, 0:256], M[pp, QA + c * 512 + b * P:QA + c * 512 + (b + 1) * P],
                    M[pp, KA + c * 768 + band0[b]:KA + c * 768 + band0[b] + 256], start=True, stop=True,
                    skip_group_check=True), False)
                done = pe([k_ready[(c, 512)]], lambda e: e.matmul(
                    PS[:, bb, 256:512], M[pp, QA + c * 512 + b * P:QA + c * 512 + (b + 1) * P],
                    M[pp, KA + c * 768 + 512:KA + c * 768 + 768], start=True, stop=True, skip_group_check=True))
                o = (i % 2) * 8
                mx, nm, su, rc = (sm(o + j, 1) for j in range(4))
                s = M[:, SA + (i % 2) * 512:SA + (i % 2) * 512 + 512]
                d = dve([done, bm_ready[hh], ov["s"][i % 2]], lambda e: e.tensor_tensor_reduce(
                    s, PS[:, bb, :], bm3[:, kind[b], :], 1.0, -3.0e38, ALU.add, ALU.max, mx))
                free[bb] = [d]
                if b == 3:
                    ov["bm"] = [d]
                d2 = dve([d], lambda e: e.tensor_scalar(nm, mx, -1.0, None, ALU.mult))
                a = act([d2], lambda e: e.activation(s, s, ACT.Exp, bias=nm, accum_out=su))
                d3 = dve([a], lambda e: e.reciprocal(rc, su))
                d4 = dve([d3], lambda e: e.tensor_scalar(s, s, rc, None, ALU.mult))
                st[i] = (s, d4)
                ov["last_score"] = done

            def turn_weights(i):
                s, d4 = st[i]
                bb = (2, 3)[i % 2]
                for kt in range(4):
                    done = pe([d4, free[bb] if kt == 0 else []], lambda e, kt=kt: e.transpose(
                        PS[:, bb, kt * P:(kt + 1) * P], s[:, kt * P:(kt + 1) * P], ident), kt == 3)
                ov["s"][i % 2] = [done]
                dst = M[:, PT + (i % 2) * 512:PT + (i % 2) * 512 + 512]
                a = act([done, ov["p"][i % 2]], lambda e: e.copy(dst, PS[:, bb, :]))
                free[bb] = [a]
                st[i] = (dst, a)

            def attend(i):
                hh, b = units[i]
                dst, a = st[i]
                r0 = (hh % 2) * 64
                ob = (4, 5)[(hh // 2) % 2]
                tiles = [starts[band0[b]], starts[band0[b] + 128], 7, 8]
                for kt in range(4):
                    vs = M[:, VV + tiles[kt] * 512 + hh * 64:VV + tiles[kt] * 512 + hh * 64 + 64]
                    done = pe([a, v_ready[tiles[kt]], free[ob] if b == 0 and kt == 0 and hh % 2 == 0 else []],
                              lambda e, kt=kt, vs=vs: e.matmul(PS[r0:r0 + 64, ob, b * P:(b + 1) * P], vs,
                                                               dst[:, kt * P:(kt + 1) * P], start=kt == 0, stop=kt == 3,
                                                               skip_group_check=True), kt == 3)
                ov["p"][i % 2] = [done]
                if b == 3 and hh % 2 == 1:
                    k = half * 4 + hh // 2
                    hi, lo = HID[:, k * 512:(k + 1) * 512], HID[:, 4096 + k * 512:4096 + (k + 1) * 512]
                    x1 = act([done, state["hid_over"]], lambda e: e.copy(hi, PS[:, ob, :]))
                    x2 = dve([x1, done], lambda e: e.tensor_tensor(lo, PS[:, ob, :], hi, ALU.subtract))
                    free[ob] = [x2]
                    y_over.append([x1, x2])
                ov["last"] = done

            for i in range(len(units) + 2):
                if i < len(units):
                    scores(i)
                if 0 <= i - 1 < len(units):
                    turn_weights(i - 1)
                if i - 2 >= 0:
                    attend(i - 2)
            ov["q"] = ov["k"] = [ov["last_score"]]
            ov["v"] = [ov["last"]]

        yacts = lambda half, k, t0, n: HID[:, half * 4096 + k * 512:half * 4096 + (k + 1) * 512]
        post = gated_add(1, 2, xt)
        for j in range(DC):
            last = column_groups(dram["na_o"][j], (SLOT,), DC, SEG1, yacts, lambda k, t0: y_over[k],
                                 lambda b, t0, n, d, j=j: post(0, j, b, t0, n, d))
        state["hid_over"] = [last]
        return xt

    q.stage("ffn1")
    x_ready = first_ffn("ffn1_pre_g", "ffn1_post_g", dram["gu1"], dram["dn1"], x_ready, ada_step)

    q.stage("mix1")
    x_ready = first_mixer(x_ready)
    ada["limit"] = 96

    q.stage("ffn2")
    x_ready = first_ffn("ffn2_pre_g", "ffn2_post_g", dram["gu2"], dram["dn2"], x_ready, ada_step)
    while ada["n"] < 96:
        ada_step()

    q.stage("ret")
    xt = {(c, 0): x_ready[c] for c in range(DC)}
    for c in range(DC):
        xt[(c, 512)] = load([ada["row_read"]], xs(c, 512, 256), dram["ctx"][c], sems["x"][c])
    h_ready, xt = begin_sublayer(0, 0, SEG2, xt)
    xt = retention(h_ready, xt)
    xt = layer_norm(0, 0, SEG2, xt)
    q.stage("ffn3")
    h_ready, xt = begin_sublayer(0, 3, SEG2, xt)
    ffn(dram["gu3"], dram["dn3"], PARTS2, SEG2, h_ready, gated_add(0, 5, xt))
    q.stage("ln3")
    xt = layer_norm(0, 1, SEG2, xt, permute=True)

    q.stage("na")
    h_ready, xt = begin_sublayer(1, 0, SEG2, xt)
    xt = {k: v for k, v in xt.items() if k[1] == 0}
    xt = neighbourhood(h_ready, xt)
    xt = layer_norm(1, 0, SEG1, xt)
    q.stage("ffn4")
    h_ready, xt = begin_sublayer(1, 3, SEG1, xt)
    ffn(dram["gu4"], dram["dn4"], PARTS1, SEG1, h_ready, gated_add(1, 5, xt))
    q.stage("end")
    stores = []

    def store(c, t0, n, token):
        stores.append(load([token], dram["out"][c], xs(c), sems["out"]))

    layer_norm(1, 1, SEG1, xt, final=store)
    q.wait("sp", stores[-1])


def build_program(nc, ins, out):
    with ExitStack() as ctx:
        def sb(name, shape, dt):
            return ctx.enter_context(nc.sbuf_tensor("t_" + name, shape, dt))

        mem = {
            "X": sb("x", [P, 6144], F32), "H": sb("h", [P, 12288], F32R), "HID": sb("hid", [P, 8192], F32R),
            "WHI": sb("whi", [P, NH, SLOT], F32R), "WLO": sb("wlo", [P, NH, SLOT], F32R),
            "RAW": sb("raw", [P, NR, SLOT], F32), "MISC": sb("misc", [P, 14976], F32),
            "TMP": sb("tmp", [P, 2840], F32), "PAR": sb("par", [P, NPAR], F32), "CON": sb("con", [P, 388], F32),
            "MOD": sb("mod", [P, 192], F32), "PS": ctx.enter_context(nc.psum_tensor("ps", [P, 8, 512], F32)),
        }
        sem = lambda name: ctx.enter_context(nc.semaphore(name))
        sems = {
            "ring": [sem(f"d_ring{i}") for i in range(NR)], "par": sem("d_par"),
            "x": [sem(f"d_x{i}") for i in range(DC)], "misc": sem("d_misc"), "strip": sem("d_strip"), "out": sem("d_out"),
        }
        dram = dict(ins)
        dram["out"] = out
        plan = []
        dry = Engines(lambda name: object())
        queue_program(dry, mem, dram, sems, None, plan)
        q = Engines(sem)
        queue_program(q, mem, dram, sems, plan, [])
        block = ctx.enter_context(nc.Block())

        @block.sync
        def _(e):
            q.replay("sp", e)

        @block.tensor
        def _(e):
            q.replay("pe", e)

        @block.scalar
        def _(e):
            q.replay("act", e)

        @block.vector
        def _(e):
            q.replay("dve", e)

        @block.gpsimd
        def _(e):
            q.replay("pool", e)


def stationary(w):
    k, n = w.shape
    return np.ascontiguousarray(w.reshape(k // P, P, n // P, P).transpose(2, 1, 0, 3)).reshape(n // P, P, k)


def moving(w):
    n = w.shape[1]
    return np.ascontiguousarray(w.reshape(4, 2, P, n // 512, 512).transpose(3, 0, 2, 1, 4)).reshape(n // 512, 4, P, 1024)


def cols(v):
    return np.asarray(v).reshape(-1, P).T


def lay_out(i):
    g = {k: np.asarray(v) for k, v in i.items()}
    heads = np.array(HEAD_ORDER)
    w_in = g["w_in"][0]
    qw = w_in[:, 1024:1536].reshape(D, 8, 64)[:, heads].reshape(D, 512)
    w_in = np.concatenate([w_in[:, :1024], qw, w_in[:, 1536:]], 1)
    w_o = g["w_o"][0]
    w_o = np.concatenate([w_o[:512], w_o[512:].reshape(8, 64, D)[heads].reshape(512, D)], 0)
    g_att = g["g_attn_out"][0].reshape(8, 64)[heads].reshape(512)
    par = {
        "ffn1_pre_g": cols(g["ffn1_pre_g"]), "ffn1_post_g": cols(g["ffn1_post_g"]), "mix_pre_g": cols(g["mix_pre_g"]),
        "conv_w": cols(g["conv_w"]), "conv_b": cols(g["conv_b"]), "b_rg": cols(g["b_rg"]), "b_ig": cols(g["b_ig"]),
        "lam": cols(g["lru_lambda"]), "g_mix": np.concatenate([cols(g["g_lru_out"]), cols(g_att)], 1),
        "mix_post_g": cols(g["mix_post_g"]), "ffn2_pre_g": cols(g["ffn2_pre_g"]), "ffn2_post_g": cols(g["ffn2_post_g"]),
        "cond": np.stack([cols(g["c_2"]), cols(g["c_ctx_2"])], 2).reshape(P, 16),
        "ada_b": cols(g["ada_b_2"]), "ln_g": cols(g["ln_g_2"]), "ln_b": cols(g["ln_b_2"]),
        "sinks": np.broadcast_to(g["sinks"][0], (P, 8)), "decay": np.broadcast_to(g["ret_decay_2"].reshape(8), (P, 8)),
    }
    a = {"params": np.ascontiguousarray(np.concatenate([par[n] for n, _ in PARAMS], 1))}
    comb = np.zeros((P, 2), np.float32)
    comb[0, 0] = comb[2, 0] = comb[1, 1] = comb[3, 1] = 1
    a["consts"] = np.concatenate([np.eye(P, dtype=np.float32), np.full((P, P), 1 / 1024, np.float32),
                                  np.full((P, P), 1 / 512, np.float32), comb,
                                  np.full((P, 1), RMS_EPS, np.float32), np.full((P, 1), LN_EPS, np.float32)], 1)
    a["x"] = np.ascontiguousarray(g["x"][0].T).reshape(DC, P, L)
    a["ctx"] = np.ascontiguousarray(g["ctx_2"][0].T).reshape(DC, P, LC)
    a["gu1"], a["dn1"] = stationary(g["ffn1_w_gu"][0]), stationary(g["ffn1_w_down"][0])
    a["gu2"], a["dn2"] = stationary(g["ffn2_w_gu"][0]), stationary(g["ffn2_w_down"][0])
    a["gu3"], a["dn3"] = stationary(g["ffn_w13_2"][0]), stationary(g["ffn_w2_2"][0])
    a["gu4"], a["dn4"] = stationary(g["ffn_w13_2"][1]), stationary(g["ffn_w2_2"][1])
    a["w_in"], a["w_o"] = stationary(w_in), stationary(w_o)
    gates = np.zeros((P, 2, 4, P), np.float32)
    for n, name in enumerate(("w_rg", "w_ig")):
        for b in range(8):
            o = (b % 2) * 64
            gates[o:o + 64, n, b // 2, o:o + 64] = g[name][0, b]
    a["gates"] = gates.reshape(P, 1024)
    qi, kj = np.arange(P)[:, None], np.arange(2 * P)[None]
    rel = qi + P - kj
    a["mask1"] = np.where((rel >= 0) & (rel < 128), 0, NEG).astype(np.float32)
    a["ada"] = np.stack([moving(g["ada_w_2"][n]) for n in range(2)])
    rw = g["ret_w_in_2"]
    a["ret_qk"], a["ret_v"], a["ret_g"] = stationary(rw[:, :2048]), moving(rw[:, 2048:4096]), stationary(rw[:, 4096:])
    a["ret_o"] = stationary(g["ret_w_out_2"])
    a["dist"] = (np.arange(1152)[None] - 384 - np.arange(P)[:, None]).astype(np.float32)
    t = np.arange(L)
    inv = (np.float32(10000.0) ** (-np.arange(64, dtype=np.float32) / np.float32(64))).astype(np.float32)
    ang = np.concatenate([(t // 64).astype(np.float32)[:, None] * inv, (t % 64).astype(np.float32)[:, None] * inv], 1)
    a["rope"] = np.ascontiguousarray(np.concatenate([np.cos(ang).T, np.sin(ang).T], 1)).astype(np.float32)
    nw = g["na_w_qkv_2"]
    a["na_qk"], a["na_v"], a["na_o"] = stationary(nw[:, :2048]), moving(nw[:, 2048:]), stationary(g["na_w_out_2"])
    ci, r = np.arange(P)[:, None, None] // 8, np.arange(P)[:, None, None] % 8
    m, rr = np.arange(48)[None, :, None], np.arange(8)[None, None]
    a["rpb"] = np.ascontiguousarray(g["na_rpb_2"][:, rr - r + 7, np.clip(m - 16 - ci + 15, 0, 30)]).reshape(16, P, 384)
    masks = []
    for b in (0, 1, 3):
        band = min(max(16 * b - 8, 0), 32)
        q = 16 * b + np.arange(P)[:, None] // 8
        k = band + np.arange(256)[None] // 8
        ws = np.clip(q - 8, 0, 48)
        masks.append(np.where((k >= ws) & (k < ws + 16), 0, NEG).astype(np.float32))
    a["mask2"] = np.concatenate(masks, 1)
    return a


def kernel(**inputs):
    import concourse.bacc as bacc
    from concourse.bass_utils import run_bass_kernel_spmd

    nc = bacc.Bacc("TRN2", target_bir_lowering=False, num_devices=1, dynamic_dma_scratch_size=1024)
    arrays = lay_out(inputs)
    ins = {k: nc.dram_tensor("in_" + k, v.shape, F32, kind="ExternalInput").ap() for k, v in arrays.items()}
    out = nc.dram_tensor("out_x", (DC, P, L), F32, kind="ExternalOutput").ap()
    build_program(nc, ins, out)
    r = run_bass_kernel_spmd(nc, [{"in_" + k: v for k, v in arrays.items()}], core_ids=[0])
    y = np.asarray(r.results[0]["out_x"]).reshape(D, 64, 8)
    return np.ascontiguousarray(y.transpose(2, 1, 0)).reshape(1, L, D)
```

```python
import numpy as np
from contextlib import ExitStack

import concourse.bass as bass
from concourse import mybir

ALU = mybir.AluOpType
ACT = mybir.ActivationFunctionType
F32 = mybir.dt.float32
F32R = mybir.dt.float32r
AX_X = mybir.AxisListType.X

P = 128
L = 512
LC = 256
D = 1024
DC = D // P
FC = 2816 // P
SLOT = 1024
NR = 3
NH = 4
PARTS1 = (8, 7, 7)
PARTS2 = (5, 5, 4, 4, 4)
ALPHA = float((2 * 2) ** 0.25)
RMS_EPS = 1e-6
LN_EPS = 1e-5
NEG = -1e30
SEG1 = ((0, 512),)
SEG2 = ((0, 512), (512, 256))
ACC = 12560
GATE = 4608
BEHIND = [(0, 0, 0, 3), (0, 1, 0, 3), (1, 0, 1, 0), (1, 1, 1, 0), (1, 0, 2, 3)]
HEAD_ORDER = (0, 4, 1, 5, 2, 6, 3, 7)

PARAMS = [
    ("ffn1_pre_g", 8), ("ffn1_post_g", 8), ("mix_pre_g", 8), ("conv_w", 16), ("conv_b", 4),
    ("b_rg", 4), ("b_ig", 4), ("lam", 4), ("g_mix", 8), ("mix_post_g", 8),
    ("ffn2_pre_g", 8), ("ffn2_post_g", 8), ("cond", 16), ("ada_b", 96), ("ln_g", 32), ("ln_b", 32),
    ("sinks", 8), ("decay", 8),
]
POFF, _n = {}, 0
for _name, _w in PARAMS:
    POFF[_name] = _n
    _n += _w
NPAR = _n

CONSTS = [("ident", 128), ("one1024", 128), ("one512", 128), ("comb", 2), ("eps", 2)]


class Engines:

    def __init__(self, sem):
        self.sem = sem
        self.queues = {k: [] for k in ("pe", "act", "dve", "pool", "sp")}
        self.now = {}
        self.count = {}
        self.waited = {}

    def stage(self, name):
        for k in ("pe", "act", "dve", "pool"):
            self.now[k] = self.sem(f"s_{k}_{name}")

    def wait(self, eng, *tokens):
        for t in tokens:
            if t is None:
                continue
            if isinstance(t, list):
                self.wait(eng, *t)
                continue
            s, v = t
            if self.waited.get((eng, id(s)), 0) < v:
                self.waited[(eng, id(s))] = v
                self.queues[eng].append(lambda e, s=s, v=v: e.wait_ge(s, v))

    def op(self, eng, waits, fn, signal=True, sem=None, step=1):
        self.wait(eng, *waits)
        if not signal:
            self.queues[eng].append(fn)
            return None
        s = self.now[eng] if sem is None else sem
        self.count[id(s)] = self.count.get(id(s), 0) + step
        self.queues[eng].append(lambda e: fn(e).then_inc(s, step))
        return (s, self.count[id(s)])

    def replay(self, eng, e):
        for fn in self.queues[eng]:
            fn(e)


class Slots:

    def __init__(self):
        self.users = {}

    def __getitem__(self, keys):
        return [self.users.get(k) for k in keys]

    def __setitem__(self, keys, tokens):
        for k in keys:
            self.users[k] = tokens


def queue_program(q, mem, dram, sems, plan, seen):
    X, H, HID, WHI, WLO, RAW = mem["X"], mem["H"], mem["HID"], mem["WHI"], mem["WLO"], mem["RAW"]
    M, TMP, PAR, CON, MOD, PS = mem["MISC"], mem["TMP"], mem["PAR"], mem["CON"], mem["MOD"], mem["PS"]

    def pe(waits, fn, signal=True):
        return q.op("pe", waits, fn, signal)

    def act(waits, fn):
        return q.op("act", waits, fn)

    def dve(waits, fn):
        return q.op("dve", waits, fn)

    def pool(waits, fn):
        return q.op("pool", waits, fn)

    def load(waits, dst, src, sem):
        return q.op("sp", waits, lambda e: e.dma_start(dst, src), sem=sem, step=16)

    def par(name, c, p0=0, p1=P):
        return PAR[p0:p1, POFF[name] + c:POFF[name] + c + 1]

    ident = CON[:, 0:128]
    one1024 = CON[:, 128:256]
    one512 = CON[:, 256:384]
    comb = CON[0:4, 384:386]
    EPS = {RMS_EPS: CON[:, 386:387], LN_EPS: CON[:, 387:388]}

    free = {b: [] for b in range(8)}
    turn = {}

    def bank(some=(0, 1, 2, 3, 4, 5)):
        i = turn.get(some, 0)
        turn[some] = i + 1
        return some[i % len(some)]

    chains = {}

    def step(s):
        wait = next(chains[s][1], None)
        if wait is None:
            del chains[s]
        else:
            chains[s][0] = wait

    def tick():
        for s in sorted(chains):
            chains[s][0] -= 1
            if chains[s][0] <= 0:
                step(s)

    def force(t0, n):
        for s in range(t0 // 256, -(-(t0 + n) // 256)):
            while s in chains:
                step(s)

    def cover(d, k, t0, n):
        return [d[(k, s)] for s in range(t0 // 256, -(-(t0 + n) // 256))]

    ring = {"used": 0, "conv": 0, "dma": 0}
    dma_done, hi_done, lo_done, mm_done = {}, {}, {}, {}

    def issue_load(j):
        waits = [] if j < NR else [hi_done[j - NR], lo_done[j - NR]]
        src, shape = plan[j]
        dst = RAW[:, j % NR, 0:int(np.prod(shape))]
        if len(shape) == 2:
            dst = dst.rearrange("p (a b) -> p a b", a=shape[0])
        dma_done[j] = load(waits, dst, src, sems["ring"][j % NR])

    def issue_split(j):
        n = int(np.prod(plan[j][1]))
        over = [mm_done[j - NH]] if j >= NH else []
        raw, hi, lo = RAW[:, j % NR, 0:n], WHI[:, j % NH, 0:n], WLO[:, j % NH, 0:n]
        hi_done[j] = act([dma_done[j], *over], lambda e: e.copy(hi, raw))
        lo_done[j] = (pool if j % 2 else dve)([dma_done[j], hi_done[j], *over], lambda e: e.tensor_tensor(lo, raw, hi, ALU.subtract))

    def prepare(upto):
        while ring["conv"] < min(upto + 1, len(plan)) and (ring["conv"] < NH or ring["conv"] - NH in mm_done):
            k = ring["conv"]
            while ring["dma"] < min(k + NR, len(plan)):
                issue_load(ring["dma"])
                ring["dma"] += 1
            issue_split(k)
            ring["conv"] += 1

    def next_block(src, shape):
        j = ring["used"]
        ring["used"] += 1
        seen.append((src, shape))
        if plan is None:
            return j, j % NH, []
        prepare(j)
        return j, j % NH, [hi_done[j], lo_done[j]]

    def block_over(j, token):
        mm_done[j] = token
        if plan is not None:
            prepare(j + NH)

    def products(out, whi, wlo, xhi, xlo, waits, first, last, signal):
        pe(waits, lambda e: e.matmul(out, whi, xlo, start=first, stop=False), False)
        pe([], lambda e: e.matmul(out, wlo, xhi, start=False, stop=False), False)
        return pe([], lambda e: e.matmul(out, whi, xhi, start=False, stop=last), signal)

    home = {"buf": X, "pitch": 768}

    def xs(c, t0=0, n=L):
        return home["buf"][:, c * home["pitch"] + t0:c * home["pitch"] + t0 + n]

    def hs(part, c, t0, n):
        base = part * 6144 + c * 768 + t0
        return H[:, base:base + n]

    def hacts(part, k, t0, n):
        return hs(part, k, t0, n)

    def columns(specs, segs, batch=1, banks=None, between=None):
        done = None
        for i in range(0, len(specs), batch):
            some = specs[i:i + batch]
            held = [next_block(sp[0], sp[1]) for sp in some]
            for si, (t0, n) in enumerate(segs):
                for (_, _, nk, acts, deps, outs), (j, slot, ready) in zip(some, held):
                    for base, post in outs:
                        force(t0, n)
                        b = bank(banks) if banks else bank()
                        for k in range(nk):
                            o = base + k * P
                            done = products(PS[:, b, 0:n], WHI[:, slot, o:o + P], WLO[:, slot, o:o + P],
                                            acts(0, k, t0, n), acts(1, k, t0, n),
                                            [*ready, deps(k, t0, n), *(free[b] if k == 0 else [])],
                                            k == 0, k == nk - 1, k == nk - 1)
                        free[b] = []
                        free[b] = free[b] + post(b, t0, n, done)
                        tick()
                    if si == len(segs) - 1:
                        block_over(j, done)
            if between:
                for _ in some:
                    between()
        return done

    def token_rows(blocks, h_ready, over, dest):
        held = [next_block(src, (SLOT,)) for src in blocks]
        v_ready = {}
        done = None
        for tt in (4, 5, 0, 1, 2, 3):
            force(tt * P, P)
            b = bank()
            for k in range(DC):
                j, slot, ready = held[k // 2]
                w = slice((k % 2) * 512, (k % 2 + 1) * 512)
                done = products(PS[:, b, :], hs(0, k, tt * P, P), hs(1, k, tt * P, P), WHI[:, slot, w], WLO[:, slot, w],
                                [*ready, cover(h_ready, k, tt * P, P), *(free[b] if k == 0 else [])],
                                k == 0, k == 7, k == 7 or (tt == 3 and k % 2 == 1))
                if tt == 3 and k % 2 == 1:
                    block_over(j, done)
            dst = dest(tt)
            v_ready[tt] = act([done, over], lambda e, dst=dst, b=b: e.copy(dst, PS[:, b, :]))
            free[b] = [v_ready[tt]]
            tick()
        return v_ready, done

    ra = {"a": 0, "b": 0}
    rfree = Slots()

    def tmp(which, n):
        w = 1 if n <= 256 else 2
        i = -(-ra[which] // w) * w % 4
        ra[which] = i + w
        base = (0 if which == "a" else 1024) + i * 256
        return TMP[:, base:base + n], [(which, i + k) for k in range(w)]

    def both(which):
        return [(which, k) for k in range(4)]

    def rs_view(n, t0=0):
        return TMP[:, 2048 + t0:2048 + t0 + n]

    rs_read = {s: {} for s in range(3)}

    def reads_rs(eng, t0, n, token):
        for s in range(t0 // 256, (t0 + n) // 256):
            rs_read[s][eng] = token

    def split(hi, lo, src, waits, over):
        a = act([waits, over], lambda e: e.copy(hi, src))
        d = dve([waits, over, a], lambda e: e.tensor_tensor(lo, src, hi, ALU.subtract))
        return [a, d]

    sums = {}

    def begin_sum(s, over):
        sums[s] = {"n": 0, "tok": [None, None], "over": over}

    def acc_view(s, part):
        return M[:, ACC + s * 512 + part * 256:ACC + s * 512 + (part + 1) * 256]

    def sum_add(s, src, tok, square):
        me = sums[s]
        part = (me["n"] + 1) % 2
        acc = acc_view(s, part)
        if me["n"] < 2:
            me["tok"][part] = act([tok, me["over"]], lambda e: e.activation(acc, src, ACT.Square if square else ACT.Identity))
        else:
            eng = dve if part == 0 else pool
            if square:
                sq, key = tmp("a", 256)
                a = act([tok, rfree[key]], lambda e: e.activation(sq, src, ACT.Square))
                me["tok"][part] = eng([a, me["tok"][part]], lambda e: e.tensor_tensor(acc, acc, sq, ALU.add))
                rfree[key] = [me["tok"][part]]
            else:
                me["tok"][part] = eng([tok, me["tok"][part]], lambda e: e.tensor_tensor(acc, acc, src, ALU.add))
        me["n"] += 1

    def join_sum(s, ones, b):
        me = sums[s]
        pe([me["tok"][1], *free[b]], lambda e: e.matmul(PS[:, b, 0:256], ones, acc_view(s, 1), start=True, stop=False), False)
        state["joined"] = pe([me["tok"][0]], lambda e: e.matmul(
            PS[:, b, 0:256], ones, acc_view(s, 0), start=False, stop=True))
        return state["joined"]

    def rstd(b, n, t0, waits, eps):
        over = [list(rs_read[s].values()) for s in range(t0 // 256, -(-(t0 + n) // 256))]
        a = act([waits, over], lambda e: e.activation(rs_view(n, t0), PS[:, b, 0:n], ACT.Sqrt, bias=EPS[eps]))
        free[b] = [a]
        return dve([a], lambda e: e.reciprocal(rs_view(n, t0), rs_view(n, t0)))

    def mean_square(tiles, waits, n, ones, b):
        last = None
        for i, t in enumerate(tiles):
            sq, key = tmp("a", n)
            a = act([waits[i], rfree[key]], lambda e, sq=sq, t=t: e.activation(sq, t, ACT.Square))
            last = pe([a, *(free[b] if i == 0 else [])],
                      lambda e, sq=sq, i=i: e.matmul(PS[:, b, 0:n], ones, sq, start=i == 0, stop=i == len(tiles) - 1))
            rfree[key] = [last]
        return last

    ada = {"n": 0, "limit": 48, "rows": None}
    ABANK, MBANK = 6, 7
    mod_ready = {}

    def ada_rows():
        if ada["rows"] is None:
            return
        layer, n, a = ada["rows"]
        ada["rows"] = None
        for j in range(4):
            col = n * 4 + j
            row = X[0:4, (j // 2) * 768 + 512 + (j % 2) * 128:(j // 2) * 768 + 640 + (j % 2) * 128]
            ada["row_read"] = pe([a, *(free[MBANK] if col == 0 else [])], lambda e, col=col, row=row: e.matmul(
                PS[:, MBANK, col * 2:col * 2 + 2], row, comb, start=True, stop=True, skip_group_check=True), j == 3)
        if n < 11:
            return
        for who in range(2):
            src = PS[:, MBANK, 0:96].rearrange("p (c w) -> p w c", w=2)[:, who, :]
            o = (layer * 2 + who) * 48
            d = dve([ada["row_read"]], lambda e, src=src, o=o, layer=layer: e.tensor_tensor(
                MOD[:, o:o + 48], src, PAR[:, POFF["ada_b"] + layer * 48:POFF["ada_b"] + layer * 48 + 48], ALU.add))
            free[MBANK] = [d]
            t = []
            for g in (1, 4):
                v = MOD[:, o + g * 8:o + g * 8 + 8]
                t.append(dve([d], lambda e, v=v: e.tensor_scalar(v, v, 1.0, None, ALU.add)))
            for idx, (lay, w, ln, g) in enumerate(BEHIND):
                if (lay, w) == (layer, who):
                    v = MOD[:, 192 + idx * 8:192 + idx * 8 + 8]
                    lb = PAR[:, POFF["ln_b"] + ln * 8:POFF["ln_b"] + ln * 8 + 8]
                    sc_, sh_ = MOD[:, o + (g + 1) * 8:o + (g + 2) * 8], MOD[:, o + g * 8:o + (g + 1) * 8]
                    x = dve([t], lambda e, v=v, lb=lb, sc_=sc_: e.tensor_tensor(v, lb, sc_, ALU.mult))
                    t.append(dve([x], lambda e, v=v, sh_=sh_: e.tensor_tensor(v, v, sh_, ALU.add)))
            mod_ready[layer] = t[-1]

    def ada_step():
        i = ada["n"]
        if i >= ada["limit"]:
            ada_rows()
            return
        ada["n"] += 1
        layer, r = divmod(i, 48)
        n, blk = divmod(r, 4)
        jj, slot, ready = next_block(dram["ada"][layer, n, blk], (SLOT,))
        out = PS[:, ABANK, 0:512]
        done = None
        for kk in range(2):
            k = blk * 2 + kk
            cnd = H[:, k * 768 + 512:k * 768 + 640]
            for w in (WHI, WLO):
                first = k == 0 and w is WHI
                last = k == 7 and w is WLO
                mv = w[:, slot, kk * 512:(kk + 1) * 512]
                done = pe([*ready, *cond_ready, *(free[ABANK] if first else [])],
                          lambda e, cnd=cnd, mv=mv, first=first, last=last: e.matmul(out, cnd, mv, start=first, stop=last),
                          kk == 1 and w is WLO)
        block_over(jj, done)
        ada_rows()
        if blk == 3:
            row = X[0:4, 0:1536].rearrange("p (c t) -> p c t", t=768)[:, :, 512:768]
            a = act([done, ada.get("row_read")], lambda e: e.copy(
                row, PS[0:4, ABANK, 0:512].rearrange("p (c t) -> p c t", c=2)))
            free[ABANK] = [a]
            ada["rows"] = (layer, n, a)

    def mod(layer, who, g, c):
        o = (layer * 2 + who) * 48 + g * 8 + c
        return MOD[:, o:o + 1]

    state = {"h_over": [], "hid_over": [], "misc_over": [], "acc_over": []}
    h_ready, xt, pre = {}, {}, {}

    def to_rms(gain):
        def send(c, s):
            hi, lo, x = hs(0, c, s * 256, 256), hs(1, c, s * 256, 256), xs(c, s * 256, 256)
            a = act([xt[(c, s)], state["h_over"]], lambda e: e.activation(hi, x, ACT.Identity, scale=par(gain, c)))
            d = dve([xt[(c, s)], a, state["h_over"]], lambda e: e.scalar_tensor_tensor(
                out=lo, in0=x, scalar=par(gain, c), in1=hi, op0=ALU.mult, op1=ALU.subtract))
            h_ready[(c, s)] = [a, d]
            if c == 0:
                begin_sum(s, [])
                pre.pop(s, None)
            sum_add(s, x, xt[(c, s)], True)
        return send

    def pre_rs(t0, n):
        for s in range(t0 // 256, (t0 + n) // 256):
            if s not in pre:
                b = bank()
                pre[s] = rstd(b, 256, s * 256, join_sum(s, one1024, b), RMS_EPS)
        return [pre[s] for s in range(t0 // 256, (t0 + n) // 256)]

    def to_modulated(layer, g):
        def send(c, s):
            who = s // 2
            hi, lo, x = hs(0, c, s * 256, 256), hs(1, c, s * 256, 256), xs(c, s * 256, 256)
            sc_, sh_ = mod(layer, who, g + 1, c), mod(layer, who, g, c)
            t, key = tmp("b", 256)
            w = [xt[(c, s)], mod_ready[layer]]
            over = state["h_over"] if s < 2 else ada["row_read"]
            a = act([w, over], lambda e: e.activation(hi, x, ACT.Identity, scale=sc_, bias=sh_))
            d = dve([w, rfree[key]], lambda e: e.tensor_scalar(t, x, sc_, sh_, ALU.mult, ALU.add))
            d2 = dve([d, a, over], lambda e: e.tensor_tensor(lo, t, hi, ALU.subtract))
            h_ready[(c, s)] = [a, d2]
            rfree[key] = [d2]
            xt[(c, s)] = act([a, d], lambda e: e.mul(x, x, ALPHA))
        return send

    def start_chain(s, wait, gen):
        chains[s] = [wait, gen]

    def norm_chain(s, F, f_tok, post, send):
        b = bank()
        r = rstd(b, 256, s * 256, join_sum(s, one1024, b), RMS_EPS)
        rs = rs_view(256, s * 256)
        for j in range(DC + 3):
            if j < DC:
                f, x = F(j)[:, s * 256:(s + 1) * 256], xs(j, s * 256, 256)
                d = dve([f_tok[(j, s)], r], lambda e, j=j, f=f: e.scalar_tensor_tensor(
                    out=f, in0=f, scalar=par(post, j), in1=rs, op0=ALU.mult, op1=ALU.mult))
                reads_rs("dve", s * 256, 256, d)
                xt[(j, s)] = pool([d, xt[(j, s)]], lambda e, f=f, x=x: e.tensor_tensor(x, x, f, ALU.add))
            if j >= 3:
                send(j - 3, s)
        state["misc_over"] = [state["misc_over"], xt[(6, s)], xt[(7, s)]]
        if False:
            yield 0

    def layer_norm_chain(s, layer, which, send, wait=2):
        b = bank()
        m = join_sum(s, one1024, b)
        begin_sum(s, [m])
        ln = layer * 2 + which
        for c in range(DC):
            x = xs(c, s * 256, 256)
            xt[(c, s)] = dve([m, xt[(c, s)]], lambda e, x=x: e.tensor_tensor(x, x, PS[:, b, 0:256], ALU.subtract))
            free[b] = [xt[(c, s)]]
        for c in range(DC):
            sum_add(s, xs(c, s * 256, 256), xt[(c, s)], True)
        yield wait
        b2 = bank()
        r = rstd(b2, 256, s * 256, join_sum(s, one1024, b2), LN_EPS)
        rs = rs_view(256, s * 256)
        held = {}
        for c in range(DC + 2):
            if c < DC:
                x = xs(c, s * 256, 256)
                g = PAR[:, POFF["ln_g"] + ln * 8 + c:POFF["ln_g"] + ln * 8 + c + 1]
                t, key = tmp("b", 256)
                d = dve([xt[(c, s)], r, rfree[key]], lambda e, t=t, x=x, g=g: e.scalar_tensor_tensor(
                    out=t, in0=x, scalar=g, in1=rs, op0=ALU.mult, op1=ALU.mult))
                reads_rs("dve", s * 256, 256, d)
                held[c] = (t, key, d)
            if c >= 2:
                t, key, d = held[c - 2]
                rfree[key] = send(c - 2, s, t, d)

    def after_ln(ln, layer, g, permute=False):
        def send(c, s, t, d):
            who = s // 2
            idx = [k for k, v in enumerate(BEHIND) if v == (layer, who, ln, g)][0]
            sc_, bs_ = mod(layer, who, g + 1, c), MOD[:, 192 + idx * 8 + c:192 + idx * 8 + c + 1]
            lb = MOD[:, 232 + ln * 8 + c:232 + ln * 8 + c + 1]
            x = xs(c, s * 256, 256)
            if permute and s < 2:
                pv = lambda part: hs(part, c, 0, 512).rearrange("p (c r) -> p r c", r=8)[:, 4 * s:4 * s + 4, :]
                sv = lambda v: v.rearrange("p (r c) -> p r c", c=64)
            else:
                pv = lambda part: hs(part, c, s * 256, 256)
                sv = lambda v: v
            u, ukey = tmp("a", 256)
            w = [d, mod_ready[layer]]
            a1 = act([w, state["h_over"]], lambda e: e.activation(pv(0), sv(t), ACT.Identity, scale=sc_, bias=bs_))
            d1 = pool([w, rfree[ukey]], lambda e: e.tensor_scalar(u, t, sc_, bs_, ALU.mult, ALU.add))
            d2 = dve([a1, d1], lambda e: e.tensor_tensor(pv(1), sv(u), pv(0), ALU.subtract))
            a2 = act([d, lnb_ready], lambda e: e.activation(x, t, ACT.Identity, scale=ALPHA, bias=lb))
            rfree[ukey] = [d2]
            h_ready[(c, s)] = [a1, d2]
            xt[(c, s)] = a2
            return [a1, a2, d1]
        return send

    def gated(layer, g, last, chain):
        def post(pi, j, b, t0, n, done):
            who = 0 if t0 < 512 else 1
            x, gt = xs(j, t0, n), mod(layer, who, g, j)
            d = dve([done, cover(xt, j, t0, n)], lambda e: e.scalar_tensor_tensor(
                out=x, in0=PS[:, b, 0:n], scalar=gt, in1=x, op0=ALU.mult, op1=ALU.add))
            for s in range(t0 // 256, (t0 + n) // 256):
                xt[(j, s)] = d
                if pi == last:
                    summed(s, j, xs(j, s * 256, 256), d, False, chain)
            return [d]
        return post

    def summed(s, j, src, tok, square, chain):
        if j == 0:
            begin_sum(s, state["acc_over"])
        sum_add(s, src, tok, square)
        if j == DC - 1:
            start_chain(s, 2, chain(s))

    def ffn(gu, dn, parts, segs, subs, down_post, scaled, between=None):
        pitch = 512 if len(segs) == 1 else 768

        def hid(half, k, t0, n):
            return HID[:, half * 4096 + k * pitch + t0:half * 4096 + k * pitch + t0 + n]

        c0 = 0
        over = state["hid_over"]
        for i in range(4):
            rfree[[("gate", i)]] = [state["misc_over"]]
        for pi, size in enumerate(parts):
            ready, gate = {}, {}

            def gate_post(k):
                def post(b, t0, n, done):
                    gi = turn.get("gate", 0)
                    turn["gate"] = gi + 1
                    s, key = M[:, GATE + gi % 4 * 512:GATE + gi % 4 * 512 + n], [("gate", gi % 4)]
                    rs = rs_view(n, t0)
                    if scaled:
                        r = pre_rs(t0, n)
                        d = dve([done, r, rfree[key]], lambda e: e.tensor_tensor(s, PS[:, b, 0:n], rs, ALU.mult))
                        a = act([d], lambda e: e.activation(s, s, ACT.Silu))
                        p_ = pool([a], lambda e: e.tensor_tensor(s, s, rs, ALU.mult))
                        reads_rs("pool", t0, n, p_)
                        gate[(k, t0)] = (s, key, p_)
                        return [d]
                    a = act([done, rfree[key]], lambda e: e.activation(s, PS[:, b, 0:n], ACT.Silu))
                    gate[(k, t0)] = (s, key, a)
                    return [a]
                return post

            def up_post(k, over=over):
                def post(b, t0, n, done):
                    s, key, a = gate[(k, t0)]
                    t, key2 = tmp("b", n)
                    d = dve([done, a, rfree[key2]], lambda e: e.tensor_tensor(t, s, PS[:, b, 0:n], ALU.mult))
                    rfree[key] = [d]
                    got = split(hid(0, k, t0, n), hid(1, k, t0, n), t, d, over)
                    rfree[key2] = got
                    for sb_ in range(t0 // 256, (t0 + n) // 256):
                        ready[(k, sb_)] = got
                    return [d]
                return post

            hw = lambda k, t0, n: cover(h_ready, k, t0, n)
            specs = []
            for k in range(size):
                specs.append((gu[c0 + k], (SLOT,), DC, hacts, hw, [(0, gate_post(k))]))
                specs.append((gu[FC + c0 + k], (SLOT,), DC, hacts, hw, [(0, up_post(k))]))
            if pi == 0:
                columns(specs[:4], subs, batch=4, between=between)
                specs = specs[4:]
            last_h = columns(specs, segs, between=between)
            hw2 = lambda k, t0, n: cover(ready, k, t0, n)
            specs = [(dn[j][:, c0 * P:(c0 + size) * P], (size * P,), size, hid, hw2,
                      [(0, lambda b, t0, n, done, j=j, pi=pi: down_post(pi, j, b, t0, n, done))]) for j in range(DC)]
            if pi == len(parts) - 1:
                state["h_over"] = [last_h]
                last = columns(specs, subs, batch=4, between=between)
            else:
                last = columns(specs, segs, between=between)
            over = [last]
            c0 += size
        state["hid_over"] = over
        state["misc_over"] = [state["misc_over"], *(rfree[[("gate", i)]] for i in range(4))]

    SUB1 = ((0, 256), (256, 256))
    SUB2 = ((512, 256), (0, 256), (256, 256))

    def first_ffn(post, gu, dn, send, between):
        F = lambda j: M[:, j * 512:(j + 1) * 512]
        f_tok = {}

        def down_post(pi, j, b, t0, n, done):
            f = F(j)[:, t0:t0 + n]
            if pi == 0:
                d = act([done, state["misc_over"]], lambda e: e.copy(f, PS[:, b, 0:n]))
            else:
                d = dve([done, cover(f_tok, j, t0, n)], lambda e: e.tensor_tensor(f, f, PS[:, b, 0:n], ALU.add))
            for s in range(t0 // 256, (t0 + n) // 256):
                f_tok[(j, s)] = d
                if pi == 2:
                    summed(s, j, F(j)[:, s * 256:(s + 1) * 256], d, True,
                           lambda s: norm_chain(s, F, f_tok, post, send))
            return [d]

        ffn(gu, dn, PARTS1, SEG1, SUB1, down_post, True, between)

    q.stage("start")
    load([], PAR[:, :], dram["params"], sems["par"])
    par_ready = load([], CON[:, :], dram["consts"], sems["par"])
    for eng in ("pe", "act", "dve", "pool"):
        q.wait(eng, par_ready)
    for c in range(DC):
        t = load([], xs(c), dram["x"][c], sems["x"][c])
        xt[(c, 0)] = xt[(c, 1)] = t
    cnd_all = H[:, 0:6144].rearrange("p (k t) -> p k t", t=768)[:, :, 512:640]
    z = TMP[:, 1024:1152]
    d0 = dve([], lambda e: e.memset(z, 0.0))
    d1 = None
    for k in range(8):
        d1 = dve([d0], lambda e, k=k: e.tensor_copy(cnd_all[:, k, :], z))
    sc = TMP[:, 1152:1168]
    a0 = act([], lambda e: e.activation(sc, PAR[:, POFF["cond"]:POFF["cond"] + 16], ACT.Silu))
    sc2 = sc.rearrange("p (k w) -> p k w", w=2)
    a1 = act([a0, d1], lambda e: e.copy(cnd_all[:, :, 0:2], sc2))
    d2 = dve([a1], lambda e: e.tensor_tensor(cnd_all[:, :, 2:4], sc2, cnd_all[:, :, 0:2], ALU.subtract))
    cond_ready = [d2]
    rfree[both("b")] = [d2, d1]
    lnb_ready = dve([], lambda e: e.tensor_scalar(
        MOD[:, 232:264], PAR[:, POFF["ln_b"]:POFF["ln_b"] + 32], ALPHA, None, ALU.mult))
    for name in ("ffn1_post_g", "ffn2_post_g"):
        v = PAR[:, POFF[name]:POFF[name] + 8]
        t = dve([], lambda e, v=v: e.tensor_scalar(v, v, 0.5, None, ALU.mult))
    q.wait("dve", t)

    def first_mixer():
        QA, KA, VA, SA, PT, OA, XL = 0, 2048, 2560, 3072, 5120, 7168, 9216
        BD, MASK, GA, SM = 11280, 12304, 12560, 14608
        XC, AA, UA = 0, 3072, 5120
        pro = state["misc_over"]
        bd_ready = load([pro], M[:, BD:BD + 1024], dram["gates"], sems["misc"])
        mask_ready = load([pro], M[:, MASK:MASK + 256], dram["mask1"], sems["misc"])
        bd_ready = mask_ready
        hw = lambda k, t0, n: cover(h_ready, k, t0, n)
        win = dram["w_in"]

        sm = lambda o, n: M[:, SM + o:SM + o + n]
        nsink = sm(0, 8)
        t = dve([pro, par_ready], lambda e: e.tensor_scalar(nsink, PAR[:, POFF["sinks"]:POFF["sinks"] + 8], -1.0, None, ALU.mult))
        nsink_ready = t
        lam = PAR[:, POFF["lam"]:POFF["lam"] + 4]
        en, den, ratio, z, pl, mn, cls, sp_ = (sm(8 + 4 * i, 4) for i in range(8))
        t = dve([pro], lambda e: e.tensor_scalar(mn, lam, -1.0, None, ALU.mult))
        t = dve([t], lambda e: e.tensor_tensor(en, mn, lam, ALU.min))
        t = act([t], lambda e: e.activation(en, en, ACT.Exp))
        t = dve([t], lambda e: e.tensor_scalar(den, en, 2.0, None, ALU.add))
        t = dve([t], lambda e: e.reciprocal(sp_, den))
        t = dve([t], lambda e: e.tensor_tensor(ratio, en, sp_, ALU.mult))
        t = dve([t], lambda e: e.tensor_tensor(z, ratio, ratio, ALU.mult))
        t = dve([t], lambda e: e.tensor_scalar(pl, z, 1.0 / 15, 1.0 / 13, ALU.mult, ALU.add))
        for k in (11, 9, 7, 5, 3, 1):
            t = dve([t], lambda e: e.tensor_tensor(pl, pl, z, ALU.mult))
            t = dve([t], lambda e, k=k: e.tensor_scalar(pl, pl, 1.0 / k, None, ALU.add))
        t = dve([t], lambda e: e.tensor_tensor(pl, pl, ratio, ALU.mult))
        t = dve([t], lambda e: e.tensor_scalar(mn, lam, 0.0, None, ALU.min))
        t = dve([t], lambda e: e.scalar_tensor_tensor(out=cls, in0=pl, scalar=-2.0, in1=mn, op0=ALU.mult, op1=ALU.add))
        cls_ready = dve([t], lambda e: e.tensor_scalar(cls, cls, 8.0, None, ALU.mult))

        q_ready = {g: [] for g in range(5)}

        def scaled_to(dst, got):
            def post(b, t0, n, done):
                r, d_ = pre_rs(t0, n), dst(t0, n)
                d = dve([done, r, pro], lambda e: e.tensor_tensor(d_, PS[:, b, 0:n], rs_view(n, t0), ALU.mult))
                reads_rs("dve", t0, n, d)
                got.append(d)
                return [d]
            return post

        at = lambda base: (lambda t0, n: M[:, base + t0:base + t0 + n])
        vt_ready = []
        specs = [(win[8 + c], (SLOT,), DC, hacts, hw, [(0, scaled_to(at(QA + c * 512), q_ready[c]))]) for c in range(5)]
        specs.append((win[13], (SLOT,), DC, hacts, hw, [(0, scaled_to(at(OA), vt_ready))]))
        columns(specs[:4], SUB1, batch=4)
        columns(specs[4:], SEG1)
        b = bank()
        for tt in range(4):
            turned = pe([vt_ready, free[b]], lambda e, tt=tt, b=b: e.transpose(
                PS[:, b, tt * P:(tt + 1) * P], M[:, OA + tt * P:OA + (tt + 1) * P], ident), tt == 3)
        v_ready = dve([turned], lambda e, b=b: e.tensor_copy(M[:, VA:VA + 512], PS[:, b, :]))
        free[b] = [v_ready]
        for bb in range(8):
            q.wait("pe", free[bb])
        pre_read = list(pre.values())

        XLc = lambda c, o, n: M[:, XL + c * 515 + o:XL + c * 515 + o + n]
        Gc = lambda c: M[:, GA + c * 512:GA + (c + 1) * 512]
        pad = [dve([pro], lambda e, c=c: e.memset(XLc(c, 0, 3), 0.0)) for c in range(4)]
        xl_ready, g_ready = {}, {}

        def lru_projection(i):
            dst = XLc(i, 3, 512) if i < 4 else Gc(i - 4)

            def post(b, t0, n, done):
                a = act([done, pro, pre_read], lambda e: e.copy(dst, PS[:, b, :]))
                p_ = pool([a, pre_read], lambda e: e.tensor_tensor(dst, dst, rs_view(L), ALU.mult))
                reads_rs("pool", 0, L, p_)
                if i < 4:
                    xl_ready[i] = p_
                else:
                    g_ready[i - 4] = act([p_], lambda e: e.activation(dst, dst, ACT.Gelu_apprx_tanh))
                return [a]

            last = columns([(win[i], (SLOT,), DC, hacts, hw, [(0, post)])], SEG1, banks=(7,))
            state["h_over"] = [last]

        units = [(n, kv) for n in range(4) for kv in range(2)]
        st = {}
        att_free = {("s", 0): [], ("s", 1): [], ("p", 0): [], ("p", 1): []}

        def scores(i):
            n, kv = units[i]
            NK = P if n == 0 else 2 * P
            k0 = n * P - (NK - P)
            b0 = (0, 2)[i % 2]
            pp = slice(kv * 64, kv * 64 + 64)
            for g in range(4):
                bb = b0 + g // 2
                done = pe([q_ready[g], q_ready[4], free[bb] if g % 2 == 0 else []], lambda e, g=g, bb=bb: e.matmul(
                    PS[:, bb, (g % 2) * 256:(g % 2) * 256 + NK], M[pp, QA + g * 512 + n * P:QA + g * 512 + (n + 1) * P],
                    M[pp, KA + k0:KA + k0 + NK], start=True, stop=True, skip_group_check=True), g == 3)
            ps = PS[:, b0:b0 + 2, :].rearrange("p b (g k) -> p (b g) k", k=256)[:, :, 0:NK]
            s = M[:, SA + (i % 2) * 1024:SA + (i % 2) * 1024 + 4 * NK].rearrange("p (g k) -> p g k", g=4)
            mk = M[:, MASK + 256 - NK:MASK + 256].unsqueeze(1).to_broadcast([P, 4, NK])
            d = dve([done, mask_ready, att_free[("s", i % 2)]], lambda e: e.scalar_tensor_tensor(
                out=s, in0=ps, scalar=0.125, in1=mk, op0=ALU.mult, op1=ALU.add))
            free[b0] = free[b0 + 1] = [d]
            o = 48 + (i % 2) * 24
            nm, es, sums, rec = sm(o, 4), sm(o + 4, 4), sm(o + 8, 4), sm(o + 12, 4)
            m1 = dve([d], lambda e: e.tensor_reduce(nm, s, AX_X, ALU.max, negate=True))
            m2 = dve([m1, nsink_ready], lambda e: e.tensor_tensor(nm, nm, sm(kv * 4, 4), ALU.min))
            m3 = dve([m2], lambda e: e.tensor_tensor(es, nm, sm(kv * 4, 4), ALU.subtract))
            x = [act([m2], lambda e, g=g: e.activation(s[:, g, :], s[:, g, :], ACT.Exp, bias=nm[:, g:g + 1],
                                                       accum_out=sums[:, g:g + 1])) for g in range(4)]
            x.append(act([m3], lambda e: e.activation(es, es, ACT.Exp)))
            r1 = dve(x, lambda e: e.tensor_tensor(es, es, sums, ALU.add))
            r2 = dve([r1], lambda e: e.reciprocal(rec, es))
            p = [dve([r2], lambda e, g=g: e.tensor_scalar(s[:, g, :], s[:, g, :], rec[:, g:g + 1], None, ALU.mult))
                 for g in range(4)]
            st[i] = (s, NK, p)

        def turn_weights(i):
            s, NK, p = st[i]
            n, kv = units[i]
            KT = NK // P
            ev = []
            for kt in range(KT):
                bb = 4 + kt
                for g in range(4):
                    done = pe([p[g], free[bb] if g == 0 else []], lambda e, g=g, bb=bb, kt=kt: e.transpose(
                        PS[:, bb, g * P:(g + 1) * P], s[:, g, kt * P:(kt + 1) * P], ident), g == 3)
                dst = M[:, PT + (i % 2) * 1024 + kt * 512:PT + (i % 2) * 1024 + (kt + 1) * 512]
                over = att_free[("p", i % 2)]
                fn = lambda e, dst=dst, bb=bb: e.tensor_copy(dst, PS[:, bb, :])
                fa = lambda e, dst=dst, bb=bb: e.copy(dst, PS[:, bb, :])
                ev.append(act([done, over], fa) if kt == 0 else dve([done, over], fn))
                free[bb] = [ev[-1]]
            att_free[("s", i % 2)] = [done]
            st[i] = (KT, ev)

        o_ready = {}

        def attend(i):
            n, kv = units[i]
            KT, ev = st[i]
            pp = slice(kv * 64, kv * 64 + 64)
            for kt in range(KT):
                tt = n - (KT - 1) + kt
                done = pe([ev[kt], v_ready, free[6] if kt == 0 else []], lambda e, kt=kt, tt=tt: e.matmul(
                    PS[pp, 6, :], M[:, VA + tt * P + kv * 64:VA + tt * P + kv * 64 + 64],
                    M[:, PT + (i % 2) * 1024 + kt * 512:PT + (i % 2) * 1024 + (kt + 1) * 512],
                    start=kt == 0, stop=kt == KT - 1), kt == KT - 1)
            att_free[("p", i % 2)] = [done]
            src = PS[pp, 6, :].rearrange("p (g t) -> p g t", g=4)
            dst = M[pp, OA:OA + 2048].rearrange("p (g t) -> p g t", g=4)[:, :, n * P:(n + 1) * P]
            d = dve([done, pro, turned], lambda e: e.tensor_copy(dst, src))
            free[6] = [d]
            o_ready[(n, kv)] = d

        for i in range(10):
            if i < 8:
                scores(i)
                lru_projection(i)
            if 0 <= i - 1 < 8:
                turn_weights(i - 1)
            if 0 <= i - 2 < 8:
                attend(i - 2)
        all_o = list(o_ready.values())

        def y_part(src, waits, c0, b):
            s = mean_square(src, waits, L, one512, b)
            r = rstd(b, L, 0, s, RMS_EPS)
            out = []
            for c in range(4):
                d = dve([r, waits[c]], lambda e, c=c: e.scalar_tensor_tensor(
                    out=src[c], in0=src[c], scalar=par("g_mix", c0 + c), in1=rs_view(L), op0=ALU.mult, op1=ALU.mult))
                reads_rs("dve", 0, L, d)
                k = c0 + c
                out.append(split(HID[:, k * 512:(k + 1) * 512], HID[:, 4096 + k * 512:4096 + (k + 1) * 512],
                                 src[c], d, state["hid_over"]))
            return out

        y_att = y_part([M[:, OA + c * 512:OA + (c + 1) * 512] for c in range(4)], [all_o] * 4, 4, 6)

        att_done = [all_o, q_ready[4]]
        XCc = lambda c: M[:, XC + c * 512:XC + (c + 1) * 512]
        Ac = lambda c: M[:, AA + c * 512:AA + (c + 1) * 512]
        Uc = lambda c: M[:, UA + c * 512:UA + (c + 1) * 512]
        cw = lambda j, c: par("conv_w", j * 4 + c)
        xc_ready, h_done = {}, {}
        for c in range(4):
            t = dve([xl_ready[c], pad[c], att_done], lambda e, c=c: e.tensor_scalar(
                XCc(c), XLc(c, 0, 512), cw(0, c), par("conv_b", c), ALU.mult, ALU.add))
            for j in range(1, 4):
                t = dve([t], lambda e, c=c, j=j: e.scalar_tensor_tensor(
                    out=XCc(c), in0=XLc(c, j, 512), scalar=cw(j, c), in1=XCc(c), op0=ALU.mult, op1=ALU.add))
            xc_ready[c] = t
        r_ready, i_ready = {}, {}
        for c in range(4):
            for gi, (dst, bias, reg) in enumerate(((Ac, "b_rg", r_ready), (Uc, "b_ig", i_ready))):
                b = bank()
                mm = pe([xc_ready[c], bd_ready, free[b]], lambda e, c=c, gi=gi, b=b: e.matmul(
                    PS[:, b, :], M[:, BD + gi * 512 + c * P:BD + gi * 512 + (c + 1) * P], XCc(c), start=True, stop=True))
                reg[c] = act([mm, att_done], lambda e, c=c, b=b, dst=dst, bias=bias: e.activation(
                    dst(c), PS[:, b, :], ACT.Sigmoid, bias=par(bias, c)))
                free[b] = [reg[c]]
        for c in range(4):
            la = dve([r_ready[c], cls_ready], lambda e, c=c: e.tensor_scalar(Ac(c), Ac(c), cls[:, c:c + 1], None, ALU.mult))
            th, key = tmp("a", L)
            a1 = act([la, rfree[key]], lambda e, c=c, th=th: e.activation(th, Ac(c), ACT.Tanh))
            a2 = act([la, a1], lambda e, c=c: e.activation(Ac(c), Ac(c), ACT.Exp))
            sq, key2 = tmp("b", L)
            t = dve([a2, rfree[key2]], lambda e, c=c, sq=sq: e.tensor_tensor(sq, Ac(c), Ac(c), ALU.mult))
            t = dve([t, a1], lambda e, c=c, sq=sq, th=th: e.scalar_tensor_tensor(
                out=sq, in0=sq, scalar=1.0, in1=th, op0=ALU.add, op1=ALU.mult))
            rfree[key] = [t]
            t = dve([t], lambda e, sq=sq: e.tensor_scalar(sq, sq, -1.0, 0.0, ALU.mult, ALU.max))
            t = act([t], lambda e, sq=sq: e.activation(sq, sq, ACT.Sqrt))
            t2 = dve([i_ready[c]], lambda e, c=c: e.tensor_tensor(Uc(c), Uc(c), XCc(c), ALU.mult))
            t = dve([t, t2], lambda e, c=c, sq=sq: e.tensor_tensor(Uc(c), Uc(c), sq, ALU.mult))
            rfree[key2] = [t]
            t = dve([t, a2], lambda e, c=c: e.tensor_tensor_scan(XLc(c, 0, 512), Ac(c), Uc(c), 0.0, ALU.mult, ALU.add))
            h_done[c] = dve([t, g_ready[c]], lambda e, c=c: e.tensor_tensor(Gc(c), XLc(c, 0, 512), Gc(c), ALU.mult))
        y_lru = y_part([Gc(c) for c in range(4)], [h_done[c] for c in range(4)], 0, bank())

        y_ready = y_lru + y_att
        F = lambda j: M[:, j * 512:(j + 1) * 512]
        f_tok = {}
        state["acc_over"] = [y_lru]
        chain = lambda s: norm_chain(s, F, f_tok, "mix_post_g", to_rms("ffn2_pre_g"))

        def o_post(j):
            def post(b, t0, n, done):
                f, s = F(j)[:, t0:t0 + n], t0 // 256
                f_tok[(j, s)] = act([done, y_lru], lambda e: e.copy(f, PS[:, b, 0:n]))
                summed(s, j, f, f_tok[(j, s)], True, chain)
                return [f_tok[(j, s)]]
            return post

        yacts = lambda half, k, t0, n: HID[:, half * 4096 + k * 512 + t0:half * 4096 + k * 512 + t0 + n]
        last = columns([(dram["w_o"][j], (SLOT,), DC, yacts, lambda k, t0, n: y_ready[k], [(0, o_post(j))])
                        for j in range(DC)], SUB1, batch=4)
        state["hid_over"] = [last]
        state["misc_over"] = [y_ready]

    def retention():
        QK, OC, VV, PA, ST, DI, CS, GG = 0, 3072, 4096, 7168, 8192, 9728, 10880, 11904
        pro = [state["misc_over"]]
        dist_ready = load(pro, M[:, DI:DI + 1152], dram["dist"], sems["misc"])
        cs_ready = load(pro, M[:, CS:CS + 1024], dram["rope"], sems["misc"])
        dist_ready = cs_ready
        hw = lambda k, t0, n: cover(h_ready, k, t0, n)
        sm = lambda o, n: TMP[:, 2816 + o:2816 + o + n]
        dec = PAR[:, POFF["decay"]:POFF["decay"] + 8]
        eg, lg, nlb = sm(0, 8), sm(8, 8), sm(16, 8)
        t = act([pro, par_ready], lambda e: e.activation(eg, dec, ACT.Exp))
        t = dve([t], lambda e: e.tensor_scalar(lg, eg, -1.0, None, ALU.mult))
        lg_ready = dve([t], lambda e: e.tensor_scalar(nlb, eg, 768.0, -1.0, ALU.mult, ALU.mult))
        cos, sin = M[:, CS:CS + 512], M[:, CS + 512:CS + 1024]
        qk = lambda w, k, t0, n: M[:, QK + (w * 2 + k) * 768 + t0:QK + (w * 2 + k) * 768 + t0 + n]
        ov = {"qk": pro, "v": pro, "oc": pro, "p": [[], []], "st": pro, "g": pro, "ol": pro}
        def decays(h):
            d_ = M[:, DI:DI + 1152]
            LL, GS = M[:, ST:ST + 896], M[:, ST + 896:ST + 1536]
            tA, tB = M[:, PA:PA + 896], TMP[:, 1024:1920]
            t1 = dve([dist_ready, lg_ready, ov["st"], *ov["p"][0], *ov["p"][1]], lambda e, h=h: e.tensor_scalar(
                tA, d_[:, 0:896], 0.0, lg[:, h:h + 1], ALU.max, ALU.mult))
            t2 = dve([ov["st"], rfree[both("b")]], lambda e, h=h: e.tensor_scalar(
                tB, d_[:, 0:896], 0.0, eg[:, 4 + h:5 + h], ALU.min, ALU.mult))
            t3 = dve([t1, t2], lambda e: e.tensor_tensor(tA, tA, tB, ALU.add))
            t4 = act([t3, ov["st"]], lambda e: e.activation(LL, tA, ACT.Exp))
            ll_ready = dve([t4], lambda e: e.tensor_tensor(LL[:, 384:512], LL[:, 384:512], ident, ALU.add))
            t5 = act([lg_ready, ov["st"]], lambda e, h=h: e.activation(GS, d_[:, 512:1152], ACT.Exp, scale=lg[:, h:h + 1]))
            t6 = act([t3, lg_ready], lambda e, h=h: e.activation(tB[:, 0:640], d_[:, 512:1152], ACT.Exp,
                                                             scale=eg[:, 4 + h:5 + h], bias=nlb[:, 4 + h:5 + h]))
            gs_ready = dve([t5, t6], lambda e: e.tensor_tensor(GS, GS, tB[:, 0:640], ALU.add))
            rfree[both("b")] = [gs_ready]
            ov["p"] = [[t4], [t4]]
            return ll_ready, gs_ready

        def v_rows(h):
            return token_rows([dram["ret_v"][h, blk] for blk in range(4)], h_ready, ov["v"],
                              lambda tt: M[:, VV + tt * 512:VV + (tt + 1) * 512])[0]

        ahead = v_rows(0)
        ov["qk"] = ov["oc"] = [state["misc_over"]]
        for h in range(4):
            v_ready = ahead
            LL, GS = M[:, ST:ST + 896], M[:, ST + 896:ST + 1536]
            qk_ready = {}
            for w in range(2):
                halves = {}

                def qk_post(b, t0, n, done, w=w, halves=halves):
                    k = halves["k"]
                    if t0 == 512:
                        a = act([done, ov["qk"]], lambda e, k=k: e.copy(qk(w, k, 512, 256), PS[:, b, 0:256]))
                        qk_ready[(w, k, 512)] = a
                        return [a]
                    if k == 0:
                        halves["b"], halves["done"] = b, done
                        return [done]
                    b0, d0_ = halves["b"], halves["done"]
                    for half in range(2):
                        (u, ku), (v, kv_) = tmp("b", 512), tmp("b", 512)
                        s1, s2 = (cos, sin) if half == 0 else (sin, cos)
                        x1 = dve([d0_, rfree[ku], cs_ready], lambda e, u=u, s1=s1: e.tensor_tensor(u, PS[:, b0, :], s1, ALU.mult))
                        x2 = dve([done, rfree[kv_]], lambda e, v=v, s2=s2: e.tensor_tensor(v, PS[:, b, :], s2, ALU.mult))
                        op = ALU.subtract if half == 0 else ALU.add
                        x3 = dve([x1, x2, ov["qk"]], lambda e, u=u, v=v, op=op, half=half: e.tensor_tensor(
                            qk(w, half, 0, 512), u, v, op))
                        rfree[ku] = rfree[kv_] = [x3]
                        qk_ready[(w, half, 0)] = x3
                    free[b0] = [x2]
                    return [x2]

                for k in range(2):
                    halves["k"] = k
                    columns([(dram["ret_qk"][w * 8 + h * 2 + k], (SLOT,), DC, hacts, hw, [(0, qk_post)])], SEG2)

            if h == 0:
                weighted = decays(0)
            ll_ready, gs_ready = weighted

            g_ready = {}

            def g_post(b, t0, n, done, c):
                dst = M[:, GG + c * 768 + t0:GG + c * 768 + t0 + n]
                g_ready[(c, t0)] = act([done, ov["g"]], lambda e: e.activation(dst, PS[:, b, 0:n], ACT.Silu))
                return [g_ready[(c, t0)]]

            last_h = columns([(dram["ret_g"][h * 4 + c], (SLOT,), DC, hacts, hw,
                               [(0, lambda b, t0, n, d, c=c: g_post(b, t0, n, d, c))]) for c in range(4)], SEG2)
            state["h_over"] = [last_h]

            y_ready = {}
            o_tok = {}
            finish = None
            for t0, n, tiles in ((512, 256, (4, 5)), (0, 512, (0, 1, 2, 3, 4, 5))):
                weights = {}

                def score(i, t0=t0, n=n, tiles=tiles, weights=weights):
                    kt = tiles[i]
                    b = (4, 5)[i % 2]
                    kseg = 0 if kt < 4 else 512
                    for k in range(2):
                        done = pe([qk_ready[(0, k, t0)], qk_ready[(1, k, kseg)], free[b] if k == 0 else []],
                                  lambda e, k=k, b=b, kt=kt: e.matmul(PS[:, b, 0:n], qk(1, k, kt * P, P), qk(0, k, t0, n),
                                                                      start=k == 0, stop=k == 1), k == 1)
                    if t0 == 0 and kt < 4:
                        dd, dr = LL[:, 384 - 128 * kt:384 - 128 * kt + 512], ll_ready
                    elif t0 == 0:
                        dd, dr = GS[:, 128 - 128 * (kt - 4):128 - 128 * (kt - 4) + 512], gs_ready
                    else:
                        dd, dr = LL[:, 384 - 128 * (kt - 4):384 - 128 * (kt - 4) + 256], ll_ready
                    pw = M[:, PA + (i % 2) * 512:PA + (i % 2) * 512 + n]
                    d = dve([done, dr, ov["p"][i % 2]], lambda e, b=b: e.scalar_tensor_tensor(
                        out=pw, in0=PS[:, b, 0:n], scalar=0.0625, in1=dd, op0=ALU.mult, op1=ALU.mult))
                    free[b] = [d]
                    weights[i] = (pw, d)
                    ov["last_score"] = done

                def value(i, t0=t0, n=n, tiles=tiles, weights=weights):
                    pw, d = weights[i]
                    kt = tiles[i]
                    for c in range(4):
                        done = pe([d, v_ready[kt], free[c] if i == 0 else []], lambda e, c=c, kt=kt: e.matmul(
                            PS[:, c, 0:n], M[:, VV + kt * 512 + c * P:VV + kt * 512 + (c + 1) * P], pw,
                            start=i == 0, stop=i == len(tiles) - 1), c == 3 or i == len(tiles) - 1)
                        o_tok[(c, t0)] = done
                    ov["p"][i % 2] = [done]

                for i in range(len(tiles) + 1):
                    if i < len(tiles):
                        score(i)
                    if i >= 1:
                        value(i - 1)
                    if i == 3 and finish:
                        finish()
                src = []
                wt = []
                for c in range(4):
                    if t0 == 512:
                        dst = M[:, OC + c * 256:OC + (c + 1) * 256]
                        over = ov["oc"]
                    else:
                        dst = M[:, QK + c * 512:QK + (c + 1) * 512]
                        over = [ov["last_score"]]
                    a = act([o_tok[(c, t0)], over], lambda e, dst=dst, c=c, n=n: e.copy(dst, PS[:, c, 0:n]))
                    free[c] = [a]
                    src.append(dst)
                    wt.append(a)

                def finish(t0=t0, n=n, src=src, wt=wt):
                    bb = 6 if t0 == 0 else 7
                    s = mean_square(src, wt, n, one512, bb)
                    r = rstd(bb, n, t0, s, RMS_EPS)
                    halves_of = lambda c: (HID[:, c * 768 + t0:c * 768 + t0 + n], HID[:, 4096 + c * 768 + t0:4096 + c * 768 + t0 + n])
                    for c in range(5):
                        if c >= 1:
                            (hi, lo), gv1, a1 = halves_of(c - 1), M[:, GG + (c - 1) * 768 + t0:GG + (c - 1) * 768 + t0 + n], y_hi
                        if c == 4:
                            y_ready[(3, t0)] = [a1, dve([a1, x2], lambda e, lo=lo, hi=hi, gv1=gv1: e.tensor_tensor(lo, gv1, hi, ALU.subtract))]
                            break
                        gv = M[:, GG + c * 768 + t0:GG + c * 768 + t0 + n]
                        o, rs = src[c], rs_view(n, t0)
                        x1 = dve([r, wt[c]], lambda e, o=o, rs=rs: e.tensor_tensor(o, o, rs, ALU.mult))
                        reads_rs("dve", t0, n, x1)
                        x2 = dve([x1, g_ready[(c, t0)]], lambda e, o=o, gv=gv: e.tensor_tensor(gv, o, gv, ALU.mult))
                        if c >= 1:
                            y_ready[(c - 1, t0)] = [a1, dve([a1, state["hid_over"]], lambda e, lo=lo, hi=hi, gv1=gv1: e.tensor_tensor(
                                lo, gv1, hi, ALU.subtract))]
                        y_hi = act([x2, state["hid_over"]], lambda e, h_=halves_of(c)[0], gv=gv: e.copy(h_, gv))
                        if t0 == 0:
                            ov["qk"] = [x2]
                        else:
                            ov["oc"] = [x2]

            ov["v"] = [o_tok[(3, 0)]]
            ov["st"] = [ov["last_score"], free[5], free[4]]
            finish()
            if h < 3:
                weighted = decays(h + 1)
                ahead = v_rows(h + 1)
            ov["g"] = [y_ready[k] for k in y_ready]

            yacts = lambda half, k, t0, n: HID[:, half * 4096 + k * 768 + t0:half * 4096 + k * 768 + t0 + n]
            state["acc_over"] = [ov["g"]]
            post = gated(0, 2, 3, lambda s: layer_norm_chain(s, 0, 0, after_ln(0, 0, 3)))
            outs = lambda j2: [(jj * 512, lambda b, t0, n, d, j=j2 * 2 + jj, h=h: post(h, j, b, t0, n, d)) for jj in range(2)]
            done = columns([(dram["ret_o"][j2 * 2:j2 * 2 + 2, :, h * 512:(h + 1) * 512].rearrange("a p n -> p a n"), (2, 512), 4,
                             yacts, lambda k, t0, n: y_ready[(k, 0 if t0 < 512 else 512)], outs(j2)) for j2 in range(4)],
                           SUB2 if h == 3 else SEG2, batch=4 if h == 3 else 1)
            state["hid_over"] = [done]
        state["misc_over"] = [ov["g"], ov["v"], ov["qk"], ov["st"], ov["oc"]]

    def neighbourhood():
        QA, KA, VV, SA, PT, BM, SM = 0, 2048, 5120, 9728, 10752, 11776, 14900
        pro = [state["misc_over"]]
        STRIP, MSK = BM + 1536, BM + 1536 + 384
        hw = lambda k, t0, n: cover(h_ready, k, t0, n)
        sm = lambda o, n: M[:, SM + o:SM + o + n]
        bm3 = M[:, BM:BM + 1536].rearrange("p (y k) -> p y k", y=3)
        msk_ready = None
        ov = {"q": pro, "k": pro, "v": pro, "s": [pro, pro, rfree[both("a")]], "p": [pro, pro], "bm": [], "strip": []}
        wbuf = (M[:, SA:SA + 512], M[:, SA + 512:SA + 1024], TMP[:, 0:512])
        band0 = (0, 64, 192, 256)
        kind = (0, 1, 1, 2)
        off = (16, 8, 0)
        starts = {0: 0, 128: 1, 256: 2, 384: 3, 64: 4, 192: 5, 320: 6}
        y_over = []

        for half in range(2):
            q_ready, k_ready = {}, {}

            def q_post(b, t0, n, done, c):
                q_ready[c] = act([done, ov["q"]], lambda e: e.mul(M[:, QA + c * 512:QA + (c + 1) * 512], PS[:, b, :], 0.125))
                return [q_ready[c]]

            def k_post(b, t0, n, done, c):
                dst = M[:, KA + c * 768 + t0:KA + c * 768 + t0 + n]
                k_ready[(c, t0)] = act([done, ov["k"]], lambda e: e.copy(dst, PS[:, b, 0:n]))
                return [k_ready[(c, t0)]]

            vslot = lambda tt: tt if tt < 4 else tt + 3
            VC = lambda s_: M[:, VV + s_ * 512:VV + (s_ + 1) * 512]
            got, _ = token_rows([dram["na_v"][half, blk] for blk in range(4)], h_ready, ov["v"], lambda tt: VC(vslot(tt)))
            v_ready = {vslot(tt): tok for tt, tok in got.items()}
            if half == 0:
                late = [pro, state["joined"]]
                msk_ready = load(late, M[:, MSK:MSK + 768], dram["mask2"], sems["misc"])
                ov["bm"] = [pool(late, lambda e: e.memset(M[:, BM:BM + 1536], 0.0))]
                ov["strip"] = late
            for i, s_ in enumerate((4, 5, 6)):
                load([v_ready[i], v_ready[i + 1], ov["v"]], M[0:64, VV + s_ * 512:VV + (s_ + 1) * 512],
                     M[64:128, VV + i * 512:VV + (i + 1) * 512], sems["vs"])
                v_ready[s_] = load([v_ready[i + 1]], M[64:128, VV + s_ * 512:VV + (s_ + 1) * 512],
                                   M[0:64, VV + (i + 1) * 512:VV + (i + 2) * 512], sems["vs"])
            for s_ in (4, 5):
                v_ready[s_] = v_ready[6]

            def q_and_k(c):
                columns([(dram["na_qk"][half * 4 + c], (SLOT,), DC, hacts, hw,
                          [(0, lambda b, t0, n, d: q_post(b, t0, n, d, c))])], SEG1, banks=(5, 6, 7))
                last_h = columns([(dram["na_qk"][8 + half * 4 + c], (SLOT,), DC, hacts, hw,
                                   [(0, lambda b, t0, n, d: k_post(b, t0, n, d, c))])], SEG2, banks=(5, 6, 7))
                state["h_over"] = [last_h]

            st = {}
            units = [(hh, b) for hh in range(8) for b in range(4)]

            def bias(hh):
                s = load([ov["strip"]], M[:, STRIP:STRIP + 384], dram["rpb"][half * 8 + hh], sems["strip"])
                last = None
                for y in range(3):
                    last = pool([s, msk_ready, ov["bm"]], lambda e, y=y: e.tensor_tensor(
                        bm3[:, y, 0:256], M[:, STRIP + off[y] * 8:STRIP + off[y] * 8 + 256],
                        M[:, MSK + y * 256:MSK + (y + 1) * 256], ALU.add))
                ov["strip"] = [last]
                return last

            bm_ready = {}

            def scores(i):
                hh, b = units[i]
                if b == 0:
                    bm_ready[hh] = bias(hh)
                c, pp = hh // 2, slice((hh % 2) * 64, (hh % 2) * 64 + 64)
                bb = (0, 1)[i % 2]
                pe([q_ready[c], k_ready[(c, 0)], free[bb]], lambda e: e.matmul(
                    PS[:, bb, 0:256], M[pp, QA + c * 512 + b * P:QA + c * 512 + (b + 1) * P],
                    M[pp, KA + c * 768 + band0[b]:KA + c * 768 + band0[b] + 256], start=True, stop=True,
                    skip_group_check=True), False)
                done = pe([k_ready[(c, 512)]], lambda e: e.matmul(
                    PS[:, bb, 256:512], M[pp, QA + c * 512 + b * P:QA + c * 512 + (b + 1) * P],
                    M[pp, KA + c * 768 + 512:KA + c * 768 + 768], start=True, stop=True, skip_group_check=True))
                o = (i % 3) * 8
                mx, nm, su, rc = (sm(o + j, 1) for j in range(4))
                s = wbuf[i % 3]
                d = dve([done, bm_ready[hh], ov["s"][i % 3]], lambda e: e.tensor_tensor_reduce(
                    s, PS[:, bb, :], bm3[:, kind[b], :], 1.0, -3.0e38, ALU.add, ALU.max, mx))
                free[bb] = [d]
                if b == 3:
                    ov["bm"] = [d]
                d2 = dve([d], lambda e: e.tensor_scalar(nm, mx, -1.0, None, ALU.mult))
                a = act([d2], lambda e: e.activation(s, s, ACT.Exp, bias=nm, accum_out=su))
                d3 = dve([a], lambda e: e.reciprocal(rc, su))
                d4 = dve([d3], lambda e: e.tensor_scalar(s, s, rc, None, ALU.mult))
                st[i] = (s, d4)
                ov["last_score"] = done

            def turn_weights(i):
                s, d4 = st[i]
                bb = (2, 3)[i % 2]
                for kt in range(4):
                    done = pe([d4, free[bb] if kt == 0 else []], lambda e, kt=kt: e.transpose(
                        PS[:, bb, kt * P:(kt + 1) * P], s[:, kt * P:(kt + 1) * P], ident), kt == 3)
                ov["s"][i % 3] = [done]
                dst = M[:, PT + (i % 2) * 512:PT + (i % 2) * 512 + 512]
                a = act([done, ov["p"][i % 2]], lambda e: e.copy(dst, PS[:, bb, :]))
                free[bb] = [a]
                st[i] = (dst, a)

            def attend(i):
                hh, b = units[i]
                dst, a = st[i]
                r0 = (hh % 2) * 64
                ob = (4, 5)[(hh // 2) % 2]
                tiles = [starts[band0[b]], starts[band0[b] + 128], 7, 8]
                for kt in range(4):
                    vs = M[:, VV + tiles[kt] * 512 + hh * 64:VV + tiles[kt] * 512 + hh * 64 + 64]
                    done = pe([a, v_ready[tiles[kt]], free[ob] if b == 0 and kt == 0 and hh % 2 == 0 else []],
                              lambda e, kt=kt, vs=vs: e.matmul(PS[r0:r0 + 64, ob, b * P:(b + 1) * P], vs,
                                                               dst[:, kt * P:(kt + 1) * P], start=kt == 0, stop=kt == 3,
                                                               skip_group_check=True), kt == 3)
                ov["p"][i % 2] = [done]
                if b == 3 and hh % 2 == 1:
                    k = half * 4 + hh // 2
                    hi, lo = HID[:, k * 512:(k + 1) * 512], HID[:, 4096 + k * 512:4096 + (k + 1) * 512]
                    x1 = act([done, state["hid_over"]], lambda e: e.copy(hi, PS[:, ob, :]))
                    x2 = dve([x1, done], lambda e: e.tensor_tensor(lo, PS[:, ob, :], hi, ALU.subtract))
                    free[ob] = [x2]
                    y_over.append([x1, x2])
                ov["last"] = done

            for i in range(len(units) + 3):
                if i < 4:
                    q_and_k(i)
                if i < len(units):
                    scores(i)
                if 0 <= i - 2 < len(units):
                    turn_weights(i - 2)
                if i - 3 >= 0:
                    attend(i - 3)
            rfree[both("a")] = ov["s"][2]
            ov["q"] = ov["k"] = [ov["last_score"]]
            ov["v"] = [ov["last"]]

        old, x_old = home["buf"], dict(xt)
        home["buf"], home["pitch"] = M, 512
        state["acc_over"] = [ov["bm"], ov["strip"], msk_ready]
        chain = lambda s: layer_norm_chain(s, 1, 0, after_ln(2, 1, 3))

        def o_post(j):
            def post(b, t0, n, done):
                s = t0 // 256
                x = xs(j, t0, n)
                from_ = old[:, j * 768:j * 768 + 512].rearrange("p (r c) -> p c r", c=64)[:, 32 * s:32 * s + 32, :]
                xt[(j, s)] = dve([done, x_old[(j, 0)], x_old[(j, 1)], ov["q"]], lambda e: e.scalar_tensor_tensor(
                    out=x.rearrange("p (c r) -> p c r", r=8), in0=PS[:, b, 0:n].rearrange("p (c r) -> p c r", r=8),
                    scalar=mod(1, 0, 2, j), in1=from_, op0=ALU.mult, op1=ALU.add))
                summed(s, j, x, xt[(j, s)], False, chain)
                return [xt[(j, s)]]
            return post

        yacts = lambda half, k, t0, n: HID[:, half * 4096 + k * 512 + t0:half * 4096 + k * 512 + t0 + n]
        last = columns([(dram["na_o"][j], (SLOT,), DC, yacts, lambda k, t0, n: y_over[k], [(0, o_post(j))])
                        for j in range(DC)], SUB1, batch=4)
        state["hid_over"] = [last]

    q.stage("ffn1")
    for _ in range(4):
        ada_step()
    for s in range(2):
        for c in range(DC):
            to_rms("ffn1_pre_g")(c, s)
    first_ffn("ffn1_post_g", dram["gu1"], dram["dn1"], to_rms("mix_pre_g"), ada_step)
    q.stage("mix1")
    first_mixer()
    q.stage("ffn2")
    ada["limit"] = 96
    context = iter(range(DC))

    def ada_or_context():
        if ada["n"] < 96 or ada["rows"]:
            ada_step()
            return
        c = next(context, None)
        if c is not None:
            xt[(c, 2)] = load([ada["row_read"]], xs(c, 512, 256), dram["ctx"][c], sems["x"][c])
            to_modulated(0, 0)(c, 2)

    first_ffn("ffn2_post_g", dram["gu2"], dram["dn2"], to_modulated(0, 0), ada_or_context)

    q.stage("ret")
    retention()
    q.stage("ffn3")
    ffn(dram["gu3"], dram["dn3"], PARTS2, SEG2, SUB2,
        gated(0, 5, 4, lambda s: layer_norm_chain(s, 0, 1, after_ln(1, 1, 0, True))), False)
    force(0, 512)
    for c in range(DC):
        h_ready[(c, 0)] = h_ready[(c, 1)] = [h_ready[(c, 0)], h_ready[(c, 1)]]
    q.stage("na")
    neighbourhood()
    q.stage("ffn4")

    def store(c, s, t, d):
        x = xs(c, s * 256, 256)
        lb = PAR[:, POFF["ln_b"] + 24 + c:POFF["ln_b"] + 25 + c]
        a = act([d], lambda e: e.activation(x, t, ACT.Identity, bias=lb))
        stores.append(load([a], dram["out"][c][:, s * 256:(s + 1) * 256], x, sems["out"]))
        return [a]

    stores = []
    ffn(dram["gu4"], dram["dn4"], PARTS1, SEG1, SUB1,
        gated(1, 5, 2, lambda s: layer_norm_chain(s, 1, 1, store)), False)
    force(0, 512)
    q.wait("sp", stores[-1])


def build_program(nc, ins, out):
    with ExitStack() as ctx:
        def sb(name, shape, dt):
            return ctx.enter_context(nc.sbuf_tensor("t_" + name, shape, dt))

        mem = {
            "X": sb("x", [P, 6144], F32), "H": sb("h", [P, 12288], F32R), "HID": sb("hid", [P, 8192], F32R),
            "WHI": sb("whi", [P, NH, SLOT], F32R), "WLO": sb("wlo", [P, NH, SLOT], F32R),
            "RAW": sb("raw", [P, NR, SLOT], F32), "MISC": sb("misc", [P, 14976], F32),
            "TMP": sb("tmp", [P, 2840], F32), "PAR": sb("par", [P, NPAR], F32), "CON": sb("con", [P, 388], F32),
            "MOD": sb("mod", [P, 264], F32), "PS": ctx.enter_context(nc.psum_tensor("ps", [P, 8, 512], F32)),
        }
        sem = lambda name: ctx.enter_context(nc.semaphore(name))
        sems = {
            "ring": [sem(f"d_ring{i}") for i in range(NR)], "par": sem("d_par"),
            "x": [sem(f"d_x{i}") for i in range(DC)], "misc": sem("d_misc"), "strip": sem("d_strip"), "vs": sem("d_vs"), "out": sem("d_out"),
        }
        dram = dict(ins)
        dram["out"] = out
        plan = []
        dry = Engines(lambda name: object())
        queue_program(dry, mem, dram, sems, None, plan)
        q = Engines(sem)
        queue_program(q, mem, dram, sems, plan, [])
        block = ctx.enter_context(nc.Block())

        @block.sync
        def _(e):
            q.replay("sp", e)

        @block.tensor
        def _(e):
            q.replay("pe", e)

        @block.scalar
        def _(e):
            q.replay("act", e)

        @block.vector
        def _(e):
            q.replay("dve", e)

        @block.gpsimd
        def _(e):
            q.replay("pool", e)


def stationary(w):
    k, n = w.shape
    return np.ascontiguousarray(w.reshape(k // P, P, n // P, P).transpose(2, 1, 0, 3)).reshape(n // P, P, k)


def moving(w):
    n = w.shape[1]
    return np.ascontiguousarray(w.reshape(4, 2, P, n // 512, 512).transpose(3, 0, 2, 1, 4)).reshape(n // 512, 4, P, 1024)


def cols(v):
    return np.asarray(v).reshape(-1, P).T


def lay_out(i):
    g = {k: np.asarray(v) for k, v in i.items()}
    heads = np.array(HEAD_ORDER)
    w_in = g["w_in"][0]
    qw = w_in[:, 1024:1536].reshape(D, 8, 64)[:, heads].reshape(D, 512)
    w_in = np.concatenate([w_in[:, :1024], qw, w_in[:, 1536:]], 1)
    w_o = g["w_o"][0]
    w_o = np.concatenate([w_o[:512], w_o[512:].reshape(8, 64, D)[heads].reshape(512, D)], 0)
    g_att = g["g_attn_out"][0].reshape(8, 64)[heads].reshape(512)
    par = {
        "ffn1_pre_g": cols(g["ffn1_pre_g"]), "ffn1_post_g": cols(g["ffn1_post_g"]), "mix_pre_g": cols(g["mix_pre_g"]),
        "conv_w": cols(g["conv_w"]), "conv_b": cols(g["conv_b"]), "b_rg": cols(g["b_rg"]), "b_ig": cols(g["b_ig"]),
        "lam": cols(g["lru_lambda"]), "g_mix": np.concatenate([cols(g["g_lru_out"]), cols(g_att)], 1),
        "mix_post_g": cols(g["mix_post_g"]), "ffn2_pre_g": cols(g["ffn2_pre_g"]), "ffn2_post_g": cols(g["ffn2_post_g"]),
        "cond": np.stack([cols(g["c_2"]), cols(g["c_ctx_2"])], 2).reshape(P, 16),
        "ada_b": cols(g["ada_b_2"]), "ln_g": cols(g["ln_g_2"]), "ln_b": cols(g["ln_b_2"]),
        "sinks": np.broadcast_to(g["sinks"][0], (P, 8)), "decay": np.broadcast_to(g["ret_decay_2"].reshape(8), (P, 8)),
    }
    a = {"params": np.ascontiguousarray(np.concatenate([par[n] for n, _ in PARAMS], 1))}
    comb = np.zeros((P, 2), np.float32)
    comb[0, 0] = comb[2, 0] = comb[1, 1] = comb[3, 1] = 1
    a["consts"] = np.concatenate([np.eye(P, dtype=np.float32), np.full((P, P), 1 / 1024, np.float32),
                                  np.full((P, P), 1 / 512, np.float32), comb,
                                  np.full((P, 1), RMS_EPS, np.float32), np.full((P, 1), LN_EPS, np.float32)], 1)
    a["x"] = np.ascontiguousarray(g["x"][0].T).reshape(DC, P, L)
    a["ctx"] = np.ascontiguousarray(g["ctx_2"][0].T).reshape(DC, P, LC)
    a["gu1"], a["dn1"] = stationary(g["ffn1_w_gu"][0]), stationary(g["ffn1_w_down"][0])
    a["gu2"], a["dn2"] = stationary(g["ffn2_w_gu"][0]), stationary(g["ffn2_w_down"][0])
    a["gu3"], a["dn3"] = stationary(g["ffn_w13_2"][0]), stationary(g["ffn_w2_2"][0])
    a["gu4"], a["dn4"] = stationary(g["ffn_w13_2"][1]), stationary(g["ffn_w2_2"][1])
    a["w_in"], a["w_o"] = stationary(w_in), stationary(w_o)
    gates = np.zeros((P, 2, 4, P), np.float32)
    for n, name in enumerate(("w_rg", "w_ig")):
        for b in range(8):
            o = (b % 2) * 64
            gates[o:o + 64, n, b // 2, o:o + 64] = g[name][0, b]
    a["gates"] = gates.reshape(P, 1024)
    qi, kj = np.arange(P)[:, None], np.arange(2 * P)[None]
    rel = qi + P - kj
    a["mask1"] = np.where((rel >= 0) & (rel < 128), 0, NEG).astype(np.float32)
    a["ada"] = np.stack([moving(g["ada_w_2"][n]) for n in range(2)])
    rw = g["ret_w_in_2"]
    a["ret_qk"], a["ret_v"], a["ret_g"] = stationary(rw[:, :2048]), moving(rw[:, 2048:4096]), stationary(rw[:, 4096:])
    a["ret_o"] = stationary(g["ret_w_out_2"])
    a["dist"] = (np.arange(1152)[None] - 384 - np.arange(P)[:, None]).astype(np.float32)
    t = np.arange(L)
    inv = (np.float32(10000.0) ** (-np.arange(64, dtype=np.float32) / np.float32(64))).astype(np.float32)
    ang = np.concatenate([(t // 64).astype(np.float32)[:, None] * inv, (t % 64).astype(np.float32)[:, None] * inv], 1)
    a["rope"] = np.ascontiguousarray(np.concatenate([np.cos(ang).T, np.sin(ang).T], 1)).astype(np.float32)
    nw = g["na_w_qkv_2"]
    a["na_qk"], a["na_v"], a["na_o"] = stationary(nw[:, :2048]), moving(nw[:, 2048:]), stationary(g["na_w_out_2"])
    ci, r = np.arange(P)[:, None, None] // 8, np.arange(P)[:, None, None] % 8
    m, rr = np.arange(48)[None, :, None], np.arange(8)[None, None]
    a["rpb"] = np.ascontiguousarray(g["na_rpb_2"][:, rr - r + 7, np.clip(m - 16 - ci + 15, 0, 30)]).reshape(16, P, 384)
    masks = []
    for b in (0, 1, 3):
        band = min(max(16 * b - 8, 0), 32)
        q = 16 * b + np.arange(P)[:, None] // 8
        k = band + np.arange(256)[None] // 8
        ws = np.clip(q - 8, 0, 48)
        masks.append(np.where((k >= ws) & (k < ws + 16), 0, NEG).astype(np.float32))
    a["mask2"] = np.concatenate(masks, 1)
    return a


def kernel(**inputs):
    import concourse.bacc as bacc
    from concourse.bass_utils import run_bass_kernel_spmd

    nc = bacc.Bacc("TRN2", target_bir_lowering=False, num_devices=1, dynamic_dma_scratch_size=1024)
    arrays = lay_out(inputs)
    ins = {k: nc.dram_tensor("in_" + k, v.shape, F32, kind="ExternalInput").ap() for k, v in arrays.items()}
    out = nc.dram_tensor("out_x", (DC, P, L), F32, kind="ExternalOutput").ap()
    build_program(nc, ins, out)
    r = run_bass_kernel_spmd(nc, [{"in_" + k: v for k, v in arrays.items()}], core_ids=[0])
    y = np.asarray(r.results[0]["out_x"]).reshape(D, 64, 8)
    return np.ascontiguousarray(y.transpose(2, 1, 0)).reshape(1, L, D)
```

```python
import numpy as np
from contextlib import ExitStack

import concourse.bass as bass
from concourse import mybir

ALU = mybir.AluOpType
ACT = mybir.ActivationFunctionType
F32 = mybir.dt.float32
F32R = mybir.dt.float32r
AX_X = mybir.AxisListType.X

P = 128
L = 512
LC = 256
D = 1024
DC = D // P
FC = 2816 // P
SLOT = 1024
NR = 3
NH = 4
PARTS1 = (7, 7, 8)
PARTS2 = (4, 4, 4, 5, 5)
ALPHA = float((2 * 2) ** 0.25)
RMS_EPS = 1e-6
LN_EPS = 1e-5
NEG = -1e30
SEG1 = ((0, 512),)
SEG2 = ((0, 512), (512, 256))
ACC = 12560
GATE = 4608
BEHIND = [(0, 0, 0, 3), (0, 1, 0, 3), (1, 0, 1, 0), (1, 1, 1, 0), (1, 0, 2, 3)]
HEAD_ORDER = (0, 4, 1, 5, 2, 6, 3, 7)

PARAMS = [
    ("ffn1_pre_g", 8), ("ffn1_post_g", 8), ("mix_pre_g", 8), ("conv_w", 16), ("conv_b", 4),
    ("b_rg", 4), ("b_ig", 4), ("lam", 4), ("g_mix", 8), ("mix_post_g", 8),
    ("ffn2_pre_g", 8), ("ffn2_post_g", 8), ("cond", 16), ("ada_b", 96), ("ln_g", 32), ("ln_b", 32),
    ("sinks", 8), ("decay", 8),
]
POFF, _n = {}, 0
for _name, _w in PARAMS:
    POFF[_name] = _n
    _n += _w
NPAR = _n

CONSTS = [("ident", 128), ("one1024", 128), ("one512", 128), ("comb", 2), ("eps", 2)]


class Engines:

    def __init__(self, sem):
        self.sem = sem
        self.queues = {k: [] for k in ("pe", "act", "dve", "pool", "sp")}
        self.now = {}
        self.count = {}
        self.waited = {}

    def stage(self, name):
        for k in ("pe", "act", "dve", "pool"):
            self.now[k] = self.sem(f"s_{k}_{name}")

    def wait(self, eng, *tokens):
        for t in tokens:
            if t is None:
                continue
            if isinstance(t, list):
                self.wait(eng, *t)
                continue
            s, v = t
            if self.waited.get((eng, id(s)), 0) < v:
                self.waited[(eng, id(s))] = v
                self.queues[eng].append(lambda e, s=s, v=v: e.wait_ge(s, v))

    def op(self, eng, waits, fn, signal=True, sem=None, step=1):
        self.wait(eng, *waits)
        if not signal:
            self.queues[eng].append(fn)
            return None
        s = self.now[eng] if sem is None else sem
        self.count[id(s)] = self.count.get(id(s), 0) + step
        self.queues[eng].append(lambda e: fn(e).then_inc(s, step))
        return (s, self.count[id(s)])

    def replay(self, eng, e):
        for fn in self.queues[eng]:
            fn(e)


class Slots:

    def __init__(self):
        self.users = {}

    def __getitem__(self, keys):
        return [self.users.get(k) for k in keys]

    def __setitem__(self, keys, tokens):
        for k in keys:
            self.users[k] = tokens


def queue_program(q, mem, dram, sems, plan, seen):
    X, H, HID, WHI, WLO, RAW = mem["X"], mem["H"], mem["HID"], mem["WHI"], mem["WLO"], mem["RAW"]
    M, TMP, PAR, CON, MOD, PS = mem["MISC"], mem["TMP"], mem["PAR"], mem["CON"], mem["MOD"], mem["PS"]

    def pe(waits, fn, signal=True):
        return q.op("pe", waits, fn, signal)

    def act(waits, fn):
        return q.op("act", waits, fn)

    def dve(waits, fn):
        return q.op("dve", waits, fn)

    def pool(waits, fn):
        return q.op("pool", waits, fn)

    def load(waits, dst, src, sem):
        return q.op("sp", waits, lambda e: e.dma_start(dst, src), sem=sem, step=16)

    def par(name, c, p0=0, p1=P):
        return PAR[p0:p1, POFF[name] + c:POFF[name] + c + 1]

    ident = CON[:, 0:128]
    one1024 = CON[:, 128:256]
    one512 = CON[:, 256:384]
    comb = CON[0:4, 384:386]
    EPS = {RMS_EPS: CON[:, 386:387], LN_EPS: CON[:, 387:388]}

    free = {b: [] for b in range(8)}
    turn = {}

    def bank(some=(0, 1, 2, 3, 4, 5)):
        i = turn.get(some, 0)
        turn[some] = i + 1
        return some[i % len(some)]

    chains = {}

    def step(s):
        wait = next(chains[s][1], None)
        if wait is None:
            del chains[s]
        else:
            chains[s][0] = wait

    def tick():
        for s in sorted(chains):
            chains[s][0] -= 1
            if chains[s][0] <= 0:
                step(s)

    def force(t0, n):
        for s in range(t0 // 256, -(-(t0 + n) // 256)):
            while s in chains:
                step(s)

    def cover(d, k, t0, n):
        return [d[(k, s)] for s in range(t0 // 256, -(-(t0 + n) // 256))]

    ring = {"used": 0, "conv": 0, "dma": 0}
    dma_done, hi_done, lo_done, mm_done = {}, {}, {}, {}

    def issue_load(j):
        waits = [] if j < NR else [hi_done[j - NR], lo_done[j - NR]]
        src, shape = plan[j]
        dst = RAW[:, j % NR, 0:int(np.prod(shape))]
        if len(shape) == 2:
            dst = dst.rearrange("p (a b) -> p a b", a=shape[0])
        dma_done[j] = load(waits, dst, src, sems["ring"][j % NR])

    def issue_split(j):
        n = int(np.prod(plan[j][1]))
        over = [mm_done[j - NH]] if j >= NH else []
        raw, hi, lo = RAW[:, j % NR, 0:n], WHI[:, j % NH, 0:n], WLO[:, j % NH, 0:n]
        hi_done[j] = act([dma_done[j], *over], lambda e: e.copy(hi, raw))
        lo_done[j] = (pool if j % 2 else dve)([dma_done[j], hi_done[j], *over], lambda e: e.tensor_tensor(lo, raw, hi, ALU.subtract))

    def prepare(upto):
        while ring["conv"] < min(upto + 1, len(plan)) and (ring["conv"] < NH or ring["conv"] - NH in mm_done):
            k = ring["conv"]
            while ring["dma"] < min(k + NR, len(plan)):
                issue_load(ring["dma"])
                ring["dma"] += 1
            issue_split(k)
            ring["conv"] += 1

    def next_block(src, shape):
        j = ring["used"]
        ring["used"] += 1
        seen.append((src, shape))
        if plan is None:
            return j, j % NH, []
        prepare(j)
        return j, j % NH, [hi_done[j], lo_done[j]]

    def block_over(j, token):
        mm_done[j] = token
        if plan is not None:
            prepare(j + NH)

    def products(out, whi, wlo, xhi, xlo, waits, first, last, signal):
        pe(waits, lambda e: e.matmul(out, whi, xlo, start=first, stop=False), False)
        pe([], lambda e: e.matmul(out, wlo, xhi, start=False, stop=False), False)
        return pe([], lambda e: e.matmul(out, whi, xhi, start=False, stop=last), signal)

    home = {"buf": X, "pitch": 768}

    def xs(c, t0=0, n=L):
        return home["buf"][:, c * home["pitch"] + t0:c * home["pitch"] + t0 + n]

    def hs(part, c, t0, n):
        base = part * 6144 + c * 768 + t0
        return H[:, base:base + n]

    def hacts(part, k, t0, n):
        return hs(part, k, t0, n)

    def columns(specs, segs, batch=1, banks=None, between=None):
        done = None
        for i in range(0, len(specs), batch):
            some = specs[i:i + batch]
            held = [next_block(sp[0], sp[1]) for sp in some]
            for si, (t0, n) in enumerate(segs):
                for (_, _, nk, acts, deps, outs), (j, slot, ready) in zip(some, held):
                    for base, post in outs:
                        force(t0, n)
                        b = bank(banks) if banks else bank()
                        for k in range(nk):
                            o = base + k * P
                            done = products(PS[:, b, 0:n], WHI[:, slot, o:o + P], WLO[:, slot, o:o + P],
                                            acts(0, k, t0, n), acts(1, k, t0, n),
                                            [*ready, deps(k, t0, n), *(free[b] if k == 0 else [])],
                                            k == 0, k == nk - 1, k == nk - 1)
                        free[b] = []
                        free[b] = free[b] + post(b, t0, n, done)
                        tick()
                    if si == len(segs) - 1:
                        block_over(j, done)
            if between:
                for _ in some:
                    between()
        return done

    def token_rows(blocks, h_ready, over, dest):
        held = [next_block(src, (SLOT,)) for src in blocks]
        v_ready = {}
        done = None
        for tt in (4, 5, 0, 1, 2, 3):
            force(tt * P, P)
            b = bank()
            for k in range(DC):
                j, slot, ready = held[k // 2]
                w = slice((k % 2) * 512, (k % 2 + 1) * 512)
                done = products(PS[:, b, :], hs(0, k, tt * P, P), hs(1, k, tt * P, P), WHI[:, slot, w], WLO[:, slot, w],
                                [*ready, cover(h_ready, k, tt * P, P), *(free[b] if k == 0 else [])],
                                k == 0, k == 7, k == 7 or (tt == 3 and k % 2 == 1))
                if tt == 3 and k % 2 == 1:
                    block_over(j, done)
            dst = dest(tt)
            v_ready[tt] = act([done, over], lambda e, dst=dst, b=b: e.copy(dst, PS[:, b, :]))
            free[b] = [v_ready[tt]]
            tick()
        return v_ready, done

    ra = {"a": 0, "b": 0}
    rfree = Slots()

    def tmp(which, n):
        w = 1 if n <= 256 else 2
        i = -(-ra[which] // w) * w % 4
        ra[which] = i + w
        base = (0 if which == "a" else 1024) + i * 256
        return TMP[:, base:base + n], [(which, i + k) for k in range(w)]

    def both(which):
        return [(which, k) for k in range(4)]

    def rs_view(n, t0=0):
        return TMP[:, 2048 + t0:2048 + t0 + n]

    rs_read = {s: {} for s in range(3)}

    def reads_rs(eng, t0, n, token):
        for s in range(t0 // 256, (t0 + n) // 256):
            rs_read[s][eng] = token

    def split(hi, lo, src, waits, over):
        a = act([waits, over], lambda e: e.copy(hi, src))
        d = dve([waits, over, a], lambda e: e.tensor_tensor(lo, src, hi, ALU.subtract))
        return [a, d]

    sums = {}

    def begin_sum(s, over):
        sums[s] = {"n": 0, "tok": [None, None], "over": over}

    def acc_view(s, part):
        return M[:, ACC + s * 512 + part * 256:ACC + s * 512 + (part + 1) * 256]

    def sum_add(s, src, tok, square):
        me = sums[s]
        part = (me["n"] + 1) % 2
        acc = acc_view(s, part)
        if me["n"] < 2:
            me["tok"][part] = act([tok, me["over"]], lambda e: e.activation(acc, src, ACT.Square if square else ACT.Identity))
        else:
            eng = dve if part == 0 else pool
            if square:
                sq, key = tmp("a", 256)
                a = act([tok, rfree[key]], lambda e: e.activation(sq, src, ACT.Square))
                me["tok"][part] = eng([a, me["tok"][part]], lambda e: e.tensor_tensor(acc, acc, sq, ALU.add))
                rfree[key] = [me["tok"][part]]
            else:
                me["tok"][part] = eng([tok, me["tok"][part]], lambda e: e.tensor_tensor(acc, acc, src, ALU.add))
        me["n"] += 1

    def join_sum(s, ones, b):
        me = sums[s]
        pe([me["tok"][1], *free[b]], lambda e: e.matmul(PS[:, b, 0:256], ones, acc_view(s, 1), start=True, stop=False), False)
        state["joined"] = pe([me["tok"][0]], lambda e: e.matmul(
            PS[:, b, 0:256], ones, acc_view(s, 0), start=False, stop=True))
        return state["joined"]

    def rstd(b, n, t0, waits, eps):
        over = [list(rs_read[s].values()) for s in range(t0 // 256, -(-(t0 + n) // 256))]
        a = act([waits, over], lambda e: e.activation(rs_view(n, t0), PS[:, b, 0:n], ACT.Sqrt, bias=EPS[eps]))
        free[b] = [a]
        return dve([a], lambda e: e.reciprocal(rs_view(n, t0), rs_view(n, t0)))

    def mean_square(tiles, waits, n, ones, b):
        last = None
        for i, t in enumerate(tiles):
            sq, key = tmp("a", n)
            a = act([waits[i], rfree[key]], lambda e, sq=sq, t=t: e.activation(sq, t, ACT.Square))
            last = pe([a, *(free[b] if i == 0 else [])],
                      lambda e, sq=sq, i=i: e.matmul(PS[:, b, 0:n], ones, sq, start=i == 0, stop=i == len(tiles) - 1))
            rfree[key] = [last]
        return last

    def mean_square4(tiles, waits, n, ones, b):
        sq, keys, a = zip(*[(*tmp("ab"[i // 2], n), None) for i in range(4)])
        a = [act([waits[i], rfree[keys[i]]], lambda e, i=i: e.activation(sq[i], tiles[i], ACT.Square)) for i in range(4)]
        x = dve([a[0], a[1]], lambda e: e.tensor_tensor(sq[0], sq[0], sq[1], ALU.add))
        y = pool([a[2], a[3]], lambda e: e.tensor_tensor(sq[2], sq[2], sq[3], ALU.add))
        yield
        pe([x, free[b]], lambda e: e.matmul(PS[:, b, 0:n], ones, sq[0], start=True, stop=False), False)
        last = pe([y], lambda e: e.matmul(PS[:, b, 0:n], ones, sq[2], start=False, stop=True))
        for key in keys:
            rfree[key] = [last]
        yield last

    ada = {"n": 0, "limit": 48, "rows": None}
    ABANK, MBANK = 6, 7
    mod_ready = {}

    def ada_rows():
        if ada["rows"] is None:
            return
        layer, n, a = ada["rows"]
        ada["rows"] = None
        for j in range(4):
            col = n * 4 + j
            row = X[0:4, (j // 2) * 768 + 512 + (j % 2) * 128:(j // 2) * 768 + 640 + (j % 2) * 128]
            ada["row_read"] = pe([a, *(free[MBANK] if col == 0 else [])], lambda e, col=col, row=row: e.matmul(
                PS[:, MBANK, col * 2:col * 2 + 2], row, comb, start=True, stop=True, skip_group_check=True), j == 3)
        if n < 11:
            return
        for who in range(2):
            src = PS[:, MBANK, 0:96].rearrange("p (c w) -> p w c", w=2)[:, who, :]
            o = (layer * 2 + who) * 48
            d = dve([ada["row_read"]], lambda e, src=src, o=o, layer=layer: e.tensor_tensor(
                MOD[:, o:o + 48], src, PAR[:, POFF["ada_b"] + layer * 48:POFF["ada_b"] + layer * 48 + 48], ALU.add))
            free[MBANK] = [d]
            t = []
            for g in (1, 4):
                v = MOD[:, o + g * 8:o + g * 8 + 8]
                t.append(dve([d], lambda e, v=v: e.tensor_scalar(v, v, 1.0, None, ALU.add)))
            for idx, (lay, w, ln, g) in enumerate(BEHIND):
                if (lay, w) == (layer, who):
                    v = MOD[:, 192 + idx * 8:192 + idx * 8 + 8]
                    lb = PAR[:, POFF["ln_b"] + ln * 8:POFF["ln_b"] + ln * 8 + 8]
                    sc_, sh_ = MOD[:, o + (g + 1) * 8:o + (g + 2) * 8], MOD[:, o + g * 8:o + (g + 1) * 8]
                    x = dve([t], lambda e, v=v, lb=lb, sc_=sc_: e.tensor_tensor(v, lb, sc_, ALU.mult))
                    t.append(dve([x], lambda e, v=v, sh_=sh_: e.tensor_tensor(v, v, sh_, ALU.add)))
            mod_ready[layer] = t[-1]

    def ada_step():
        i = ada["n"]
        if i >= ada["limit"]:
            ada_rows()
            return
        ada["n"] += 1
        layer, r = divmod(i, 48)
        n, blk = divmod(r, 4)
        jj, slot, ready = next_block(dram["ada"][layer, n, blk], (SLOT,))
        out = PS[:, ABANK, 0:512]
        done = None
        for kk in range(2):
            k = blk * 2 + kk
            cnd = H[:, k * 768 + 512:k * 768 + 640]
            for w in (WHI, WLO):
                first = k == 0 and w is WHI
                last = k == 7 and w is WLO
                mv = w[:, slot, kk * 512:(kk + 1) * 512]
                done = pe([*ready, *cond_ready, *(free[ABANK] if first else [])],
                          lambda e, cnd=cnd, mv=mv, first=first, last=last: e.matmul(out, cnd, mv, start=first, stop=last),
                          kk == 1 and w is WLO)
        block_over(jj, done)
        ada_rows()
        if blk == 3:
            row = X[0:4, 0:1536].rearrange("p (c t) -> p c t", t=768)[:, :, 512:768]
            a = act([done, ada.get("row_read")], lambda e: e.copy(
                row, PS[0:4, ABANK, 0:512].rearrange("p (c t) -> p c t", c=2)))
            free[ABANK] = [a]
            ada["rows"] = (layer, n, a)

    def mod(layer, who, g, c):
        o = (layer * 2 + who) * 48 + g * 8 + c
        return MOD[:, o:o + 1]

    state = {"h_over": [], "hid_over": [], "misc_over": [], "acc_over": []}
    h_ready, xt, pre = {}, {}, {}

    def to_rms(gain):
        def send(c, s):
            hi, lo, x = hs(0, c, s * 256, 256), hs(1, c, s * 256, 256), xs(c, s * 256, 256)
            a = act([xt[(c, s)], state["h_over"]], lambda e: e.activation(hi, x, ACT.Identity, scale=par(gain, c)))
            d = dve([xt[(c, s)], a, state["h_over"]], lambda e: e.scalar_tensor_tensor(
                out=lo, in0=x, scalar=par(gain, c), in1=hi, op0=ALU.mult, op1=ALU.subtract))
            h_ready[(c, s)] = [a, d]
            if c == 0:
                begin_sum(s, [])
                pre.pop(s, None)
            sum_add(s, x, xt[(c, s)], True)
        return send

    def pre_rs(t0, n):
        for s in range(t0 // 256, (t0 + n) // 256):
            if s not in pre:
                b = bank()
                pre[s] = rstd(b, 256, s * 256, join_sum(s, one1024, b), RMS_EPS)
        return [pre[s] for s in range(t0 // 256, (t0 + n) // 256)]

    def to_modulated(layer, g):
        def send(c, s):
            who = s // 2
            hi, lo, x = hs(0, c, s * 256, 256), hs(1, c, s * 256, 256), xs(c, s * 256, 256)
            sc_, sh_ = mod(layer, who, g + 1, c), mod(layer, who, g, c)
            t, key = tmp("b", 256)
            w = [xt[(c, s)], mod_ready[layer]]
            over = state["h_over"] if s < 2 else ada["row_read"]
            a = act([w, over], lambda e: e.activation(hi, x, ACT.Identity, scale=sc_, bias=sh_))
            d = dve([w, rfree[key]], lambda e: e.tensor_scalar(t, x, sc_, sh_, ALU.mult, ALU.add))
            d2 = dve([d, a, over], lambda e: e.tensor_tensor(lo, t, hi, ALU.subtract))
            h_ready[(c, s)] = [a, d2]
            rfree[key] = [d2]
            xt[(c, s)] = act([a, d], lambda e: e.mul(x, x, ALPHA))
        return send

    def start_chain(s, wait, gen):
        chains[s] = [wait, gen]

    def once(fn):
        fn()
        yield from ()

    def norm_chain(s, F, f_tok, post, send):
        b = bank()
        r = rstd(b, 256, s * 256, join_sum(s, one1024, b), RMS_EPS)
        rs = rs_view(256, s * 256)
        for j in range(DC + 3):
            if j < DC:
                f, x = F(j)[:, s * 256:(s + 1) * 256], xs(j, s * 256, 256)
                d = dve([f_tok[(j, s)], r], lambda e, j=j, f=f: e.scalar_tensor_tensor(
                    out=f, in0=f, scalar=par(post, j), in1=rs, op0=ALU.mult, op1=ALU.mult))
                reads_rs("dve", s * 256, 256, d)
                xt[(j, s)] = pool([d, xt[(j, s)]], lambda e, f=f, x=x: e.tensor_tensor(x, x, f, ALU.add))
            if j >= 3:
                send(j - 3, s)
                if j in (7,):
                    yield 1
        state["misc_over"] = [state["misc_over"], xt[(6, s)], xt[(7, s)]]

    def layer_norm_chain(s, layer, which, send, wait=2):
        b = bank()
        m = join_sum(s, one1024, b)
        begin_sum(s, [m])
        ln = layer * 2 + which
        for c in range(DC):
            x = xs(c, s * 256, 256)
            xt[(c, s)] = dve([m, xt[(c, s)]], lambda e, x=x: e.tensor_tensor(x, x, PS[:, b, 0:256], ALU.subtract))
            free[b] = [xt[(c, s)]]
        for c in range(DC):
            sum_add(s, xs(c, s * 256, 256), xt[(c, s)], True)
        yield wait
        b2 = bank()
        r = rstd(b2, 256, s * 256, join_sum(s, one1024, b2), LN_EPS)
        rs = rs_view(256, s * 256)
        held = {}
        for c in range(DC + 2):
            if c < DC:
                x = xs(c, s * 256, 256)
                g = PAR[:, POFF["ln_g"] + ln * 8 + c:POFF["ln_g"] + ln * 8 + c + 1]
                t, key = tmp("b", 256)
                d = dve([xt[(c, s)], r, rfree[key]], lambda e, t=t, x=x, g=g: e.scalar_tensor_tensor(
                    out=t, in0=x, scalar=g, in1=rs, op0=ALU.mult, op1=ALU.mult))
                reads_rs("dve", s * 256, 256, d)
                held[c] = (t, key, d)
            if c >= 2:
                t, key, d = held[c - 2]
                rfree[key] = send(c - 2, s, t, d)
                if c in (5,):
                    yield 1

    def after_ln(ln, layer, g, permute=False):
        def send(c, s, t, d):
            who = s // 2
            idx = [k for k, v in enumerate(BEHIND) if v == (layer, who, ln, g)][0]
            sc_, bs_ = mod(layer, who, g + 1, c), MOD[:, 192 + idx * 8 + c:192 + idx * 8 + c + 1]
            lb = MOD[:, 232 + ln * 8 + c:232 + ln * 8 + c + 1]
            x = xs(c, s * 256, 256)
            if permute and s < 2:
                pv = lambda part: hs(part, c, 0, 512).rearrange("p (c r) -> p r c", r=8)[:, 4 * s:4 * s + 4, :]
                sv = lambda v: v.rearrange("p (r c) -> p r c", c=64)
            else:
                pv = lambda part: hs(part, c, s * 256, 256)
                sv = lambda v: v
            u, ukey = tmp("a", 256)
            w = [d, mod_ready[layer]]
            a1 = act([w, state["h_over"]], lambda e: e.activation(pv(0), sv(t), ACT.Identity, scale=sc_, bias=bs_))
            d1 = pool([w, rfree[ukey]], lambda e: e.tensor_scalar(u, t, sc_, bs_, ALU.mult, ALU.add))
            d2 = dve([a1, d1], lambda e: e.tensor_tensor(pv(1), sv(u), pv(0), ALU.subtract))
            a2 = act([d, lnb_ready], lambda e: e.activation(x, t, ACT.Identity, scale=ALPHA, bias=lb))
            rfree[ukey] = [d2]
            h_ready[(c, s)] = [a1, d2]
            xt[(c, s)] = a2
            return [a1, a2, d1]
        return send

    def gated(layer, g, last, chain):
        def post(pi, j, b, t0, n, done):
            who = 0 if t0 < 512 else 1
            x, gt = xs(j, t0, n), mod(layer, who, g, j)
            d = dve([done, cover(xt, j, t0, n)], lambda e: e.scalar_tensor_tensor(
                out=x, in0=PS[:, b, 0:n], scalar=gt, in1=x, op0=ALU.mult, op1=ALU.add))
            for s in range(t0 // 256, (t0 + n) // 256):
                xt[(j, s)] = d
                if pi == last:
                    summed(s, j, xs(j, s * 256, 256), d, False, chain)
            return [d]
        return post

    def summed(s, j, src, tok, square, chain):
        if j == 0:
            begin_sum(s, state["acc_over"])
        sum_add(s, src, tok, square)
        if j == DC - 1:
            start_chain(s, 2, chain(s))

    def ffn(gu, dn, parts, segs, subs, down_post, scaled, between=None):
        pitch = 512 if len(segs) == 1 else 768

        def hid(half, k, t0, n):
            return HID[:, half * 4096 + k * pitch + t0:half * 4096 + k * pitch + t0 + n]

        c0 = 0
        over = state["hid_over"]
        for i in range(4):
            rfree[[("gate", i)]] = [state["misc_over"]]
        for pi, size in enumerate(parts):
            ready, gate = {}, {}

            def gate_post(k):
                def post(b, t0, n, done):
                    gi = turn.get("gate", 0)
                    turn["gate"] = gi + 1
                    s, key = M[:, GATE + gi % 4 * 512:GATE + gi % 4 * 512 + n], [("gate", gi % 4)]
                    rs = rs_view(n, t0)
                    if scaled:
                        r = pre_rs(t0, n)
                        d = dve([done, r, rfree[key]], lambda e: e.tensor_tensor(s, PS[:, b, 0:n], rs, ALU.mult))
                        a = act([d], lambda e: e.activation(s, s, ACT.Silu))
                        p_ = pool([a], lambda e: e.tensor_tensor(s, s, rs, ALU.mult))
                        reads_rs("pool", t0, n, p_)
                        gate[(k, t0)] = (s, key, p_)
                        return [d]
                    a = act([done, rfree[key]], lambda e: e.activation(s, PS[:, b, 0:n], ACT.Silu))
                    gate[(k, t0)] = (s, key, a)
                    return [a]
                return post

            def up_post(k, over=over):
                def post(b, t0, n, done):
                    s, key, a = gate[(k, t0)]
                    t, key2 = tmp("b", n)
                    d = dve([done, a, rfree[key2]], lambda e: e.tensor_tensor(t, s, PS[:, b, 0:n], ALU.mult))
                    rfree[key] = [d]
                    got = split(hid(0, k, t0, n), hid(1, k, t0, n), t, d, over)
                    rfree[key2] = got
                    for sb_ in range(t0 // 256, (t0 + n) // 256):
                        ready[(k, sb_)] = got
                    return [d]
                return post

            hw = lambda k, t0, n: cover(h_ready, k, t0, n)
            specs = []
            for k in range(size):
                specs.append((gu[c0 + k], (SLOT,), DC, hacts, hw, [(0, gate_post(k))]))
                specs.append((gu[FC + c0 + k], (SLOT,), DC, hacts, hw, [(0, up_post(k))]))
            if pi == 0:
                columns(specs[:4], subs, batch=4, between=between)
                specs = specs[4:]
            last_h = columns(specs, segs, between=between)
            hw2 = lambda k, t0, n: cover(ready, k, t0, n)
            specs = [(dn[j][:, c0 * P:(c0 + size) * P], (size * P,), size, hid, hw2,
                      [(0, lambda b, t0, n, done, j=j, pi=pi: down_post(pi, j, b, t0, n, done))]) for j in range(DC)]
            if pi == len(parts) - 1:
                state["h_over"] = [last_h]
                last = columns(specs, subs, batch=4, between=between)
            else:
                last = columns(specs, segs, between=between)
            over = [last]
            c0 += size
        state["hid_over"] = over
        state["misc_over"] = [state["misc_over"], *(rfree[[("gate", i)]] for i in range(4))]

    SUB1 = ((0, 256), (256, 256))
    SUB2 = ((512, 256), (0, 256), (256, 256))

    def first_ffn(post, gu, dn, send, between):
        F = lambda j: M[:, j * 512:(j + 1) * 512]
        f_tok = {}

        def down_post(pi, j, b, t0, n, done):
            f = F(j)[:, t0:t0 + n]
            if pi == 0:
                d = act([done, state["misc_over"]], lambda e: e.copy(f, PS[:, b, 0:n]))
            else:
                d = dve([done, cover(f_tok, j, t0, n)], lambda e: e.tensor_tensor(f, f, PS[:, b, 0:n], ALU.add))
            for s in range(t0 // 256, (t0 + n) // 256):
                f_tok[(j, s)] = d
                if pi == 2:
                    summed(s, j, F(j)[:, s * 256:(s + 1) * 256], d, True,
                           lambda s: norm_chain(s, F, f_tok, post, send))
            return [d]

        ffn(gu, dn, PARTS1, SEG1, SUB1, down_post, True, between)

    q.stage("start")
    load([], PAR[:, :], dram["params"], sems["par"])
    par_ready = load([], CON[:, :], dram["consts"], sems["par"])
    for eng in ("pe", "act", "dve", "pool"):
        q.wait(eng, par_ready)
    x_all = X[:, :].rearrange("p (c t) -> p c t", c=DC)
    for i in range(3):
        if plan is not None and i >= 1:
            issue_load(ring["dma"])
            ring["dma"] += 1
        if i < 2:
            t = load([], x_all[:, :, i * 256:(i + 1) * 256],
                     dram["x"].rearrange("c p t -> p c t")[:, :, i * 256:(i + 1) * 256], sems["x"][i])
            for c in range(DC):
                xt[(c, i)] = t
    cnd_all = H[:, 0:6144].rearrange("p (k t) -> p k t", t=768)[:, :, 512:640]
    z = TMP[:, 1024:1152]
    d0 = dve([], lambda e: e.memset(z, 0.0))
    d1 = None
    for k in range(8):
        d1 = dve([d0], lambda e, k=k: e.tensor_copy(cnd_all[:, k, :], z))
    sc = TMP[:, 1152:1168]
    a0 = act([], lambda e: e.activation(sc, PAR[:, POFF["cond"]:POFF["cond"] + 16], ACT.Silu))
    sc2 = sc.rearrange("p (k w) -> p k w", w=2)
    a1 = act([a0, d1], lambda e: e.copy(cnd_all[:, :, 0:2], sc2))
    d2 = dve([a1], lambda e: e.tensor_tensor(cnd_all[:, :, 2:4], sc2, cnd_all[:, :, 0:2], ALU.subtract))
    cond_ready = [d2]
    rfree[both("b")] = [d2, d1]
    lnb_ready = dve([], lambda e: e.tensor_scalar(
        MOD[:, 232:264], PAR[:, POFF["ln_b"]:POFF["ln_b"] + 32], ALPHA, None, ALU.mult))
    for name in ("ffn1_post_g", "ffn2_post_g"):
        v = PAR[:, POFF[name]:POFF[name] + 8]
        t = dve([], lambda e, v=v: e.tensor_scalar(v, v, 0.5, None, ALU.mult))
    q.wait("dve", t)

    def first_mixer():
        QA, KA, VA, SA, PT, OA, XL = 0, 2048, 2560, 3072, 5120, 7168, 9216
        BD, MASK, GA, SM = 11280, 12304, 12560, 14608
        pro = state["misc_over"]
        bd_ready = load([pro], M[:, BD:BD + 1024], dram["gates"], sems["misc"])
        mask_ready = load([pro], M[:, MASK:MASK + 256], dram["mask1"], sems["misc"])
        bd_ready = mask_ready
        hw = lambda k, t0, n: cover(h_ready, k, t0, n)
        win = dram["w_in"]

        sm = lambda o, n: M[:, SM + o:SM + o + n]
        nsink = sm(0, 8)
        t = dve([pro, par_ready], lambda e: e.tensor_scalar(nsink, PAR[:, POFF["sinks"]:POFF["sinks"] + 8], -1.0, None, ALU.mult))
        nsink_ready = t
        lam = PAR[:, POFF["lam"]:POFF["lam"] + 4]
        en, den, ratio, z, pl, mn, cls, sp_ = (sm(8 + 4 * i, 4) for i in range(8))
        t = dve([pro], lambda e: e.tensor_scalar(mn, lam, -1.0, None, ALU.mult))
        t = dve([t], lambda e: e.tensor_tensor(en, mn, lam, ALU.min))
        t = act([t], lambda e: e.activation(en, en, ACT.Exp))
        t = dve([t], lambda e: e.tensor_scalar(den, en, 2.0, None, ALU.add))
        t = dve([t], lambda e: e.reciprocal(sp_, den))
        t = dve([t], lambda e: e.tensor_tensor(ratio, en, sp_, ALU.mult))
        t = dve([t], lambda e: e.tensor_tensor(z, ratio, ratio, ALU.mult))
        t = dve([t], lambda e: e.tensor_scalar(pl, z, 1.0 / 15, 1.0 / 13, ALU.mult, ALU.add))
        for k in (11, 9, 7, 5, 3, 1):
            t = dve([t], lambda e: e.tensor_tensor(pl, pl, z, ALU.mult))
            t = dve([t], lambda e, k=k: e.tensor_scalar(pl, pl, 1.0 / k, None, ALU.add))
        t = dve([t], lambda e: e.tensor_tensor(pl, pl, ratio, ALU.mult))
        t = dve([t], lambda e: e.tensor_scalar(mn, lam, 0.0, None, ALU.min))
        t = dve([t], lambda e: e.scalar_tensor_tensor(out=cls, in0=pl, scalar=-2.0, in1=mn, op0=ALU.mult, op1=ALU.add))
        cls_ready = dve([t], lambda e: e.tensor_scalar(cls, cls, 8.0, None, ALU.mult))

        def scaled_to(dst, got, by=None):
            def post(b, t0, n, done):
                r, d_ = pre_rs(t0, n), dst(t0, n)
                if by is None:
                    d = dve([done, r, pro], lambda e: e.tensor_tensor(d_, PS[:, b, 0:n], rs_view(n, t0), ALU.mult))
                else:
                    d = dve([done, r, pro], lambda e: e.scalar_tensor_tensor(
                        out=d_, in0=PS[:, b, 0:n], scalar=by, in1=rs_view(n, t0), op0=ALU.mult, op1=ALU.mult))
                reads_rs("dve", t0, n, d)
                got.append(d)
                return [d]
            return post

        XLc = lambda c, o, n: M[:, XL + c * 515 + o:XL + c * 515 + o + n]
        XCc, Uc, Ac, Gc = (lambda c, base=base: M[:, base + c * 512:base + (c + 1) * 512] for base in (OA, SA, PT, GA))
        at = lambda base: (lambda t0, n: M[:, base + t0:base + t0 + n])
        spec = lambda w, post: (win[w], (SLOT,), DC, hacts, hw, [(0, post)])
        cw = lambda j, c: par("conv_w", j * 4 + c)
        q_ready, g_raw = {g: [] for g in range(5)}, {c: [] for c in range(4)}
        xl_ready, xc_ready, r_ready, i_ready, g_ready, h_done = {}, {}, {}, {}, {}, {}
        vt_ready = []
        for c in range(4):
            xl_ready[c] = [dve([pro], lambda e, c=c: e.memset(XLc(c, 0, 3), 0.0))]

        def convolve(c):
            t = dve([xl_ready[c]], lambda e: e.tensor_scalar(
                XCc(c), XLc(c, 0, 512), cw(0, c), par("conv_b", c), ALU.mult, ALU.add))
            for j in range(1, 4):
                t = dve([t], lambda e, j=j: e.scalar_tensor_tensor(
                    out=XCc(c), in0=XLc(c, j, 512), scalar=cw(j, c), in1=XCc(c), op0=ALU.mult, op1=ALU.add))
            xc_ready[c] = t

        def lru_gates(c):
            for gi, (dst, bias, reg) in enumerate(((Ac, "b_rg", r_ready), (Uc, "b_ig", i_ready))):
                b = bank()
                mm = pe([xc_ready[c], bd_ready, free[b]], lambda e, gi=gi, b=b: e.matmul(
                    PS[:, b, :], M[:, BD + gi * 512 + c * P:BD + gi * 512 + (c + 1) * P], XCc(c), start=True, stop=True))
                reg[c] = act([mm], lambda e, b=b, dst=dst, bias=bias: e.activation(
                    dst(c), PS[:, b, :], ACT.Sigmoid, bias=par(bias, c)))
                free[b] = [reg[c]]

        def recurrences():
            th, keys, a1, a2, u1, sq, wide = {}, {}, {}, {}, {}, {}, {}
            for c in range(4):
                which = "a" if c < 2 else "b"
                th[c], keys[c] = tmp(which, L)
                la = dve([r_ready[c], cls_ready], lambda e, c=c: e.tensor_scalar(Ac(c), Ac(c), cls[:, c:c + 1], None, ALU.mult))
                u1[c] = pool([i_ready[c]], lambda e, c=c: e.tensor_tensor(Uc(c), Uc(c), XCc(c), ALU.mult))
                a1[c] = act([la, rfree[keys[c]]], lambda e, c=c: e.activation(th[c], Ac(c), ACT.Tanh))
            for c in range(4):
                a2[c] = act([a1[c]], lambda e, c=c: e.activation(Ac(c), Ac(c), ACT.Exp))
                sq[c] = act([a2[c], xc_ready[c]], lambda e, c=c: e.activation(XLc(c, 0, L), Ac(c), ACT.Square))
            yield
            for c in range(4):
                t = dve([sq[c]], lambda e, c=c: e.scalar_tensor_tensor(
                    out=th[c], in0=XLc(c, 0, L), scalar=1.0, in1=th[c], op0=ALU.add, op1=ALU.mult))
                wide[c] = dve([t], lambda e, c=c: e.tensor_scalar(th[c], th[c], -1.0, 0.0, ALU.mult, ALU.max))
            for c in range(4):
                wide[c] = act([wide[c]], lambda e, c=c: e.activation(th[c], th[c], ACT.Sqrt))
            yield
            for c in range(4):
                t = dve([wide[c], u1[c]], lambda e, c=c: e.tensor_tensor(Uc(c), Uc(c), th[c], ALU.mult))
                rfree[keys[c]] = [t]
                h_done[c] = dve([t], lambda e, c=c: e.tensor_tensor_scan(
                    XLc(c, 0, 512), Ac(c), Uc(c), 0.0, ALU.mult, ALU.add))
            yield
            for c in range(4):
                g_ready[c] = act(g_raw[c], lambda e, c=c: e.activation(Gc(c), Gc(c), ACT.Gelu_apprx_tanh))
            for c in range(4):
                g_ready[c] = pool([g_ready[c], h_done[c]], lambda e, c=c: e.tensor_tensor(Gc(c), XLc(c, 0, 512), Gc(c), ALU.mult))

        columns([spec(c, scaled_to(lambda t0, n, c=c: XLc(c, 3 + t0, n), xl_ready[c])) for c in range(4)], SUB1, batch=4)
        lru = recurrences()
        for c in range(4):
            if c == 0:
                convolve(0)
            if c < 3:
                convolve(c + 1)
            columns([spec(8 + c, scaled_to(at(QA + c * 512), q_ready[c], 0.125))], SEG1)
            lru_gates(c)
        next(lru)
        columns([spec(12, scaled_to(at(KA), q_ready[4]))], SEG1)
        next(lru)
        columns([spec(13, scaled_to(at(GA + 1536), vt_ready))], SEG1)
        def g_projection(c):
            state["h_over"] = [columns([spec(4 + c, scaled_to(at(GA + c * 512), g_raw[c]))], SEG1, banks=(7,) if c > 1 else None)]

        g_projection(0)
        b = bank()
        for tt in range(4):
            turned = pe([vt_ready, free[b]], lambda e, tt=tt: e.transpose(
                PS[:, b, tt * P:(tt + 1) * P], M[:, GA + 1536 + tt * P:GA + 1536 + (tt + 1) * P], ident), tt == 3)
        v_ready = act([turned], lambda e: e.copy(M[:, VA:VA + 512], PS[:, b, :]))
        free[b] = [v_ready]
        g_projection(1)
        next(lru)
        lru_over = [h_done[c] for c in range(4)]

        units = [(n, kv) for n in range(4) for kv in range(2)]
        st = {}
        wbuf = (M[:, SA:SA + 1024], M[:, SA + 1024:SA + 2048], TMP[:, 1024:2048])
        att_free = {("s", 0): lru_over, ("s", 1): lru_over, ("s", 2): rfree[both("b")], ("p", 0): lru_over, ("p", 1): lru_over}

        def scores(i):
            n, kv = units[i]
            NK = P if n == 0 else 2 * P
            k0 = n * P - (NK - P)
            b0 = (0, 2)[i % 2]
            pp = slice(kv * 64, kv * 64 + 64)
            for g in range(4):
                bb = b0 + g // 2
                done = pe([q_ready[g], q_ready[4], free[bb] if g % 2 == 0 else []], lambda e, g=g, bb=bb: e.matmul(
                    PS[:, bb, (g % 2) * 256:(g % 2) * 256 + NK], M[pp, QA + g * 512 + n * P:QA + g * 512 + (n + 1) * P],
                    M[pp, KA + k0:KA + k0 + NK], start=True, stop=True, skip_group_check=True), g == 3)
            s = wbuf[i % 3][:, 0:4 * NK].rearrange("p (g k) -> p g k", g=4)
            o = 48 + (i % 3) * 24
            mx, nm, es, sums, rec = (sm(o + 4 * j, 4) for j in range(5))
            for g in range(4):
                d = dve([done, mask_ready, att_free[("s", i % 3)]], lambda e, g=g: e.tensor_tensor_reduce(
                    s[:, g, :], PS[:, b0 + g // 2, (g % 2) * 256:(g % 2) * 256 + NK], M[:, MASK + 256 - NK:MASK + 256],
                    1.0, -3.0e38, ALU.add, ALU.max, mx[:, g:g + 1]))
            free[b0] = free[b0 + 1] = [d]
            m2 = dve([d, nsink_ready], lambda e: e.scalar_tensor_tensor(
                out=nm, in0=mx, scalar=-1.0, in1=sm(kv * 4, 4), op0=ALU.mult, op1=ALU.min))
            m3 = dve([m2], lambda e: e.tensor_tensor(es, nm, sm(kv * 4, 4), ALU.subtract))
            x = [act([m2], lambda e, g=g: e.activation(s[:, g, :], s[:, g, :], ACT.Exp, bias=nm[:, g:g + 1],
                                                       accum_out=sums[:, g:g + 1])) for g in range(4)]
            x.append(act([m3], lambda e: e.activation(es, es, ACT.Exp)))
            r1 = dve(x, lambda e: e.tensor_tensor(es, es, sums, ALU.add))
            r2 = dve([r1], lambda e: e.reciprocal(rec, es))
            far = pool([r2], lambda e: e.tensor_tensor(
                s[:, 2:4, :], s[:, 2:4, :], rec[:, 2:4].unsqueeze(2).to_broadcast([P, 2, NK]), ALU.mult))
            p = [dve([r2], lambda e, g=g: e.tensor_scalar(s[:, g, :], s[:, g, :], rec[:, g:g + 1], None, ALU.mult))
                 for g in range(2)]
            st[i] = (s, NK, p + [far, far])

        def turn_weights(i):
            s, NK, p = st[i]
            KT = NK // P
            ev = []
            for kt in range(KT):
                bb = 4 + kt
                for g in range(4):
                    done = pe([p[g], free[bb] if g == 0 else []], lambda e, g=g, bb=bb, kt=kt: e.transpose(
                        PS[:, bb, g * P:(g + 1) * P], s[:, g, kt * P:(kt + 1) * P], ident), g == 3)
                dst = M[:, PT + (i % 2) * 1024 + kt * 512:PT + (i % 2) * 1024 + (kt + 1) * 512]
                ev.append(act([done, att_free[("p", i % 2)]], lambda e, dst=dst, bb=bb: e.copy(dst, PS[:, bb, :])))
                free[bb] = [ev[-1]]
            att_free[("s", i % 3)] = [done]
            st[i] = (KT, ev)

        o_ready = {}

        def attend(i):
            n, kv = units[i]
            KT, ev = st[i]
            pp = slice(kv * 64, kv * 64 + 64)
            for kt in range(KT):
                tt = n - (KT - 1) + kt
                done = pe([ev[kt], v_ready, free[6] if kt == 0 else []], lambda e, kt=kt, tt=tt: e.matmul(
                    PS[pp, 6, :], M[:, VA + tt * P + kv * 64:VA + tt * P + kv * 64 + 64],
                    M[:, PT + (i % 2) * 1024 + kt * 512:PT + (i % 2) * 1024 + (kt + 1) * 512],
                    start=kt == 0, stop=kt == KT - 1), kt == KT - 1)
            att_free[("p", i % 2)] = [done]
            src = PS[pp, 6, :].rearrange("p (g t) -> p g t", g=4)
            dst = M[pp, OA:OA + 2048].rearrange("p (g t) -> p g t", g=4)[:, :, n * P:(n + 1) * P]
            o_ready[(n, kv)] = dve([done, pro, lru_over], lambda e: e.tensor_copy(dst, src))
            free[6] = [o_ready[(n, kv)]]

        y_ready = {}
        y_at = lambda half, k, t0, n: HID[:, half * 4096 + k * 512 + t0:half * 4096 + k * 512 + t0 + n]

        def norm_queries(n):
            o = M[:, OA:OA + 2048].rearrange("p (g t) -> p g t", g=4)[:, :, n * P:(n + 1) * P]
            sq, key = tmp("a", L)
            sq = sq.rearrange("p (g t) -> p g t", g=4)
            got = [o_ready[(n, 0)], o_ready[(n, 1)]]
            a = act([got, rfree[key]], lambda e: e.activation(sq, o, ACT.Square))
            for g in range(4):
                m = pe([a, free[7] if g == 0 else []], lambda e, g=g: e.matmul(
                    PS[:, 7, 0:P], one512, sq[:, g, :], start=g == 0, stop=g == 3), g == 3)
            rfree[key] = [m]
            rs = rs_view(P, n * P)
            a = act([m, list(rs_read[n // 2].values())], lambda e: e.activation(rs, PS[:, 7, 0:P], ACT.Sqrt, bias=EPS[RMS_EPS]))
            free[7] = [a]
            r = dve([a], lambda e: e.reciprocal(rs, rs))
            x = dve([r, got], lambda e: e.tensor_tensor(o, o, rs.unsqueeze(1).to_broadcast([P, 4, P]), ALU.mult))
            rs_read[n // 2]["dve"] = x
            hi_ = [act([x, state["hid_over"]], lambda e, g=g: e.activation(
                y_at(0, 4 + g, n * P, P), o[:, g, :], ACT.Identity, scale=par("g_mix", 4 + g))) for g in range(4)]
            for g in range(4):
                d = dve([hi_[g], x, state["hid_over"]], lambda e, g=g: e.scalar_tensor_tensor(
                    out=y_at(1, 4 + g, n * P, P), in0=o[:, g, :], scalar=par("g_mix", 4 + g),
                    in1=y_at(0, 4 + g, n * P, P), op0=ALU.mult, op1=ALU.subtract))
                y_ready[(4 + g, n)] = [hi_[g], d]

        def norm_lru():
            all_h = [g_ready[c] for c in range(4)]
            m = mean_square([Gc(c) for c in range(4)], all_h, L, one512, 7)
            rs = XLc(0, 0, L)
            yield
            a = act([m, all_h], lambda e: e.activation(rs, PS[:, 7, :], ACT.Sqrt, bias=EPS[RMS_EPS]))
            free[7] = [a]
            r = dve([a], lambda e: e.reciprocal(rs[:, 0:256], rs[:, 0:256]))
            yield
            r = dve([a], lambda e: e.reciprocal(rs[:, 256:512], rs[:, 256:512]))
            for c in range(4):
                hi, lo = y_at(0, c, 0, L), y_at(1, c, 0, L)
                d = dve([r], lambda e, c=c: e.scalar_tensor_tensor(
                    out=Gc(c), in0=Gc(c), scalar=par("g_mix", c), in1=rs, op0=ALU.mult, op1=ALU.mult))
                a = act([d, state["hid_over"]], lambda e, c=c, hi=hi: e.copy(hi, Gc(c)))
                p_ = pool([a, d, state["hid_over"]], lambda e, c=c, hi=hi, lo=lo: e.tensor_tensor(lo, Gc(c), hi, ALU.subtract))
                for n in range(4):
                    y_ready[(c, n)] = [a, p_]
                if c == 1:
                    yield
            state["acc_over"] = [p_]

        y_lru = norm_lru()

        def unit_step(i):
            if i < 8:
                scores(i)
            if i < 2:
                g_projection(2 + i)
                if i == 1:
                    next(lru, None)
            if 0 <= i - 2 < 8:
                turn_weights(i - 2)
            if 0 <= i - 3 < 8:
                attend(i - 3)
            if i in (5, 7, 9):
                norm_queries((i - 5) // 2)
            if i in (2, 3, 4, 6):
                next(y_lru, None)

        for i in range(9):
            unit_step(i)

        def last_units():
            for i in (9, 10):
                unit_step(i)
                yield 1
            norm_queries(3)

        start_chain(1, 1, last_units())

        F = lambda j: M[:, j * 512:(j + 1) * 512]
        f_tok = {}
        chain = lambda s: norm_chain(s, F, f_tok, "mix_post_g", to_rms("ffn2_pre_g"))

        def o_post(j):
            def post(b, t0, n, done):
                f, s = F(j)[:, t0:t0 + n], t0 // 256
                f_tok[(j, s)] = act([done], lambda e: e.copy(f, PS[:, b, 0:n]))
                summed(s, j, f, f_tok[(j, s)], True, chain)
                return [f_tok[(j, s)]]
            return post

        last = columns([(dram["w_o"][j], (SLOT,), DC, y_at,
                         lambda k, t0, n: [y_ready[(k, i)] for i in range(t0 // P, (t0 + n) // P)], [(0, o_post(j))])
                        for j in range(DC)], SUB1, batch=4)
        state["hid_over"] = [last]
        state["misc_over"] = [list(y_ready.values())]

    def retention():
        QK, OC, VV, PA, ST, DI, CS, GG = 0, 3072, 4096, 7168, 8192, 9728, 10880, 11904
        pro = [state["misc_over"]]
        dist_ready = load(pro, M[:, DI:DI + 1152], dram["dist"], sems["misc"])
        cs_ready = load(pro, M[:, CS:CS + 1024], dram["rope"], sems["misc"])
        dist_ready = cs_ready
        hw = lambda k, t0, n: cover(h_ready, k, t0, n)
        sm = lambda o, n: TMP[:, 2816 + o:2816 + o + n]
        dec = PAR[:, POFF["decay"]:POFF["decay"] + 8]
        eg, lg, nlb = sm(0, 8), sm(8, 8), sm(16, 8)
        t = act([pro, par_ready], lambda e: e.activation(eg, dec, ACT.Exp))
        t = dve([t], lambda e: e.tensor_scalar(lg, eg, -1.0, None, ALU.mult))
        lg_ready = dve([t], lambda e: e.tensor_scalar(nlb, eg, 768.0, -1.0, ALU.mult, ALU.mult))
        cos, sin = M[:, CS:CS + 512], M[:, CS + 512:CS + 1024]
        qk = lambda w, k, t0, n: M[:, QK + (w * 2 + k) * 768 + t0:QK + (w * 2 + k) * 768 + t0 + n]
        ov = {"qk": pro, "v": pro, "oc": pro, "p": [[], []], "st": pro, "g": pro, "ol": pro}
        def decays(h):
            d_ = M[:, DI:DI + 1152]
            LL, GS = M[:, ST:ST + 896], M[:, ST + 896:ST + 1536]
            tA, tB = M[:, PA:PA + 896], TMP[:, 1024:1920]
            t1 = dve([dist_ready, lg_ready, ov["st"], *ov["p"][0], *ov["p"][1]], lambda e, h=h: e.tensor_scalar(
                tA, d_[:, 0:896], 0.0, lg[:, h:h + 1], ALU.max, ALU.mult))
            t2 = dve([ov["st"], rfree[both("b")]], lambda e, h=h: e.tensor_scalar(
                tB, d_[:, 0:896], 0.0, eg[:, 4 + h:5 + h], ALU.min, ALU.mult))
            t3 = dve([t1, t2], lambda e: e.tensor_tensor(tA, tA, tB, ALU.add))
            t4 = act([t3, ov["st"]], lambda e: e.activation(LL, tA, ACT.Exp))
            ll_ready = dve([t4], lambda e: e.tensor_tensor(LL[:, 384:512], LL[:, 384:512], ident, ALU.add))
            t5 = act([lg_ready, ov["st"]], lambda e, h=h: e.activation(GS, d_[:, 512:1152], ACT.Exp, scale=lg[:, h:h + 1]))
            t6 = act([t3, lg_ready], lambda e, h=h: e.activation(tB[:, 0:640], d_[:, 512:1152], ACT.Exp,
                                                             scale=eg[:, 4 + h:5 + h], bias=nlb[:, 4 + h:5 + h]))
            gs_ready = dve([t5, t6], lambda e: e.tensor_tensor(GS, GS, tB[:, 0:640], ALU.add))
            rfree[both("b")] = [gs_ready]
            ov["p"] = [[t4], [t4]]
            return ll_ready, gs_ready

        def v_rows(h):
            return token_rows([dram["ret_v"][h, blk] for blk in range(4)], h_ready, ov["v"],
                              lambda tt: M[:, VV + tt * 512:VV + (tt + 1) * 512])[0]

        ahead = v_rows(0)
        ov["qk"] = ov["oc"] = [state["misc_over"]]
        for h in range(4):
            v_ready = ahead
            LL, GS = M[:, ST:ST + 896], M[:, ST + 896:ST + 1536]
            qk_ready = {}
            for w in range(2):
                halves = {}

                def qk_post(b, t0, n, done, w=w, halves=halves):
                    k = halves["k"]
                    if t0 == 512:
                        a = act([done, ov["qk"]], lambda e, k=k: e.copy(qk(w, k, 512, 256), PS[:, b, 0:256]))
                        qk_ready[(w, k, 512)] = a
                        return [a]
                    if k == 0:
                        halves["b"], halves["done"] = b, done
                        return [done]
                    b0, d0_ = halves["b"], halves["done"]
                    for half in range(2):
                        (u, ku), (v, kv_) = tmp("b", 512), tmp("b", 512)
                        s1, s2 = (cos, sin) if half == 0 else (sin, cos)
                        x1 = dve([d0_, rfree[ku], cs_ready], lambda e, u=u, s1=s1: e.tensor_tensor(u, PS[:, b0, :], s1, ALU.mult))
                        x2 = dve([done, rfree[kv_]], lambda e, v=v, s2=s2: e.tensor_tensor(v, PS[:, b, :], s2, ALU.mult))
                        op = ALU.subtract if half == 0 else ALU.add
                        x3 = dve([x1, x2, ov["qk"]], lambda e, u=u, v=v, op=op, half=half: e.tensor_tensor(
                            qk(w, half, 0, 512), u, v, op))
                        rfree[ku] = rfree[kv_] = [x3]
                        qk_ready[(w, half, 0)] = x3
                    free[b0] = [x2]
                    return [x2]

                for k in range(2):
                    halves["k"] = k
                    columns([(dram["ret_qk"][w * 8 + h * 2 + k], (SLOT,), DC, hacts, hw, [(0, qk_post)])], SEG2)

            if h == 0:
                weighted = decays(0)
            ll_ready, gs_ready = weighted

            g_ready = {}

            def g_post(b, t0, n, done, c):
                dst = M[:, GG + c * 768 + t0:GG + c * 768 + t0 + n]
                g_ready[(c, t0)] = act([done, ov["g"]], lambda e: e.activation(dst, PS[:, b, 0:n], ACT.Silu))
                return [g_ready[(c, t0)]]

            last_h = columns([(dram["ret_g"][h * 4 + c], (SLOT,), DC, hacts, hw,
                               [(0, lambda b, t0, n, d, c=c: g_post(b, t0, n, d, c))]) for c in range(4)], SEG2)
            state["h_over"] = [last_h]

            y_ready = {}
            o_tok = {}
            finish = None
            for t0, n, tiles in ((512, 256, (4, 5)), (0, 512, (0, 1, 2, 3, 4, 5))):
                weights = {}

                def score(i, t0=t0, n=n, tiles=tiles, weights=weights):
                    kt = tiles[i]
                    b = (4, 5)[i % 2]
                    kseg = 0 if kt < 4 else 512
                    for k in range(2):
                        done = pe([qk_ready[(0, k, t0)], qk_ready[(1, k, kseg)], free[b] if k == 0 else []],
                                  lambda e, k=k, b=b, kt=kt: e.matmul(PS[:, b, 0:n], qk(1, k, kt * P, P), qk(0, k, t0, n),
                                                                      start=k == 0, stop=k == 1), k == 1)
                    if t0 == 0 and kt < 4:
                        dd, dr = LL[:, 384 - 128 * kt:384 - 128 * kt + 512], ll_ready
                    elif t0 == 0:
                        dd, dr = GS[:, 128 - 128 * (kt - 4):128 - 128 * (kt - 4) + 512], gs_ready
                    else:
                        dd, dr = LL[:, 384 - 128 * (kt - 4):384 - 128 * (kt - 4) + 256], ll_ready
                    pw = M[:, PA + (i % 2) * 512:PA + (i % 2) * 512 + n]
                    d = dve([done, dr, ov["p"][i % 2]], lambda e, b=b: e.scalar_tensor_tensor(
                        out=pw, in0=PS[:, b, 0:n], scalar=0.0625, in1=dd, op0=ALU.mult, op1=ALU.mult))
                    free[b] = [d]
                    weights[i] = (pw, d)
                    ov["last_score"] = done

                def value(i, t0=t0, n=n, tiles=tiles, weights=weights):
                    pw, d = weights[i]
                    kt = tiles[i]
                    for c in range(4):
                        done = pe([d, v_ready[kt], free[c] if i == 0 else []], lambda e, c=c, kt=kt: e.matmul(
                            PS[:, c, 0:n], M[:, VV + kt * 512 + c * P:VV + kt * 512 + (c + 1) * P], pw,
                            start=i == 0, stop=i == len(tiles) - 1), c == 3 or i == len(tiles) - 1)
                        o_tok[(c, t0)] = done
                    ov["p"][i % 2] = [done]

                for i in range(len(tiles) + 1):
                    if i < len(tiles):
                        score(i)
                    if i >= 1:
                        value(i - 1)
                    if i == 3 and finish:
                        finish()
                src = []
                wt = []
                for c in range(4):
                    if t0 == 512:
                        dst = M[:, OC + c * 256:OC + (c + 1) * 256]
                        over = ov["oc"]
                    else:
                        dst = M[:, QK + c * 512:QK + (c + 1) * 512]
                        over = [ov["last_score"]]
                    a = act([o_tok[(c, t0)], over], lambda e, dst=dst, c=c, n=n: e.copy(dst, PS[:, c, 0:n]))
                    free[c] = [a]
                    src.append(dst)
                    wt.append(a)

                bb = 6 if t0 == 0 else 7
                mean = mean_square4(src, wt, n, one512, bb)
                next(mean)

                def finish(t0=t0, n=n, src=src, bb=bb, mean=mean):
                    r = rstd(bb, n, t0, next(mean), RMS_EPS)
                    rs = rs_view(n, t0)
                    with_gate = [M[:, GG + c * 768 + t0:GG + c * 768 + t0 + n] for c in range(4)]
                    done, his = {}, {}
                    for c in range(5):
                        if c < 4:
                            x1 = dve([r], lambda e, o=src[c]: e.tensor_tensor(o, o, rs, ALU.mult))
                            reads_rs("dve", t0, n, x1)
                            done[c] = dve([x1, g_ready[(c, t0)]], lambda e, c=c: e.tensor_tensor(
                                with_gate[c], src[c], with_gate[c], ALU.mult))
                            hi = HID[:, c * 768 + t0:c * 768 + t0 + n]
                            his[c] = act([done[c], state["hid_over"]], lambda e, c=c, hi=hi: e.copy(hi, with_gate[c]))
                        if c > 0:
                            k = c - 1
                            hi = HID[:, k * 768 + t0:k * 768 + t0 + n]
                            lo = HID[:, 4096 + k * 768 + t0:4096 + k * 768 + t0 + n]
                            y_ready[(k, t0)] = [his[k], dve([his[k], done[k], state["hid_over"]], lambda e, k=k, hi=hi, lo=lo: e.tensor_tensor(
                                lo, with_gate[k], hi, ALU.subtract))]
                    ov["qk" if t0 == 0 else "oc"] = [done[3]]

            ov["v"] = [o_tok[(3, 0)]]
            ov["st"] = [ov["last_score"], free[5], free[4]]
            if h < 3:
                start_chain(3, 1, once(finish))
                ahead = v_rows(h + 1)
                weighted = decays(h + 1)
            else:
                finish()
            ov["g"] = [y_ready[k] for k in y_ready]

            yacts = lambda half, k, t0, n: HID[:, half * 4096 + k * 768 + t0:half * 4096 + k * 768 + t0 + n]
            state["acc_over"] = [ov["g"]]
            post = gated(0, 2, 3, lambda s: layer_norm_chain(s, 0, 0, after_ln(0, 0, 3)))
            outs = lambda j2: [(jj * 512, lambda b, t0, n, d, j=j2 * 2 + jj, h=h: post(h, j, b, t0, n, d)) for jj in range(2)]
            done = columns([(dram["ret_o"][j2 * 2:j2 * 2 + 2, :, h * 512:(h + 1) * 512].rearrange("a p n -> p a n"), (2, 512), 4,
                             yacts, lambda k, t0, n: y_ready[(k, 0 if t0 < 512 else 512)], outs(j2)) for j2 in range(4)],
                           SUB2 if h == 3 else SEG2, batch=4 if h == 3 else 1)
            state["hid_over"] = [done]
        state["misc_over"] = [ov["g"], ov["v"], ov["qk"], ov["st"], ov["oc"]]

    def neighbourhood():
        QA, KA, VV, SA, PT, BM, SM = 0, 2048, 5120, 9728, 10752, 11776, 14900
        pro = [state["misc_over"]]
        STRIP, MSK = BM + 1536, BM + 1536 + 384
        hw = lambda k, t0, n: cover(h_ready, k, t0, n)
        sm = lambda o, n: M[:, SM + o:SM + o + n]
        bm3 = M[:, BM:BM + 1536].rearrange("p (y k) -> p y k", y=3)
        msk_ready = None
        ov = {"q": pro, "k": pro, "v": pro, "s": [pro, pro, rfree[both("a")]], "p": [pro, pro], "bm": [], "strip": []}
        wbuf = (M[:, SA:SA + 512], M[:, SA + 512:SA + 1024], TMP[:, 0:512])
        band0 = (0, 64, 192, 256)
        kind = (0, 1, 1, 2)
        off = (16, 8, 0)
        starts = {0: 0, 128: 1, 256: 2, 384: 3, 64: 4, 192: 5, 320: 6}
        y_over = []

        for half in range(2):
            q_ready, k_ready = {}, {}

            def q_post(b, t0, n, done, c):
                q_ready[c] = act([done, ov["q"]], lambda e: e.mul(M[:, QA + c * 512:QA + (c + 1) * 512], PS[:, b, :], 0.125))
                return [q_ready[c]]

            def k_post(b, t0, n, done, c):
                dst = M[:, KA + c * 768 + t0:KA + c * 768 + t0 + n]
                k_ready[(c, t0)] = act([done, ov["k"]], lambda e: e.copy(dst, PS[:, b, 0:n]))
                return [k_ready[(c, t0)]]

            vslot = lambda tt: tt if tt < 4 else tt + 3
            VC = lambda s_: M[:, VV + s_ * 512:VV + (s_ + 1) * 512]
            got, _ = token_rows([dram["na_v"][half, blk] for blk in range(4)], h_ready, ov["v"], lambda tt: VC(vslot(tt)))
            v_ready = {vslot(tt): tok for tt, tok in got.items()}
            if half == 0:
                late = [pro, state["joined"]]
                msk_ready = load(late, M[:, MSK:MSK + 768], dram["mask2"], sems["misc"])
                ov["bm"] = [pool(late, lambda e: e.memset(M[:, BM:BM + 1536], 0.0))]
                ov["strip"] = late
            for i, s_ in enumerate((4, 5, 6)):
                load([v_ready[i], v_ready[i + 1], ov["v"]], M[0:64, VV + s_ * 512:VV + (s_ + 1) * 512],
                     M[64:128, VV + i * 512:VV + (i + 1) * 512], sems["vs"])
                v_ready[s_] = load([v_ready[i + 1]], M[64:128, VV + s_ * 512:VV + (s_ + 1) * 512],
                                   M[0:64, VV + (i + 1) * 512:VV + (i + 2) * 512], sems["vs"])
            for s_ in (4, 5):
                v_ready[s_] = v_ready[6]

            def q_and_k(c):
                columns([(dram["na_qk"][half * 4 + c], (SLOT,), DC, hacts, hw,
                          [(0, lambda b, t0, n, d: q_post(b, t0, n, d, c))])], SEG1, banks=(5, 6, 7))
                last_h = columns([(dram["na_qk"][8 + half * 4 + c], (SLOT,), DC, hacts, hw,
                                   [(0, lambda b, t0, n, d: k_post(b, t0, n, d, c))])], SEG2, banks=(5, 6, 7))
                state["h_over"] = [last_h]

            st = {}
            units = [(hh, b) for hh in range(8) for b in range(4)]

            def bias(hh):
                s = load([ov["strip"]], M[:, STRIP:STRIP + 384], dram["rpb"][half * 8 + hh], sems["strip"])
                last = None
                for y in range(3):
                    last = pool([s, msk_ready, ov["bm"]], lambda e, y=y: e.tensor_tensor(
                        bm3[:, y, 0:256], M[:, STRIP + off[y] * 8:STRIP + off[y] * 8 + 256],
                        M[:, MSK + y * 256:MSK + (y + 1) * 256], ALU.add))
                ov["strip"] = [last]
                return last

            bm_ready = {}

            def scores(i):
                hh, b = units[i]
                if b == 0:
                    bm_ready[hh] = bias(hh)
                c, pp = hh // 2, slice((hh % 2) * 64, (hh % 2) * 64 + 64)
                bb = (0, 1)[i % 2]
                pe([q_ready[c], k_ready[(c, 0)], free[bb]], lambda e: e.matmul(
                    PS[:, bb, 0:256], M[pp, QA + c * 512 + b * P:QA + c * 512 + (b + 1) * P],
                    M[pp, KA + c * 768 + band0[b]:KA + c * 768 + band0[b] + 256], start=True, stop=True,
                    skip_group_check=True), False)
                done = pe([k_ready[(c, 512)]], lambda e: e.matmul(
                    PS[:, bb, 256:512], M[pp, QA + c * 512 + b * P:QA + c * 512 + (b + 1) * P],
                    M[pp, KA + c * 768 + 512:KA + c * 768 + 768], start=True, stop=True, skip_group_check=True))
                o = (i % 3) * 8
                mx, nm, su, rc = (sm(o + j, 1) for j in range(4))
                s = wbuf[i % 3]
                d = dve([done, bm_ready[hh], ov["s"][i % 3]], lambda e: e.tensor_tensor_reduce(
                    s, PS[:, bb, :], bm3[:, kind[b], :], 1.0, -3.0e38, ALU.add, ALU.max, mx))
                free[bb] = [d]
                if b == 3:
                    ov["bm"] = [d]
                d2 = dve([d], lambda e: e.tensor_scalar(nm, mx, -1.0, None, ALU.mult))
                a = act([d2], lambda e: e.activation(s, s, ACT.Exp, bias=nm, accum_out=su))
                d3 = dve([a], lambda e: e.reciprocal(rc, su))
                d4 = dve([d3], lambda e: e.tensor_scalar(s, s, rc, None, ALU.mult))
                st[i] = (s, d4)
                ov["last_score"] = done

            def turn_weights(i):
                s, d4 = st[i]
                bb = (2, 3)[i % 2]
                for kt in range(4):
                    done = pe([d4, free[bb] if kt == 0 else []], lambda e, kt=kt: e.transpose(
                        PS[:, bb, kt * P:(kt + 1) * P], s[:, kt * P:(kt + 1) * P], ident), kt == 3)
                ov["s"][i % 3] = [done]
                dst = M[:, PT + (i % 2) * 512:PT + (i % 2) * 512 + 512]
                a = act([done, ov["p"][i % 2]], lambda e: e.copy(dst, PS[:, bb, :]))
                free[bb] = [a]
                st[i] = (dst, a)

            def attend(i):
                hh, b = units[i]
                dst, a = st[i]
                r0 = (hh % 2) * 64
                ob = (4, 5)[(hh // 2) % 2]
                tiles = [starts[band0[b]], starts[band0[b] + 128], 7, 8]
                for kt in range(4):
                    vs = M[:, VV + tiles[kt] * 512 + hh * 64:VV + tiles[kt] * 512 + hh * 64 + 64]
                    done = pe([a, v_ready[tiles[kt]], free[ob] if b == 0 and kt == 0 and hh % 2 == 0 else []],
                              lambda e, kt=kt, vs=vs: e.matmul(PS[r0:r0 + 64, ob, b * P:(b + 1) * P], vs,
                                                               dst[:, kt * P:(kt + 1) * P], start=kt == 0, stop=kt == 3,
                                                               skip_group_check=True), kt == 3)
                ov["p"][i % 2] = [done]
                if b == 3 and hh % 2 == 1:
                    k = half * 4 + hh // 2
                    hi, lo = HID[:, k * 512:(k + 1) * 512], HID[:, 4096 + k * 512:4096 + (k + 1) * 512]
                    x1 = act([done, state["hid_over"]], lambda e: e.copy(hi, PS[:, ob, :]))
                    x2 = dve([x1, done], lambda e: e.tensor_tensor(lo, PS[:, ob, :], hi, ALU.subtract))
                    free[ob] = [x2]
                    y_over.append([x1, x2])
                ov["last"] = done

            for i in range(len(units) + 3):
                if i < 4:
                    q_and_k(i)
                if i < len(units):
                    scores(i)
                if 0 <= i - 2 < len(units):
                    turn_weights(i - 2)
                if i - 3 >= 0:
                    attend(i - 3)
            rfree[both("a")] = ov["s"][2]
            ov["q"] = ov["k"] = [ov["last_score"]]
            ov["v"] = [ov["last"]]

        old, x_old = home["buf"], dict(xt)
        home["buf"], home["pitch"] = M, 512
        state["acc_over"] = [ov["bm"], ov["strip"], msk_ready]
        chain = lambda s: layer_norm_chain(s, 1, 0, after_ln(2, 1, 3))

        def o_post(j):
            def post(b, t0, n, done):
                s = t0 // 256
                x = xs(j, t0, n)
                from_ = old[:, j * 768:j * 768 + 512].rearrange("p (r c) -> p c r", c=64)[:, 32 * s:32 * s + 32, :]
                xt[(j, s)] = dve([done, x_old[(j, 0)], x_old[(j, 1)], ov["q"]], lambda e: e.scalar_tensor_tensor(
                    out=x.rearrange("p (c r) -> p c r", r=8), in0=PS[:, b, 0:n].rearrange("p (c r) -> p c r", r=8),
                    scalar=mod(1, 0, 2, j), in1=from_, op0=ALU.mult, op1=ALU.add))
                summed(s, j, x, xt[(j, s)], False, chain)
                return [xt[(j, s)]]
            return post

        yacts = lambda half, k, t0, n: HID[:, half * 4096 + k * 512 + t0:half * 4096 + k * 512 + t0 + n]
        last = columns([(dram["na_o"][j], (SLOT,), DC, yacts, lambda k, t0, n: y_over[k], [(0, o_post(j))])
                        for j in range(DC)], SUB1, batch=4)
        state["hid_over"] = [last]

    q.stage("ffn1")
    for s in range(2):
        for c in range(DC):
            if plan is not None and (s, c) in ((0, 4), (1, 0), (1, 2), (1, 4)):
                prepare(ring["conv"])
            to_rms("ffn1_pre_g")(c, s)
    first_ffn("ffn1_post_g", dram["gu1"], dram["dn1"], to_rms("mix_pre_g"), ada_step)
    q.stage("mix1")
    first_mixer()
    q.stage("ffn2")
    ada["limit"] = 96
    context = iter(range(DC))

    def ada_or_context():
        if ada["n"] < 96 or ada["rows"]:
            ada_step()
            return
        c = next(context, None)
        if c is not None:
            xt[(c, 2)] = load([ada["row_read"]], xs(c, 512, 256), dram["ctx"][c], sems["x"][c])
            to_modulated(0, 0)(c, 2)

    first_ffn("ffn2_post_g", dram["gu2"], dram["dn2"], to_modulated(0, 0), ada_or_context)

    q.stage("ret")
    retention()
    q.stage("ffn3")
    ffn(dram["gu3"], dram["dn3"], PARTS2, SEG2, SUB2,
        gated(0, 5, 4, lambda s: layer_norm_chain(s, 0, 1, after_ln(1, 1, 0, True))), False)
    force(0, 512)
    for c in range(DC):
        h_ready[(c, 0)] = h_ready[(c, 1)] = [h_ready[(c, 0)], h_ready[(c, 1)]]
    q.stage("na")
    neighbourhood()
    q.stage("ffn4")

    def store(c, s, t, d):
        x = xs(c, s * 256, 256)
        lb = PAR[:, POFF["ln_b"] + 24 + c:POFF["ln_b"] + 25 + c]
        a = act([d], lambda e: e.activation(x, t, ACT.Identity, bias=lb))
        stores.append(load([a], dram["out"][c][:, s * 256:(s + 1) * 256], x, sems["out"]))
        return [a]

    stores = []
    ffn(dram["gu4"], dram["dn4"], PARTS1, SEG1, SUB1,
        gated(1, 5, 2, lambda s: layer_norm_chain(s, 1, 1, store)), False)
    force(0, 512)
    q.wait("sp", stores[-1])


def build_program(nc, ins, out):
    with ExitStack() as ctx:
        def sb(name, shape, dt):
            return ctx.enter_context(nc.sbuf_tensor("t_" + name, shape, dt))

        mem = {
            "X": sb("x", [P, 6144], F32), "H": sb("h", [P, 12288], F32R), "HID": sb("hid", [P, 8192], F32R),
            "WHI": sb("whi", [P, NH, SLOT], F32R), "WLO": sb("wlo", [P, NH, SLOT], F32R),
            "RAW": sb("raw", [P, NR, SLOT], F32), "MISC": sb("misc", [P, 14976], F32),
            "TMP": sb("tmp", [P, 2840], F32), "PAR": sb("par", [P, NPAR], F32), "CON": sb("con", [P, 388], F32),
            "MOD": sb("mod", [P, 264], F32), "PS": ctx.enter_context(nc.psum_tensor("ps", [P, 8, 512], F32)),
        }
        sem = lambda name: ctx.enter_context(nc.semaphore(name))
        sems = {
            "ring": [sem(f"d_ring{i}") for i in range(NR)], "par": sem("d_par"),
            "x": [sem(f"d_x{i}") for i in range(DC)], "misc": sem("d_misc"), "strip": sem("d_strip"), "vs": sem("d_vs"), "out": sem("d_out"),
        }
        dram = dict(ins)
        dram["out"] = out
        plan = []
        dry = Engines(lambda name: object())
        queue_program(dry, mem, dram, sems, None, plan)
        q = Engines(sem)
        queue_program(q, mem, dram, sems, plan, [])
        block = ctx.enter_context(nc.Block())

        @block.sync
        def _(e):
            q.replay("sp", e)

        @block.tensor
        def _(e):
            q.replay("pe", e)

        @block.scalar
        def _(e):
            q.replay("act", e)

        @block.vector
        def _(e):
            q.replay("dve", e)

        @block.gpsimd
        def _(e):
            q.replay("pool", e)


def stationary(w):
    k, n = w.shape
    return np.ascontiguousarray(w.reshape(k // P, P, n // P, P).transpose(2, 1, 0, 3)).reshape(n // P, P, k)


def moving(w):
    n = w.shape[1]
    return np.ascontiguousarray(w.reshape(4, 2, P, n // 512, 512).transpose(3, 0, 2, 1, 4)).reshape(n // 512, 4, P, 1024)


def cols(v):
    return np.asarray(v).reshape(-1, P).T


def lay_out(i):
    g = {k: np.asarray(v) for k, v in i.items()}
    heads = np.array(HEAD_ORDER)
    w_in = g["w_in"][0]
    qw = w_in[:, 1024:1536].reshape(D, 8, 64)[:, heads].reshape(D, 512)
    w_in = np.concatenate([w_in[:, :1024], qw, w_in[:, 1536:]], 1)
    w_o = g["w_o"][0]
    w_o = np.concatenate([w_o[:512], w_o[512:].reshape(8, 64, D)[heads].reshape(512, D)], 0)
    g_att = g["g_attn_out"][0].reshape(8, 64)[heads].reshape(512)
    par = {
        "ffn1_pre_g": cols(g["ffn1_pre_g"]), "ffn1_post_g": cols(g["ffn1_post_g"]), "mix_pre_g": cols(g["mix_pre_g"]),
        "conv_w": cols(g["conv_w"]), "conv_b": cols(g["conv_b"]), "b_rg": cols(g["b_rg"]), "b_ig": cols(g["b_ig"]),
        "lam": cols(g["lru_lambda"]), "g_mix": np.concatenate([cols(g["g_lru_out"]), cols(g_att)], 1),
        "mix_post_g": cols(g["mix_post_g"]), "ffn2_pre_g": cols(g["ffn2_pre_g"]), "ffn2_post_g": cols(g["ffn2_post_g"]),
        "cond": np.stack([cols(g["c_2"]), cols(g["c_ctx_2"])], 2).reshape(P, 16),
        "ada_b": cols(g["ada_b_2"]), "ln_g": cols(g["ln_g_2"]), "ln_b": cols(g["ln_b_2"]),
        "sinks": np.broadcast_to(g["sinks"][0], (P, 8)), "decay": np.broadcast_to(g["ret_decay_2"].reshape(8), (P, 8)),
    }
    a = {"params": np.ascontiguousarray(np.concatenate([par[n] for n, _ in PARAMS], 1))}
    comb = np.zeros((P, 2), np.float32)
    comb[0, 0] = comb[2, 0] = comb[1, 1] = comb[3, 1] = 1
    a["consts"] = np.concatenate([np.eye(P, dtype=np.float32), np.full((P, P), 1 / 1024, np.float32),
                                  np.full((P, P), 1 / 512, np.float32), comb,
                                  np.full((P, 1), RMS_EPS, np.float32), np.full((P, 1), LN_EPS, np.float32)], 1)
    a["x"] = np.ascontiguousarray(g["x"][0].T).reshape(DC, P, L)
    a["ctx"] = np.ascontiguousarray(g["ctx_2"][0].T).reshape(DC, P, LC)
    a["gu1"], a["dn1"] = stationary(g["ffn1_w_gu"][0]), stationary(g["ffn1_w_down"][0])
    a["gu2"], a["dn2"] = stationary(g["ffn2_w_gu"][0]), stationary(g["ffn2_w_down"][0])
    a["gu3"], a["dn3"] = stationary(g["ffn_w13_2"][0]), stationary(g["ffn_w2_2"][0])
    a["gu4"], a["dn4"] = stationary(g["ffn_w13_2"][1]), stationary(g["ffn_w2_2"][1])
    a["w_in"], a["w_o"] = stationary(w_in), stationary(w_o)
    gates = np.zeros((P, 2, 4, P), np.float32)
    for n, name in enumerate(("w_rg", "w_ig")):
        for b in range(8):
            o = (b % 2) * 64
            gates[o:o + 64, n, b // 2, o:o + 64] = g[name][0, b]
    a["gates"] = gates.reshape(P, 1024)
    qi, kj = np.arange(P)[:, None], np.arange(2 * P)[None]
    rel = qi + P - kj
    a["mask1"] = np.where((rel >= 0) & (rel < 128), 0, NEG).astype(np.float32)
    a["ada"] = np.stack([moving(g["ada_w_2"][n]) for n in range(2)])
    rw = g["ret_w_in_2"]
    a["ret_qk"], a["ret_v"], a["ret_g"] = stationary(rw[:, :2048]), moving(rw[:, 2048:4096]), stationary(rw[:, 4096:])
    a["ret_o"] = stationary(g["ret_w_out_2"])
    a["dist"] = (np.arange(1152)[None] - 384 - np.arange(P)[:, None]).astype(np.float32)
    t = np.arange(L)
    inv = (np.float32(10000.0) ** (-np.arange(64, dtype=np.float32) / np.float32(64))).astype(np.float32)
    ang = np.concatenate([(t // 64).astype(np.float32)[:, None] * inv, (t % 64).astype(np.float32)[:, None] * inv], 1)
    a["rope"] = np.ascontiguousarray(np.concatenate([np.cos(ang).T, np.sin(ang).T], 1)).astype(np.float32)
    nw = g["na_w_qkv_2"]
    a["na_qk"], a["na_v"], a["na_o"] = stationary(nw[:, :2048]), moving(nw[:, 2048:]), stationary(g["na_w_out_2"])
    ci, r = np.arange(P)[:, None, None] // 8, np.arange(P)[:, None, None] % 8
    m, rr = np.arange(48)[None, :, None], np.arange(8)[None, None]
    a["rpb"] = np.ascontiguousarray(g["na_rpb_2"][:, rr - r + 7, np.clip(m - 16 - ci + 15, 0, 30)]).reshape(16, P, 384)
    masks = []
    for b in (0, 1, 3):
        band = min(max(16 * b - 8, 0), 32)
        q = 16 * b + np.arange(P)[:, None] // 8
        k = band + np.arange(256)[None] // 8
        ws = np.clip(q - 8, 0, 48)
        masks.append(np.where((k >= ws) & (k < ws + 16), 0, NEG).astype(np.float32))
    a["mask2"] = np.concatenate(masks, 1)
    return a


def kernel(**inputs):
    import concourse.bacc as bacc
    from concourse.bass_utils import run_bass_kernel_spmd

    nc = bacc.Bacc("TRN2", target_bir_lowering=False, num_devices=1, dynamic_dma_scratch_size=1024)
    arrays = lay_out(inputs)
    ins = {k: nc.dram_tensor("in_" + k, v.shape, F32, kind="ExternalInput").ap() for k, v in arrays.items()}
    out = nc.dram_tensor("out_x", (DC, P, L), F32, kind="ExternalOutput").ap()
    build_program(nc, ins, out)
    r = run_bass_kernel_spmd(nc, [{"in_" + k: v for k, v in arrays.items()}], core_ids=[0])
    y = np.asarray(r.results[0]["out_x"]).reshape(D, 64, 8)
    return np.ascontiguousarray(y.transpose(2, 1, 0)).reshape(1, L, D)
```
